# Optimizing a Trainium2 kernel written in Bass

```python
import jax, jax.numpy as jnp
from jax import lax
import numpy as np

D_MODEL = 1024
BATCH = 1
SEQ = 128
DEPTH = 2
DEC_BATCH = 1
DEC_SEQ = 512
PAST_LEN = 128

GRID_W = 64
N_MIXERS = 2
N_CONV_LAYERS = (DEPTH + 1) // 2
N_SSD_LAYERS = DEPTH // 2
CONV_K = 31
SSM_INNER = 2 * D_MODEL
SSM_HEAD_DIM = 64
SSM_HEADS = SSM_INNER // SSM_HEAD_DIM
SSM_GROUPS = 4
HEADS_PER_GROUP = SSM_HEADS // SSM_GROUPS
D_STATE = 128
SSM_CONV_K = 5
SSM_CONV_DIM = SSM_INNER + 2 * SSM_GROUPS * D_STATE
SSM_IN_DIM = SSM_INNER + SSM_CONV_DIM + 2 * SSM_HEADS
SSD_CHUNK = 128
N_EXPERTS = 16
EXPERT_FF = D_MODEL
EC_CAPACITY_FACTOR = 2
ALPHA = (2 * DEPTH) ** 0.25
BETA = (8 * DEPTH) ** -0.25
LN_EPS = 1e-5

kernel_name = "hybrid_conv_ssd_ecmoe_diffusion_step"

def layer_norm(x, g, b):
    x32 = x.astype(jnp.float32)
    mu = jnp.mean(x32, -1, keepdims=True)
    var = jnp.mean(jnp.square(x32 - mu), -1, keepdims=True)
    return ((x32 - mu) * lax.rsqrt(var + LN_EPS) * g + b).astype(x.dtype)

def ada_mod(cvec, w, b):
    m = jax.nn.silu(cvec) @ w + b
    return jnp.split(m[..., None, :], 6, axis=-1)

def depthwise_conv2d(x, w, b, kh, kw):
    C = x.shape[-1]
    taps = w.reshape(kh, kw, 1, C).astype(x.dtype)
    y = lax.conv_general_dilated(x, taps, window_strides=(1, 1),
                                 padding=((kh // 2, kh // 2), (kw // 2, kw // 2)),
                                 dimension_numbers=("NHWC", "HWIO", "NHWC"),
                                 feature_group_count=C)
    return y + b

def conformer_conv(h, pw1_w, pw1_b, dw_w, dw_b, ln_g, ln_b, pw2_w, pw2_b, axis):
    u = h @ pw1_w + pw1_b
    a, g = jnp.split(u, 2, axis=-1)
    u = a * jax.nn.sigmoid(g)
    bsz, L, dm = u.shape
    if axis == "seq":
        grid, kh, kw = u[:, None], 1, CONV_K
    elif axis == "row":
        grid, kh, kw = u.reshape(bsz, L // GRID_W, GRID_W, dm), 1, CONV_K
    else:
        grid, kh, kw = u.reshape(bsz, L // GRID_W, GRID_W, dm), CONV_K, 1
    v = depthwise_conv2d(grid, dw_w, dw_b, kh, kw).reshape(bsz, L, dm)
    v = jax.nn.silu(layer_norm(v, ln_g, ln_b))
    return v @ pw2_w + pw2_b

def segsum(a):
    T = a.shape[-1]
    cs = jnp.cumsum(a, axis=-1)
    diff = cs[..., :, None] - cs[..., None, :]
    mask = jnp.tril(jnp.ones((T, T), dtype=bool))
    return jnp.where(mask, diff, -jnp.inf)

def ssd_scan(x, dt, A, B, C, init):
    b, L = x.shape[:2]
    nc = L // SSD_CHUNK
    X = (x * dt[..., None]).reshape(b, nc, SSD_CHUNK, SSM_GROUPS, HEADS_PER_GROUP, SSM_HEAD_DIM)
    a = (dt * A).reshape(b, nc, SSD_CHUNK, SSM_GROUPS, HEADS_PER_GROUP).transpose(0, 3, 4, 1, 2)
    Bc = B.reshape(b, nc, SSD_CHUNK, SSM_GROUPS, D_STATE)
    Cc = C.reshape(b, nc, SSD_CHUNK, SSM_GROUPS, D_STATE)
    a_cum = jnp.cumsum(a, axis=-1)
    Lm = jnp.exp(segsum(a))
    y_diag = jnp.einsum("bclgn,bcsgn,bgjcls,bcsgjp->bclgjp", Cc, Bc, Lm, X)
    decay_states = jnp.exp(a_cum[..., -1:] - a_cum)
    states = jnp.einsum("bclgn,bgjcl,bclgjp->bcgjpn", Bc, decay_states, X)
    init_g = init.reshape(b, SSM_GROUPS, HEADS_PER_GROUP, SSM_HEAD_DIM, D_STATE)
    states = jnp.concatenate([init_g[:, None], states], axis=1)
    chunk_a = jnp.pad(a_cum[..., -1], ((0, 0), (0, 0), (0, 0), (1, 0)))
    decay_chunk = jnp.exp(segsum(chunk_a))
    new_states = jnp.einsum("bgjzc,bcgjpn->bzgjpn", decay_chunk, states)
    prev_states, final = new_states[:, :-1], new_states[:, -1]
    y_off = jnp.einsum("bclgn,bcgjpn,bgjcl->bclgjp", Cc, prev_states, jnp.exp(a_cum))
    y = (y_diag + y_off).reshape(b, L, SSM_HEADS, SSM_HEAD_DIM)
    return y, final.reshape(b, SSM_HEADS, SSM_HEAD_DIM, D_STATE)

def ssd_mixer(h, in_w, conv_w, conv_b, dt_bias, a_log, d_skip, norm_w, out_w, init_f, init_b):
    bsz, L, _ = h.shape
    zxbcdt = h @ in_w
    z = zxbcdt[..., :SSM_INNER]
    xbc = zxbcdt[..., SSM_INNER:SSM_INNER + SSM_CONV_DIM]
    dt_raw = zxbcdt[..., SSM_INNER + SSM_CONV_DIM:]
    xbc = jax.nn.silu(depthwise_conv2d(xbc[:, None], conv_w, conv_b, 1, SSM_CONV_K)[:, 0])
    gn = SSM_GROUPS * D_STATE
    xs = xbc[..., :SSM_INNER].astype(jnp.float32).reshape(bsz, L, SSM_HEADS, SSM_HEAD_DIM)
    Bm = xbc[..., SSM_INNER:SSM_INNER + gn].astype(jnp.float32).reshape(bsz, L, SSM_GROUPS, D_STATE)
    Cm = xbc[..., SSM_INNER + gn:].astype(jnp.float32).reshape(bsz, L, SSM_GROUPS, D_STATE)
    dt = jax.nn.softplus(dt_raw.astype(jnp.float32).reshape(bsz, L, 2, SSM_HEADS) + dt_bias.astype(jnp.float32))
    A = -jnp.exp(a_log.astype(jnp.float32))
    y_f, s_f = ssd_scan(xs, dt[:, :, 0], A[0], Bm, Cm, init_f.astype(jnp.float32))
    flip = lambda t: t[:, ::-1]
    y_b, s_b = ssd_scan(flip(xs), flip(dt[:, :, 1]), A[1], flip(Bm), flip(Cm), init_b.astype(jnp.float32))
    y = y_f + flip(y_b) + d_skip.astype(jnp.float32)[:, None] * xs
    y = y.reshape(bsz, L, SSM_INNER) * jax.nn.silu(z.astype(jnp.float32))
    yg = y.reshape(bsz, L, SSM_GROUPS, SSM_INNER // SSM_GROUPS)
    yg = yg * lax.rsqrt(jnp.mean(jnp.square(yg), -1, keepdims=True) + LN_EPS)
    y = yg.reshape(bsz, L, SSM_INNER) * norm_w
    return y.astype(h.dtype) @ out_w, s_f, s_b

def ec_moe(h, router_w, w_gate, w_up, w_down):
    T = h.shape[0]
    cap = EC_CAPACITY_FACTOR * T // N_EXPERTS
    aff = jax.nn.softmax((h @ router_w).astype(jnp.float32), axis=-1)
    gates, idx = lax.top_k(aff.T, cap)
    xin = h[idx]
    hid = jax.nn.silu(jnp.einsum("ecd,edf->ecf", xin, w_gate)) * jnp.einsum("ecd,edf->ecf", xin, w_up)
    out = jnp.einsum("ecf,efd->ecd", hid, w_down) * gates[..., None].astype(h.dtype)
    return jnp.zeros_like(h).at[idx.reshape(-1)].add(out.reshape(-1, h.shape[-1]))

def setup_inputs(seed: int = 0) -> dict:
    key = jax.random.key(seed)
    ks = iter(jax.random.split(key, 40))
    f32 = jnp.float32
    nrm = lambda shape, s: jax.random.normal(next(ks), shape, f32) * s
    D, NC, NS = D_MODEL, N_CONV_LAYERS, N_SSD_LAYERS
    gate_offset = jnp.repeat(jnp.array([0., 0., 1., 0., 0., 1.], f32), D)
    dt0 = jnp.exp(jax.random.uniform(next(ks), (NS, 2, SSM_HEADS), f32) * (np.log(0.1) - np.log(0.001)) + np.log(0.001))
    return {
        "x_prompt": nrm((BATCH, SEQ, D), 1.0),
        "x_sample": nrm((DEC_BATCH, DEC_SEQ, D), 1.0),
        "state_ssd": nrm((DEC_BATCH, NS, 2, SSM_HEADS, SSM_HEAD_DIM, D_STATE), 0.1),
        "c": nrm((DEC_BATCH, D), 1.0),
        "c_ctx": nrm((D,), 1.0),
        "ada_w": nrm((DEPTH, D, 6 * D), D ** -0.5),
        "ada_b": nrm((DEPTH, 6 * D), 0.02) + gate_offset,
        "ln_mix_g": 1.0 + nrm((DEPTH, D), 0.02),
        "ln_mix_b": nrm((DEPTH, D), 0.02),
        "ln_ffn_g": 1.0 + nrm((DEPTH, D), 0.02),
        "ln_ffn_b": nrm((DEPTH, D), 0.02),
        "conv_pw1_w": nrm((NC, D, 2 * D), D ** -0.5),
        "conv_pw1_b": nrm((NC, 2 * D), 0.02),
        "conv_dw_w": nrm((NC, CONV_K, D), CONV_K ** -0.5),
        "conv_dw_b": nrm((NC, D), 0.02),
        "conv_ln_g": 1.0 + nrm((NC, D), 0.02),
        "conv_ln_b": nrm((NC, D), 0.02),
        "conv_pw2_w": nrm((NC, D, D), BETA * D ** -0.5),
        "conv_pw2_b": nrm((NC, D), 0.02),
        "ssd_in_w": nrm((NS, D, SSM_IN_DIM), D ** -0.5),
        "ssd_conv_w": nrm((NS, SSM_CONV_K, SSM_CONV_DIM), SSM_CONV_K ** -0.5),
        "ssd_conv_b": nrm((NS, SSM_CONV_DIM), 0.02),
        "ssd_dt_bias": dt0 + jnp.log(-jnp.expm1(-dt0)),
        "ssd_a_log": jnp.log(jax.random.uniform(next(ks), (NS, 2, SSM_HEADS), f32, 1.0, 16.0)),
        "ssd_d_skip": 1.0 + nrm((NS, SSM_HEADS), 0.1),
        "ssd_norm_w": 1.0 + nrm((NS, SSM_INNER), 0.02),
        "ssd_out_w": nrm((NS, SSM_INNER, D), BETA * SSM_INNER ** -0.5),
        "router_w": nrm((DEPTH, D, N_EXPERTS), D ** -0.5),
        "moe_w_gate": nrm((DEPTH, N_EXPERTS, D, EXPERT_FF), D ** -0.5),
        "moe_w_up": nrm((DEPTH, N_EXPERTS, D, EXPERT_FF), D ** -0.5),
        "moe_w_down": nrm((DEPTH, N_EXPERTS, EXPERT_FF, D), BETA * EXPERT_FF ** -0.5),
    }

def reference(x_prompt, x_sample, state_ssd, c, c_ctx, ada_w, ada_b, ln_mix_g, ln_mix_b,
              ln_ffn_g, ln_ffn_b, conv_pw1_w, conv_pw1_b, conv_dw_w, conv_dw_b, conv_ln_g,
              conv_ln_b, conv_pw2_w, conv_pw2_b, ssd_in_w, ssd_conv_w, ssd_conv_b, ssd_dt_bias,
              ssd_a_log, ssd_d_skip, ssd_norm_w, ssd_out_w, router_w, moe_w_gate, moe_w_up,
              moe_w_down):
    yp, ys = x_prompt, x_sample
    new_states = []
    for i in range(DEPTH):
        sh_mp, sc_mp, g_mp, sh_fp, sc_fp, g_fp = ada_mod(c_ctx, ada_w[i], ada_b[i])
        sh_ms, sc_ms, g_ms, sh_fs, sc_fs, g_fs = ada_mod(c, ada_w[i], ada_b[i])
        hp = yp * (1 + sc_mp) + sh_mp
        hs = ys * (1 + sc_ms) + sh_ms
        k = i // N_MIXERS
        if i % N_MIXERS == 0:
            cp = (conv_pw1_w[k], conv_pw1_b[k], conv_dw_w[k], conv_dw_b[k],
                  conv_ln_g[k], conv_ln_b[k], conv_pw2_w[k], conv_pw2_b[k])
            mp = conformer_conv(hp, *cp, axis="seq")
            ms = conformer_conv(hs, *cp, axis="row" if k % 2 == 0 else "col")
        else:
            sp = (ssd_in_w[k], ssd_conv_w[k], ssd_conv_b[k], ssd_dt_bias[k], ssd_a_log[k],
                  ssd_d_skip[k], ssd_norm_w[k], ssd_out_w[k])
            zero = jnp.zeros((yp.shape[0], SSM_HEADS, SSM_HEAD_DIM, D_STATE), jnp.float32)
            mp, s_f, s_b = ssd_mixer(hp, *sp, zero, zero)
            ms, _, _ = ssd_mixer(hs, *sp, state_ssd[:, k, 0], state_ssd[:, k, 1])
            new_states.append(jnp.stack([s_f, s_b], axis=1).astype(x_prompt.dtype))
        yp = layer_norm(ALPHA * yp + g_mp * mp, ln_mix_g[i], ln_mix_b[i])
        ys = layer_norm(ALPHA * ys + g_ms * ms, ln_mix_g[i], ln_mix_b[i])
        moe_p = (router_w[i], moe_w_gate[i], moe_w_up[i], moe_w_down[i])
        hp = yp * (1 + sc_fp) + sh_fp
        hs = ys * (1 + sc_fs) + sh_fs
        fp = ec_moe(hp.reshape(-1, D_MODEL), *moe_p).reshape(yp.shape)
        fs = ec_moe(hs.reshape(-1, D_MODEL), *moe_p).reshape(ys.shape)
        yp = layer_norm(ALPHA * yp + g_fp * fp, ln_ffn_g[i], ln_ffn_b[i])
        ys = layer_norm(ALPHA * ys + g_fs * fs, ln_ffn_g[i], ln_ffn_b[i])
    new_state_ssd = jnp.stack(new_states, axis=1)
    return (yp, ys, new_state_ssd)


_drawn_inputs = setup_inputs


def setup_inputs(seed=0):
    import zlib

    import numpy as np

    out = dict(_drawn_inputs(seed))
    spreads = {}
    factors = {'conv_pw1_b': 5.186,
     'conv_dw_b': 4.384,
     'conv_ln_g': 5.225,
     'conv_ln_b': 4.056,
     'ssd_d_skip': 3.343,
     'ssd_norm_w': 4.54,
     'conv_pw2_b': 2.817}
    for name, (base, spread) in spreads.items():
        noise = np.random.default_rng([zlib.crc32(name.encode()), seed]).standard_normal(out[name].shape)
        drawn = base * np.exp(spread * noise) if base else spread * noise
        out[name] = __import__('jax').numpy.asarray(drawn.astype(out[name].dtype))
    for name, factor in factors.items():
        out[name] = (out[name] * factor).astype(out[name].dtype)
    return out
```

```python
from contextlib import ExitStack

import numpy as np

import concourse.bass as bass
from concourse import mybir

F32 = mybir.dt.float32
ALU = mybir.AluOpType
ACT = mybir.ActivationFunctionType
AX = mybir.AxisListType

P = 128
D = 1024
KC = D // P
NS = 4
NT = 5
TOK = NT * P
SAMPLE = NS * P
DEPTH = 2
ALPHA = (2 * DEPTH) ** 0.25
EPS = 1e-5
TAPS = 31
HALO = TAPS // 2
GRID_W = 64
ROWS = TOK // GRID_W
PITCH = GRID_W + 2 * HALO
EXPERTS = 16
PAIRS = EXPERTS // 2
CAP_S, CAP_P = 64, 16
SLOTS = CAP_S + CAP_P
GROUPS = 4
GC = 512
HEADS = 32
HG = 8
HD = 64
STAPS = 5
R = 3
UNIT = KC * 512

U_ADA0 = 0
U_PW1 = 12
U_ADA1 = 16
U_PW2 = 28
U_MOE0 = 30
U_SSD = U_MOE0 + 6 * EXPERTS
U_MOE1 = U_SSD + 4 * GROUPS
UNITS = U_MOE1 + 6 * EXPERTS

COLS = {}
_n = 0
for _name, _k in (("ada_b", 96), ("pw1_b", 16), ("dw_w", KC * TAPS), ("dw_b", KC), ("cln_g", KC), ("cln_b", KC),
                  ("sc_w", 24 * STAPS), ("sc_b", 24), ("norm_w", 16), ("cond", KC * 2)):
    COLS[_name] = (_n, _n + _k)
    _n += _k
NCOLS = _n
C_ID, C_LE, C_GE, C_GT, C_LT, C_ONE, C_MEAN, C_IOTA = (i * P for i in range(8))
NCONST = C_IOTA + CAP_S


def scan_tasks():
    back = [(1, c, 1, int(c > 0)) for c in range(NS - 1, -1, -1)] + [(1, NS, 0, 1)]
    fwd = [(0, c, 1, int(c < NS - 1)) for c in range(NS)] + [(0, NS, 0, 1)]
    return back + fwd


class Steps:

    def __init__(self, eng, sem):
        self.eng, self.sem, self.n, self.off = eng, sem, 0, 0

    def __call__(self, ins):
        ins.then_inc(self.sem, 1)
        self.n += 1

    def sync(self):
        self.eng.wait_ge(self.sem, self.off + self.n)


def build(nc, w_stream, x_in, params, consts, router, w_dt, ln_rows, pw2_b, ssd_rows, state_in, y_out, state_out):
    ctx = ExitStack()
    with ctx:
        def sb(name, shape):
            return ctx.enter_context(nc.sbuf_tensor(name, shape, F32))

        def sem(name):
            return ctx.enter_context(nc.semaphore(name))

        bank = [ctx.enter_context(nc.psum_tensor(f"bank{i}", [P, 512], F32)) for i in range(8)]

        ring = [sb(f"ring{i}", [P, UNIT]) for i in range(R)]
        X = sb("X", [P, NT, D])
        hT = sb("hT", [P, KC, TOK])
        cst = sb("cst", [P, NCONST])
        par = sb("par", [P, NCOLS])
        mT = sb("mT", [P, DEPTH, 48, 2])
        csil = sb("csil", [P, KC, 2])
        gate_bc = sb("gate_bc", [P, 2, D])
        ln_gb = sb("ln_gb", [P, 2, D])
        wr = sb("wr", [P, DEPTH, KC, EXPERTS])
        st = sb("st", [P, NT, 2, 6])
        mv = sb("mv", [P, NT, 2])
        rst = sb("rst", [P, NT])
        tmp = sb("tmp", [P, 2, 512])

        SCR = 23480
        scr = sb("scr", [P, SCR])
        at = {"conv": 0, "moe": 0, "ssd": 0}

        def take(stage, *shape):
            n = int(np.prod(shape))
            o = at[stage]
            at[stage] = o + n
            assert at[stage] <= SCR, (stage, at[stage])
            v = scr[:, o:o + n]
            if len(shape) == 2:
                return v.rearrange("p (a b) -> p a b", b=shape[1])
            if len(shape) == 3:
                return v.rearrange("p (a b c) -> p a b c", b=shape[1], c=shape[2])
            return v

        upad = take("conv", KC, ROWS, PITCH)
        v = take("conv", KC, TOK)
        sig = take("conv", 2, TOK)
        sq = take("conv", 2, TOK)
        rstd = take("conv", TOK)
        pwb = take("conv", D)
        mrow = take("conv", 2, 512)
        xin = take("moe", 2, KC, SLOTS)
        hid = take("moe", 2, 512)
        sil = take("moe", 2, 512)
        hidT = take("moe", KC, SLOTS)
        psel = take("moe", NS, 2, CAP_S)
        psel_p = take("moe", 2, CAP_P)
        pg = take("moe", NS, 2 * CAP_S)
        pg_p = take("moe", 2, 32)
        PT = take("moe", SAMPLE)
        PT_p = take("moe", P)
        out_s = take("moe", D)
        out_p = take("moe", D)
        aff = take("moe", NT, EXPERTS)
        lg = take("moe", NT, EXPERTS)
        posT = take("moe", NT, EXPERTS)
        small = take("moe", 4, NT)
        affT = take("moe", TOK)
        work = take("moe", TOK)
        pos = take("moe", TOK)
        top8 = take("moe", 8)
        ccol = take("moe", 3, NT, 2)
        facc_m = take("moe", NT, D)
        facc_s = take("ssd", NT, D)
        xs = take("ssd", NT, GC)
        Y = take("ssd", NT, GC)
        Btok = take("ssd", NT, P)
        BT = take("ssd", TOK)
        CT = take("ssd", TOK)
        dt = take("ssd", NT, 64)
        da = take("ssd", NT, 64)
        Ex = take("ssd", NT, 192)
        wst = take("ssd", NT, 64)
        srow = take("ssd", 160)
        prevS = take("ssd", 2, GC)
        rms = take("ssd", 2, NT)
        mark = at["ssd"]
        CBm = take("ssd", 2, NT * P)
        at["ssd"] = mark
        dtmp = take("ssd", 3, NT * 64)
        at["ssd"] = mark + 2 * NT * P
        mark = at["ssd"]
        raw = take("ssd", 2, SAMPLE + P + 8)
        cv = take("ssd", 2, TOK)
        xf = take("ssd", 2, TOK)
        at["ssd"] = mark
        aM = take("ssd", 4, 512)
        Em = take("ssd", 4, 512)
        end = at["ssd"]
        at["ssd"] = mark
        yT = take("ssd", 4, TOK)
        at["ssd"] = end
        Xd = take("ssd", 4, 256)
        at["ssd"] = end
        wdt = take("ssd", KC, 64)
        at["ssd"] = end + 4 * 256
        xw = take("ssd", 2, GC)
        at["ssd"] -= 2 * GC
        zt = take("ssd", 2, GC)

        ident = cst[:, C_ID:C_ID + P]
        m_le, m_ge = cst[:, C_LE:C_LE + P], cst[:, C_GE:C_GE + P]
        m_gt, m_lt = cst[:, C_GT:C_GT + P], cst[:, C_LT:C_LT + P]
        ones, mean_w = cst[:, C_ONE:C_ONE + P], cst[:, C_MEAN:C_MEAN + P]
        iota = cst[:, C_IOTA:C_IOTA + CAP_S]

        def par_v(name, *shape):
            a, b = COLS[name]
            w = par[:, a:b]
            return w.rearrange("p (a b) -> p a b", b=shape[-1]) if shape else w

        ada_bT = par_v("ada_b")
        pw1_b = par_v("pw1_b")
        dw_w = par_v("dw_w", TAPS)
        dw_b = par_v("dw_b")
        cln_g, cln_b = par_v("cln_g"), par_v("cln_b")
        sc_w, sc_b = par_v("sc_w", STAPS), par_v("sc_b")
        norm_w = par_v("norm_w")
        cond = par_v("cond")

        landed = [sem(f"slot_landed{i}") for i in range(R)]
        names = """x_loaded par_loaded cst_loaded wr_loaded ln_loaded pwb_loaded ssdp_loaded state_loaded
            dve_step act_step pool_step adab_ready cond_ready ada_mm mrow_ready ada_tr mT_ready
            hT_tr hTs_ready hTp_ready gate_mm gate_ready upad_zero pw1_done glu_a glu_sig conv_ready mean_mm centered
            sq_ready var_mm var_ready rstd_ready normed v_ready f_mm f_added ln_stat ln_rstd x_ready
            logits_mm lg_ready exp_ready aff_ready aff_tr posm_ready pos_tr psel_ready pg_ready gather_mm xin_ready
            gu_mm silu_ready hid_ready hidT_tr hidT_ready down_mm down_out pt_tr pt_ready comb_mm comb_added
            dtr_mm dt_a dt_b dt_c da_ready cum_mm ex_ready cproj_mm raw_ready cconv_ready xf_ready xtr_mm xs_a xs_v
            z_mm z_silu y_z ss_ready rms_a rms_b y_normed ytr_mm yT_ready out_mm out_added cb_mm cbm_ready y_init
            aM_ready seg_mm exp_m m_ready xd_ready yd_mm yd_added xw_ready off_mm off_added st_mm prev_ready
            st_out y_stored""".split()

        s = {n: sem(n) for n in names}

        block = ctx.enter_context(nc.Block())
        hT_f = hT[:, :, :]

        def gate_part(stage):
            return 16 if stage % 2 == 0 else 40

        def shift_part(stage):
            return 0 if stage % 2 == 0 else 24

        @block.sync
        def _(sp):
            sp.dma_start(par[:, :], params).then_inc(s["par_loaded"], 16)
            for j in range(R):
                sp.dma_start(ring[j][:, :], w_stream[j]).then_inc(landed[j], 16)
            sp.dma_start(cst[:, :], consts).then_inc(s["cst_loaded"], 16)
            sp.dma_start(X[:, :, :], x_in).then_inc(s["x_loaded"], 16)

            def used(u, p=0):
                if u < U_PW1:
                    return s["ada_mm"], u + 1
                if u < U_ADA1:
                    return s["pw1_done"], 4 * (u - U_PW1 + 1)
                if u < U_PW2:
                    return s["ada_mm"], 12 + u - U_ADA1 + 1
                if u < U_MOE0:
                    return s["f_mm"], NT * (u - U_PW2 + 1)
                if U_SSD <= u < U_MOE1:
                    g, k = (u - U_SSD) // 4, (u - U_SSD) % 4
                    return ((s["cproj_mm"], 6 * g + 2), (s["cproj_mm"], 6 * g + 6), (s["z_mm"], NT * (g + 1)),
                            (s["out_mm"], 2 * NT * (g + 1)))[k]
                L, u0 = (0, U_MOE0) if u < U_SSD else (1, U_MOE1)
                e, k = (u - u0) // 6, (u - u0) % 6
                if k < 4:
                    return s["gu_mm"], p * 8 + (4 * (16 * L + e) + k + 1)
                return s["down_mm"], p * 4 + (2 * (16 * L + e) + k - 3)

            def load(u, p=0):
                j = u % R
                sp.wait_ge(*used(u - R, p))
                w = UNIT // 2 if U_SSD <= u < U_MOE1 and (u - U_SSD) % 4 == 0 else UNIT
                sp.dma_start(ring[j][:, 0:w], w_stream[p * 12 + u, :, 0:w]).then_inc(landed[j], 16)

            for u in range(R, U_MOE0 + 12):
                load(u)
            with sp.Fori(0, PAIRS - 1) as p:
                for k in range(12):
                    load(U_MOE0 + 12 + k, p)
            for u in range(U_SSD, U_MOE1 + 12):
                load(u)
            with sp.Fori(0, PAIRS - 1) as p:
                for k in range(12):
                    load(U_MOE1 + 12 + k, p)
            for t in range(NT):
                sp.wait_ge(s["x_ready"], 15 + t + 1)
                sp.dma_start(y_out[:, t, :], X[:, t, :]).then_inc(s["y_stored"], 16)
            sp.wait_ge(s["y_stored"], 16 * NT)
            sp.wait_ge(s["st_out"], 16 * 2 * GROUPS)

        @block.tensor
        def _(pe):
            def unit_wait(u0, k, p=0):
                j = (u0 + k) % R
                pe.wait_ge(landed[j], 16 * ((u0 + k) // R + 1) + p * (16 * 12 // R))
                return ring[j][:, :].rearrange("p (k n) -> p k n", n=512)

            def ada(L, u0):
                def tr(u):
                    pe.wait_ge(s["mrow_ready"], 12 * L + u + 1)
                    for i in range(4):
                        ins = pe.transpose(bank[6 + u % 2][:, 2 * i:2 * i + 2], mrow[0:2, u % 2, i * P:(i + 1) * P],
                                           ident[0:2, 0:2])
                    ins.then_inc(s["ada_tr"], 1)

                for u in range(12):
                    w = unit_wait(u0, u)
                    if u >= 2:
                        pe.wait_ge(s["mrow_ready"], 12 * L + u - 1)
                    for k in range(KC):
                        ins = pe.matmul(bank[4 + u % 2][0:2, :], csil[:, k, :], w[:, k, :],
                                        start=(k == 0), stop=(k == KC - 1))
                    ins.then_inc(s["ada_mm"], 1)
                    if u:
                        if u >= 3:
                            pe.wait_ge(s["mT_ready"], 4 * (12 * L + u - 2))
                        tr(u - 1)
                pe.wait_ge(s["mT_ready"], 4 * (12 * L + 10))
                tr(11)

            def build_hT(b):
                if b == 0:
                    pe.wait_ge(s["x_loaded"], 16)
                else:
                    pe.wait_ge(s["x_ready"], 5 * b)
                for k in range(KC):
                    if k >= 2:
                        pe.wait_ge(s["hTs_ready"], 8 * b + k - 1)
                        pe.wait_ge(s["hTp_ready"], 8 * b + k - 1)
                    for t in range(NT):
                        out = bank[k % 2][:, t * P:(t + 1) * P] if t < NS else bank[2 + k % 2][:, 0:P]
                        ins = pe.transpose(out, X[:, t, k * P:(k + 1) * P], ident)
                    ins.then_inc(s["hT_tr"], 1)

            def gates(b):
                L, g0 = b // 2, gate_part(b)
                pe.wait_ge(s["mT_ready"], 48 * (L + 1))
                for c in range(2):
                    for h in range(2):
                        for i in range(4):
                            ins = pe.matmul(bank[4 + 2 * c + h][:, i * P:(i + 1) * P],
                                            mT[:, L, g0 + 4 * h + i, c:c + 1].broadcast_to([P, P]), ident,
                                            start=True, stop=True)
                        ins.then_inc(s["gate_mm"], 1)

            def hT_whole(b):
                pe.wait_ge(s["hTs_ready"], 8 * (b + 1))
                pe.wait_ge(s["hTp_ready"], 8 * (b + 1))

            pe.wait_ge(s["cst_loaded"], 16)
            pe.wait_ge(s["cond_ready"], 1)
            ada(0, U_ADA0)
            build_hT(0)
            gates(0)
            hT_whole(0)
            for i in range(16):
                if i % 4 == 0:
                    w = unit_wait(U_PW1, i // 4)
                if i >= 2:
                    pe.wait_ge(s["glu_a"], 1 * (i - 1))
                for k in range(KC):
                    lw = w[:, k, (i % 4) * P:(i % 4 + 1) * P]
                    pe.matmul(bank[i % 2][:, :], lw, hT[:, k, 0:SAMPLE], start=(k == 0), stop=(k == KC - 1))
                    ins = pe.matmul(bank[2 + i % 2][:, 0:P], lw, hT[:, k, SAMPLE:TOK], start=(k == 0), stop=(k == KC - 1))
                ins.then_inc(s["pw1_done"], 1)
            pe.wait_ge(s["gate_ready"], 4)
            ada(1, U_ADA1)
            for k in range(KC):
                pe.wait_ge(s["conv_ready"], k + 1)
                if k == 0:
                    pe.wait_ge(s["glu_a"], 16)
                pe.matmul(bank[0][:, :], mean_w, v[:, k, 0:SAMPLE], start=(k == 0), stop=(k == KC - 1))
                ins = pe.matmul(bank[2][:, 0:P], mean_w, v[:, k, SAMPLE:TOK], start=(k == 0), stop=(k == KC - 1))
            ins.then_inc(s["mean_mm"], 1)
            for k in range(KC):
                pe.wait_ge(s["sq_ready"], k + 1)
                pe.matmul(bank[1][:, :], mean_w, sq[:, k % 2, 0:SAMPLE], start=(k == 0), stop=(k == KC - 1))
                pe.matmul(bank[3][:, 0:P], mean_w, sq[:, k % 2, SAMPLE:TOK], start=(k == 0),
                          stop=(k == KC - 1)).then_inc(s["var_mm"], 1)
            pe.wait_ge(s["v_ready"], 8)
            pe.wait_ge(s["pwb_loaded"], 16)
            pe.wait_ge(s["mT_ready"], 96)
            for nb in range(2):
                w = unit_wait(U_PW2, nb)
                for t in range(NT):
                    i = nb * NT + t
                    if i >= 8:
                        pe.wait_ge(s["f_added"], i - 7)
                    for k in range(KC):
                        pe.matmul(bank[i % 8][:, :], v[:, k, t * P:(t + 1) * P], w[:, k, :], start=(k == 0), stop=False)
                    ins = pe.matmul(bank[i % 8][:, :], ones[0:1, :], pwb[0:1, nb * 512:(nb + 1) * 512],
                                    start=False, stop=True)
                    ins.then_inc(s["f_mm"], 1)

            def gather(Pi):
                pe.wait_ge(s["psel_ready"], Pi + 1)
                for k in range(KC):
                    ins = pe.matmul(bank[5][:, 128 + 32 * k:160 + 32 * k], X[:, NS, k * P:(k + 1) * P],
                                    psel_p[:, :, :], start=True, stop=True)
                ins.then_inc(s["gather_mm"], 1)
                for half in range(2):
                    for kk in range(4):
                        k = 4 * half + kk
                        for t in range(NS):
                            ins = pe.matmul(bank[6 + half][:, kk * P:(kk + 1) * P], X[:, t, k * P:(k + 1) * P],
                                            psel[:, t, :, :], start=(t == 0), stop=(t == NS - 1))
                    ins.then_inc(s["gather_mm"], 1)

            def combine(Pi):
                pe.wait_ge(s["down_out"], 8 * Pi + 8)
                pe.wait_ge(s["pt_ready"], 2 * Pi + 2)
                for i in range(2 * NT):
                    t, h = i // 2, i % 2
                    if i >= 2:
                        pe.wait_ge(s["comb_added"], 10 * Pi + (i - 1))
                    if t < NS:
                        ins = pe.matmul(bank[6 + h][:, :], PT[:, t * P:(t + 1) * P], out_s[:, h * 512:(h + 1) * 512],
                                        start=True, stop=True)
                    else:
                        ins = pe.matmul(bank[6 + h][:, :], PT_p[0:64, :], out_p[0:64, h * 512:(h + 1) * 512],
                                        start=True, stop=True)
                    ins.then_inc(s["comb_mm"], 1)

            def expert(L, u0, p, e):
                Pi = 8 * L + p
                Ei = 16 * L + 2 * p + e
                if e == 0:
                    pe.wait_ge(s["xin_ready"], 16 * Pi + 16)
                    if not (L == 0 and isinstance(p, int) and p == 0):
                        pe.wait_ge(s["pt_ready"], 2 * Pi)
                for i in range(4):
                    w = unit_wait(u0, 6 * e + i, p)
                    if i == 2 or i == 3:
                        pe.wait_ge(s["down_out"], 4 * Ei + (-2 if i == 2 else 0)) if not (L == 0 and e == 0 and isinstance(p, int) and p == 0) else None
                    for k in range(KC):
                        ins = pe.matmul(bank[i][0:SLOTS, :], xin[:, e, k, :], w[:, k, :], start=(k == 0), stop=(k == KC - 1))
                    ins.then_inc(s["gu_mm"], 1)

            def expert_down(L, u0, p, e):
                Pi = 8 * L + p
                Ei = 16 * L + 2 * p + e
                for h in range(2):
                    pe.wait_ge(s["hid_ready"], 2 * Ei + (h + 1))
                    for i in range(4):
                        ins = pe.transpose(bank[4 + h][:, i * SLOTS:(i + 1) * SLOTS], hid[0:SLOTS, h, i * P:(i + 1) * P],
                                           ident[0:SLOTS, 0:SLOTS])
                    ins.then_inc(s["hidT_tr"], 1)
                pe.wait_ge(s["hidT_ready"], 2 * Ei + 2)
                for h in range(2):
                    w = unit_wait(u0, 6 * e + 4 + h, p)
                    for k in range(KC):
                        ins = pe.matmul(bank[2 + h][0:SLOTS, :], hidT[:, k, :], w[:, k, :], start=(k == 0), stop=(k == KC - 1))
                    ins.then_inc(s["down_mm"], 1)

            def pair(L, u0, p, first, last):
                Pi = 8 * L + p
                expert(L, u0, p, 0)
                if not first:
                    combine(Pi - 1)
                expert_down(L, u0, p, 0)
                expert(L, u0, p, 1)
                pe.wait_ge(s["pg_ready"], Pi + 1)
                pe.wait_ge(s["hid_ready"], 4 * Pi + 3)
                for t in range(NS):
                    ins = pe.transpose(bank[0][:, t * P:(t + 1) * P], pg[:, t, :], ident)
                ins.then_inc(s["pt_tr"], 1)
                pe.transpose(bank[1][0:64, 0:P], pg_p[:, :, :], ident).then_inc(s["pt_tr"], 1)
                if not last:
                    if not first:
                        pe.wait_ge(s["comb_added"], 10 * Pi)
                    gather(Pi + 1)
                    pe.wait_ge(s["xin_ready"], 16 * Pi + 24)
                expert_down(L, u0, p, 1)

            def moe(L, u0):
                b = 2 * L + 1
                build_hT(b)
                gates(b)
                hT_whole(b)
                pe.wait_ge(s["gate_ready"], 4 * (b + 1))
                pe.wait_ge(s["wr_loaded"], 16)
                for t in range(NT):
                    for k in range(KC):
                        ins = pe.matmul(bank[4][:, t * EXPERTS:(t + 1) * EXPERTS], hT[:, k, t * P:(t + 1) * P],
                                        wr[:, L, k, :], start=(k == 0), stop=(k == KC - 1))
                ins.then_inc(s["logits_mm"], 1)
                pe.wait_ge(s["aff_ready"], L + 1)
                for t in range(NT):
                    out = bank[5][0:EXPERTS, t * P:(t + 1) * P] if t < NS else bank[6][0:EXPERTS, 0:P]
                    ins = pe.transpose(out, aff[:, t, :], ident)
                ins.then_inc(s["aff_tr"], 1)
                pe.wait_ge(s["posm_ready"], L + 1)
                for t in range(NT):
                    ins = pe.transpose(bank[4][:, t * EXPERTS:(t + 1) * EXPERTS], pos[0:EXPERTS, t * P:(t + 1) * P],
                                       ident[0:EXPERTS, 0:EXPERTS])
                ins.then_inc(s["pos_tr"], 1)
                gather(8 * L)
                pair(L, u0, 0, True, False)
                with pe.Fori(1, PAIRS - 1) as p:
                    pair(L, u0, p, False, False)
                pair(L, u0, PAIRS - 1, False, True)
                combine(8 * L + 7)

            moe(0, U_MOE0)

            build_hT(2)
            gates(2)
            hT_whole(2)
            pe.wait_ge(s["gate_ready"], 12)
            pe.wait_ge(s["ssdp_loaded"], 32)
            for t in range(NT):
                for k in range(KC):
                    ins = pe.matmul(bank[7][:, t * 64:(t + 1) * 64], hT[:, k, t * P:(t + 1) * P], wdt[:, k, :],
                                    start=(k == 0), stop=(k == KC - 1))
            ins.then_inc(s["dtr_mm"], 1)

            def ssd_project(g, j, w):
                i = 6 * g + j
                if i >= 2:
                    pe.wait_ge(s["raw_ready"], i - 1)
                c0 = (j if j < 2 else j - 2) * P
                for k in range(KC):
                    pe.matmul(bank[i % 2][:, :], w[:, k, c0:c0 + P], hT[:, k, 0:SAMPLE], start=(k == 0), stop=(k == KC - 1))
                    ins = pe.matmul(bank[2 + i % 2][:, 0:P], w[:, k, c0:c0 + P], hT[:, k, SAMPLE:TOK],
                                    start=(k == 0), stop=(k == KC - 1))
                ins.then_inc(s["cproj_mm"], 1)

            def ssd_turn(g, j):
                i = 6 * g + j
                n = 5 * g + (0 if j == 0 else j - 1)
                pe.wait_ge(s["xf_ready"], i + 1)
                if n >= 2:
                    pe.wait_ge(s["xs_a"], n - 1)
                    pe.wait_ge(s["xs_v"], n - 1)
                src = BT if j == 0 else xf[:, j % 2, :]
                for t in range(NT):
                    out = bank[4 + n % 2][:, t * P:(t + 1) * P] if t < NS else bank[6 + n % 2][:, 0:P]
                    ins = pe.transpose(out, src[:, t * P:(t + 1) * P], ident)
                ins.then_inc(s["xtr_mm"], 1)

            for g in range(GROUPS):
                u0 = U_SSD + 4 * g
                if g:
                    pe.wait_ge(s["out_added"], 10 * g)
                j0 = u0 % R
                pe.wait_ge(landed[j0], 16 * (u0 // R + 1))
                w_bc = ring[j0][:, 0:UNIT // 2].rearrange("p (k n) -> p k n", n=256)
                ssd_project(g, 0, w_bc)
                if g == 0:
                    pe.wait_ge(s["dt_a"], 1)
                ssd_project(g, 1, w_bc)
                w_x = unit_wait(u0, 1)
                for j in range(2, 6):
                    ssd_project(g, j, w_x)
                    if j != 3:
                        ssd_turn(g, j - 2)
                ssd_turn(g, 4)
                ssd_turn(g, 5)
                if g == 0:
                    pe.wait_ge(s["da_ready"], 1)
                    pe.wait_ge(s["xs_a"], 5)
                    pe.wait_ge(s["xs_v"], 5)
                    for c in range(NT):
                        bk = bank[(7, 7, 6, 6, 5)[c]]
                        o = 192 * (c % 2)
                        pe.matmul(bk[:, o:o + 32], m_le, da[:, c, 0:32], start=True, stop=True)
                        pe.matmul(bk[:, o + 32:o + 64], m_ge, da[:, c, 32:64], start=True, stop=True)
                        pe.matmul(bk[:, o + 64:o + 96], m_gt, da[:, c, 0:32], start=True, stop=True)
                        pe.matmul(bk[:, o + 96:o + 128], m_lt, da[:, c, 32:64], start=True, stop=True)
                        pe.matmul(bk[:, o + 128:o + 192], ones, da[:, c, :], start=True, stop=True).then_inc(s["cum_mm"], 1)
                pe.wait_ge(s["xs_a"], 5 * g + 5)
                pe.wait_ge(s["xs_v"], 5 * g + 5)
                if g == 0:
                    pe.wait_ge(s["ex_ready"], 5)
                for c in range(NT):
                    out = bank[4][:, c * P:(c + 1) * P] if c < NS else bank[5][:, 0:P]
                    ins = pe.matmul(out, BT[:, c * P:(c + 1) * P], CT[:, c * P:(c + 1) * P], start=True, stop=True)
                ins.then_inc(s["cb_mm"], 1)
                pe.wait_ge(s["raw_ready"], 6 * g + 6)
                pe.wait_ge(s["cbm_ready"], 4 * (g + 1))

                def seg(i):
                    n = 10 * g + i
                    if n >= 2:
                        pe.wait_ge(s["exp_m"], 2 * (n - 1))
                    for dr in range(2):
                        pe.wait_ge(s["aM_ready"], 2 * n + dr + 1)
                        for h in range(4):
                            ins = pe.matmul(bank[2 * dr + n % 2][:, h * P:(h + 1) * P],
                                            aM[:, 2 * (n % 2) + dr, h * P:(h + 1) * P], m_le if dr == 0 else m_ge,
                                            start=True, stop=True)
                        ins.then_inc(s["seg_mm"], 1)

                def ydiag(i):
                    n = 10 * g + i
                    if n >= 2:
                        pe.wait_ge(s["yd_added"], n - 1)
                    pe.wait_ge(s["m_ready"], 2 * n + 2)
                    pe.wait_ge(s["xd_ready"], 2 * n + 2)
                    for h in range(4):
                        for dr in range(2):
                            a = 2 * (n % 2) + dr
                            ins = pe.matmul(bank[4 + n % 2][:, h * HD:(h + 1) * HD], Em[:, a, h * P:(h + 1) * P],
                                            Xd[:, a, h * HD:(h + 1) * HD], start=(dr == 0), stop=(dr == 1))
                    ins.then_inc(s["yd_mm"], 1)

                seg(0)
                for i in range(1, 2 * NT):
                    seg(i)
                    ydiag(i - 1)
                ydiag(2 * NT - 1)
                for i, (dr, c, off, stt) in enumerate(scan_tasks()):
                    noff = 8 * g + sum(x[2] for x in scan_tasks()[:i])
                    nst = 8 * g + sum(x[3] for x in scan_tasks()[:i])
                    if off:
                        if noff:
                            pe.wait_ge(s["off_added"], noff)
                        pe.wait_ge(s["state_loaded"], 32 * (g + 1))
                        if nst:
                            pe.wait_ge(s["prev_ready"], nst)
                        pe.matmul(bank[6][:, :], CT[:, c * P:(c + 1) * P], prevS[:, dr, :], start=True, stop=True)\
                          .then_inc(s["off_mm"], 1)
                    if stt:
                        pe.wait_ge(s["xw_ready"], nst + 1)
                        if nst:
                            pe.wait_ge(s["prev_ready"], nst)
                        pe.matmul(bank[7][:, :], Btok[:, c, :], xw[:, nst % 2, :], start=True, stop=True)\
                          .then_inc(s["st_mm"], 1)
                w = unit_wait(u0, 2)
                for t in range(NT):
                    n = NT * g + t
                    if t >= 4:
                        pe.wait_ge(s["z_silu"], n - 3)
                    for k in range(KC):
                        ins = pe.matmul(bank[t % 4][:, :], hT[:, k, t * P:(t + 1) * P], w[:, k, :],
                                        start=(k == 0), stop=(k == KC - 1))
                    ins.then_inc(s["z_mm"], 1)
                pe.wait_ge(s["yd_added"], 10 * (g + 1))
                for t in range(NT):
                    n = NT * g + t
                    pe.wait_ge(s["y_normed"], n + 1)
                    if t >= 2:
                        pe.wait_ge(s["yT_ready"], 4 * (n - 1))
                    for i in range(4):
                        ins = pe.transpose(bank[4 + t % 2][:, i * P:(i + 1) * P], Y[:, t, i * P:(i + 1) * P], ident)
                    ins.then_inc(s["ytr_mm"], 1)
                j3 = (u0 + 3) % R
                pe.wait_ge(landed[j3], 16 * ((u0 + 3) // R + 1))
                w_o = ring[j3][:, :].rearrange("p (k n) -> p k n", n=D)
                pe.wait_ge(s["yT_ready"], 20 * (g + 1))
                pe.wait_ge(s["z_silu"], NT * (g + 1))
                for i in range(2 * NT):
                    t, h = i // 2, i % 2
                    if i >= 8:
                        pe.wait_ge(s["out_added"], 10 * g + i - 7)
                    for k in range(4):
                        ins = pe.matmul(bank[i % 8][:, :], yT[:, k, t * P:(t + 1) * P], w_o[:, k, h * 512:(h + 1) * 512],
                                        start=(k == 0), stop=(k == 3))
                    ins.then_inc(s["out_mm"], 1)

            moe(1, U_MOE1)

        @block.scalar
        def _(act):
            step = Steps(act, s["act_step"])
            A = nc.scalar.activation

            def ada(L):
                def bias_cols(u):
                    act.wait_ge(s["ada_tr"], 12 * L + u + 1)
                    if L == 0 and u == 0:
                        act.wait_ge(s["adab_ready"], 4)
                    for i in range(4):
                        c = 4 * u + i
                        A(mT[:, L, c, :], bank[6 + u % 2][:, 2 * i:2 * i + 2], ACT.Identity,
                          bias=ada_bT[:, 48 * L + c:48 * L + c + 1]).then_inc(s["mT_ready"], 1)

                for u in range(12):
                    act.wait_ge(s["ada_mm"], 12 * L + u + 1)
                    if u >= 2:
                        act.wait_ge(s["ada_tr"], 12 * L + u - 1)
                    A(mrow[0:2, u % 2, :], bank[4 + u % 2][0:2, :], ACT.Copy).then_inc(s["mrow_ready"], 1)
                    if u:
                        bias_cols(u - 1)
                bias_cols(11)

            def hT_evac(b):
                L, sh = b // 2, shift_part(b)
                act.wait_ge(s["mT_ready"], 48 * (L + 1))
                for k in range(KC):
                    act.wait_ge(s["hT_tr"], 8 * b + k + 1)
                    A(hT[:, k, 0:SAMPLE], bank[k % 2][:, :], ACT.Identity, bias=mT[:, L, sh + k, 0:1],
                      scale=mT[:, L, sh + 8 + k, 0:1]).then_inc(s["hTs_ready"], 1)

            def gate_evac(b):
                for i in range(4):
                    act.wait_ge(s["gate_mm"], 4 * b + i + 1)
                    A(gate_bc[:, i // 2, (i % 2) * 512:(i % 2 + 1) * 512], bank[4 + i][:, :], ACT.Copy)\
                        .then_inc(s["gate_ready"], 1)

            def ln_sqrt(b):
                act.wait_ge(s["ln_stat"], b + 1)
                A(rst[:, :], rst[:, :], ACT.Sqrt).then_inc(s["ln_rstd"], 1)

            act.wait_ge(s["par_loaded"], 16)
            A(csil[:, :, :].rearrange("p a b -> p (a b)"), cond, ACT.Silu).then_inc(s["cond_ready"], 1)
            ada(0)
            hT_evac(0)
            gate_evac(0)
            act.wait_ge(s["upad_zero"], 1)
            for i in range(16):
                c = (i // 8) * 4 + i % 4
                act.wait_ge(s["pw1_done"], i + 1)
                a, b = bank[i % 2], bank[2 + i % 2]
                if (i // 4) % 2 == 0:
                    bias = pw1_b[:, c:c + 1]
                    step(A(upad[:, c, 0:8, HALO:HALO + GRID_W], a[:, :].rearrange("p (r w) -> p r w", w=GRID_W),
                           ACT.Identity, bias=bias))
                    step(A(upad[:, c, 8, HALO:PITCH], b[:, 0:PITCH - HALO], ACT.Identity, bias=bias))
                    step.sync()
                    A(upad[:, c, 9, 0:PITCH - HALO], b[:, GRID_W - HALO:P], ACT.Identity, bias=bias).then_inc(s["glu_a"], 1)
                else:
                    ng = (i // 8) * 4 + i % 4
                    if ng >= 2:
                        act.wait_ge(s["glu_sig"], ng - 1)
                    bias = pw1_b[:, 8 + c:9 + c]
                    step(A(sig[:, ng % 2, 0:SAMPLE], a[:, :], ACT.Sigmoid, bias=bias))
                    step.sync()
                    A(sig[:, ng % 2, SAMPLE:TOK], b[:, 0:P], ACT.Sigmoid, bias=bias).then_inc(s["glu_a"], 1)
            ada(1)
            for k in range(KC):
                act.wait_ge(s["centered"], k + 1)
                if k >= 2:
                    act.wait_ge(s["var_mm"], k - 1)
                A(sq[:, k % 2, :], v[:, k, :], ACT.Square).then_inc(s["sq_ready"], 1)
            act.wait_ge(s["var_ready"], 2)
            A(rstd, rstd, ACT.Sqrt).then_inc(s["rstd_ready"], 1)
            for k in range(KC):
                act.wait_ge(s["normed"], k + 1)
                A(v[:, k, :], v[:, k, :], ACT.Silu, bias=cln_b[:, k:k + 1], scale=cln_g[:, k:k + 1])\
                    .then_inc(s["v_ready"], 1)
            ln_sqrt(0)

            def xin_evac(L, Pi):
                sh = shift_part(1)
                act.wait_ge(s["gather_mm"], 3 * Pi + 1)
                for k in range(KC):
                    A(xin[:, :, k, CAP_S:SLOTS],
                      bank[5][:, 128 + 32 * k:160 + 32 * k].rearrange("p (e c) -> p e c", c=CAP_P), ACT.Identity,
                      bias=mT[:, L, sh + k, 1:2], scale=mT[:, L, sh + 8 + k, 1:2]).then_inc(s["xin_ready"], 1)
                for k in range(KC):
                    if k % 4 == 0:
                        act.wait_ge(s["gather_mm"], 3 * Pi + (2 + k // 4))
                    A(xin[:, :, k, 0:CAP_S],
                      bank[6 + k // 4][:, (k % 4) * P:(k % 4 + 1) * P].rearrange("p (e c) -> p e c", c=CAP_S),
                      ACT.Identity, bias=mT[:, L, sh + k, 0:1], scale=mT[:, L, sh + 8 + k, 0:1])\
                        .then_inc(s["xin_ready"], 1)

            def silus(L, p, e):
                Ei = 16 * L + 2 * p + e
                for h in range(2):
                    act.wait_ge(s["gu_mm"], 4 * Ei + (2 * h + 1))
                    if not (L == 0 and e == 0 and isinstance(p, int) and p == 0):
                        act.wait_ge(s["hid_ready"], 2 * Ei + (h - 1))
                    A(sil[0:SLOTS, h, :], bank[2 * h][0:SLOTS, :], ACT.Silu).then_inc(s["silu_ready"], 1)

            def down_evac(L, p, e):
                Ei = 16 * L + 2 * p + e
                for h in range(2):
                    act.wait_ge(s["down_mm"], 2 * Ei + (h + 1))
                    c = slice(h * 512, (h + 1) * 512)
                    A(out_s[64 * e:64 * e + CAP_S, c], bank[2 + h][0:CAP_S, :], ACT.Copy).then_inc(s["down_out"], 1)
                    A(out_p[32 * e:32 * e + CAP_P, c], bank[2 + h][CAP_S:SLOTS, :], ACT.Copy).then_inc(s["down_out"], 1)

            def pair(L, p, last):
                Pi = 8 * L + p
                silus(L, p, 0)
                down_evac(L, p, 0)
                silus(L, p, 1)
                act.wait_ge(s["pt_tr"], 2 * Pi + 1)
                A(PT, bank[0][:, :], ACT.Copy).then_inc(s["pt_ready"], 1)
                act.wait_ge(s["pt_tr"], 2 * Pi + 2)
                A(PT_p[0:64, :], bank[1][0:64, 0:P], ACT.Copy).then_inc(s["pt_ready"], 1)
                if not last:
                    xin_evac(L, Pi + 1)
                down_evac(L, p, 1)

            def moe(L):
                b = 2 * L + 1
                hT_evac(b)
                gate_evac(b)
                act.wait_ge(s["lg_ready"], L + 1)
                A(lg, lg, ACT.Exp).then_inc(s["exp_ready"], 1)
                xin_evac(L, 8 * L)
                pair(L, 0, False)
                with act.Fori(1, PAIRS - 1) as p:
                    pair(L, p, False)
                pair(L, PAIRS - 1, True)
                ln_sqrt(b)

            moe(0)

            hT_evac(2)
            gate_evac(2)
            act.wait_ge(s["ssdp_loaded"], 32)
            A(srow[:, 64:128], srow[:, 64:128], ACT.Exp).then_inc(s["dt_b"], 1)
            act.wait_ge(s["dt_a"], 2)
            A(dtmp[:, 1, :], dtmp[:, 1, :], ACT.Exp).then_inc(s["dt_b"], 1)
            act.wait_ge(s["dt_a"], 3)
            A(dtmp[:, 2, :], dtmp[:, 2, :], ACT.Ln).then_inc(s["dt_b"], 1)

            def ssd_raw(g, j):
                i = 6 * g + j
                act.wait_ge(s["cproj_mm"], i + 1)
                if i >= 2:
                    act.wait_ge(s["cconv_ready"], i - 1)
                step(A(raw[:, i % 2, 2:2 + SAMPLE], bank[i % 2][:, :], ACT.Copy))
                step.sync()
                A(raw[:, i % 2, SAMPLE + 6:SAMPLE + 6 + P], bank[2 + i % 2][:, 0:P], ACT.Copy).then_inc(s["raw_ready"], 1)

            def ssd_silu(g, j):
                i = 6 * g + j
                act.wait_ge(s["cconv_ready"], i + 1)
                if j >= 4:
                    act.wait_ge(s["xtr_mm"], 5 * g + j - 2)
                dst = (BT, CT)[j] if j < 2 else xf[:, j % 2, :]
                A(dst, cv[:, i % 2, :], ACT.Silu).then_inc(s["xf_ready"], 1)

            def ssd_xs(g, j):
                n = 5 * g + (0 if j == 0 else j - 1)
                act.wait_ge(s["xtr_mm"], n + 1)
                src = bank[4 + n % 2][:, :].rearrange("p (t c) -> p t c", c=P)
                dst = Btok[:, 0:NS, :] if j == 0 else xs[:, 0:NS, (j - 2) * P:(j - 1) * P]
                A(dst, src, ACT.Copy).then_inc(s["xs_a"], 1)

            for g in range(GROUPS):
                if g:
                    act.wait_ge(s["out_mm"], 10 * g)
                act.wait_ge(s["upad_zero"], g + 2)
                ssd_raw(g, 0)
                for j in range(6):
                    if j < 5:
                        ssd_raw(g, j + 1)
                    ssd_silu(g, j)
                    if j == 2:
                        ssd_xs(g, 0)
                    if j >= 4:
                        ssd_xs(g, j - 2)
                ssd_xs(g, 4)
                ssd_xs(g, 5)
                if g == 0:
                    for c in range(NT):
                        act.wait_ge(s["cum_mm"], NT)
                        o = 192 * (c % 2)
                        A(Ex[:, c, :], bank[(7, 7, 6, 6, 5)[c]][:, o:o + 192], ACT.Exp).then_inc(s["ex_ready"], 1)
                for i in range(2 * NT):
                    n = 10 * g + i
                    if n >= 2:
                        act.wait_ge(s["yd_mm"], n - 1)
                    for dr in range(2):
                        act.wait_ge(s["seg_mm"], 2 * n + dr + 1)
                        A(Em[:, 2 * (n % 2) + dr, :], bank[2 * dr + n % 2][:, :], ACT.Exp).then_inc(s["exp_m"], 1)
                for t in range(NT):
                    n = NT * g + t
                    act.wait_ge(s["z_mm"], n + 1)
                    if n >= 2:
                        act.wait_ge(s["y_z"], n - 1)
                    A(zt[:, n % 2, :], bank[t % 4][:, :], ACT.Silu).then_inc(s["z_silu"], 1)
                act.wait_ge(s["rms_a"], g + 1)
                A(rms[:, 1, :], rms[:, 1, :], ACT.Sqrt).then_inc(s["rms_b"], 1)
                for t in range(NT):
                    n = NT * g + t
                    act.wait_ge(s["ytr_mm"], n + 1)
                    for i in range(4):
                        A(yT[:, i, t * P:(t + 1) * P], bank[4 + t % 2][:, i * P:(i + 1) * P], ACT.Copy,
                          scale=norm_w[:, 4 * g + i:4 * g + i + 1]).then_inc(s["yT_ready"], 1)
            ln_sqrt(2)
            moe(1)

        @block.gpsimd
        def _(pool):
            step = Steps(pool, s["pool_step"])
            pool.dma_start(wr[:, :, :, :], router).then_inc(s["wr_loaded"], 16)
            pool.dma_start(pwb[0:1, :], pw2_b).then_inc(s["pwb_loaded"], 16)
            pool.dma_start(ln_gb[:, :, :], ln_rows[0:1].partition_broadcast(P)).then_inc(s["ln_loaded"], 16)
            nc.gpsimd.memset(upad.rearrange("p a b c -> p (a b c)"), 0.0).then_inc(s["upad_zero"], 1)
            for b in range(1, 4):
                pool.wait_ge(s["x_ready"], 5 * b)
                pool.wait_ge(s["ln_loaded"], 16 * b)
                pool.dma_start(ln_gb[:, :, :], ln_rows[b:b + 1].partition_broadcast(P)).then_inc(s["ln_loaded"], 16)
                if b != 2:
                    continue
                pool.dma_start(srow, ssd_rows.partition_broadcast(P)).then_inc(s["ssdp_loaded"], 16)
                pool.dma_start(wdt, w_dt).then_inc(s["ssdp_loaded"], 16)
                for g in range(GROUPS):
                    if g:
                        pool.wait_ge(s["out_mm"], 10 * g)
                    nc.gpsimd.memset(raw, 0.0).then_inc(s["upad_zero"], 1)
                    for dr in range(2):
                        if g:
                            pool.wait_ge(s["off_mm"], 8 * g)
                            pool.wait_ge(s["st_out"], 32 * g)
                        pool.dma_start(prevS[:, dr, :], state_in[dr, :, g * GC:(g + 1) * GC]).then_inc(s["state_loaded"], 16)
                    pool.wait_ge(s["xs_a"], 5 * g + 5)
                    pool.wait_ge(s["xs_v"], 5 * g + 5)
                    for t in range(NT):
                        ins = nc.gpsimd.tensor_tensor(
                            Y[:, t, :].rearrange("p (h d) -> p h d", d=HD), xs[:, t, :].rearrange("p (h d) -> p h d", d=HD),
                            srow[:, 128 + HG * g:128 + HG * (g + 1)].rearrange("p (h d) -> p h d", d=1).broadcast_to([P, HG, HD]),
                            ALU.mult).then_inc(s["y_init"], 1)
                    if g == 0:
                        pool.wait_ge(s["da_ready"], 1)
                    for i in range(2 * NT):
                        n = 10 * g + i
                        c, q = i // 2, i % 2
                        if n >= 2:
                            pool.wait_ge(s["seg_mm"], 2 * (n - 1))
                        for dr in range(2):
                            h0 = 32 * dr + HG * g + 4 * q
                            nc.gpsimd.tensor_tensor(
                                aM[:, 2 * (n % 2) + dr, :].rearrange("p (h k) -> p h k", k=P),
                                (m_gt if dr == 0 else m_lt).rearrange("p (h k) -> p h k", h=1).broadcast_to([P, 4, P]),
                                da[:, c, h0:h0 + 4].rearrange("p (h k) -> p h k", k=1).broadcast_to([P, 4, P]),
                                ALU.mult).then_inc(s["aM_ready"], 1)
                    for k, (dr, c, _, _) in enumerate([x for x in scan_tasks() if x[3]]):
                        n = 8 * g + k
                        if n >= 2:
                            pool.wait_ge(s["st_mm"], n - 1)
                        if n == 0:
                            pool.wait_ge(s["dt_c"], 1)
                        h0 = 32 * dr + HG * g
                        nc.gpsimd.tensor_tensor(
                            xw[:, n % 2, :].rearrange("p (h d) -> p h d", d=HD), xs[:, c, :].rearrange("p (h d) -> p h d", d=HD),
                            wst[:, c, h0:h0 + HG].rearrange("p (h d) -> p h d", d=1).broadcast_to([P, HG, HD]),
                            ALU.mult).then_inc(s["xw_ready"], 1)
                        if k == 3 or k == 7:
                            pool.wait_ge(s["prev_ready"], n + 1)
                            pool.dma_start(state_out[dr, :, g * GC:(g + 1) * GC], prevS[:, dr, :]).then_inc(s["st_out"], 16)

        @block.vector
        def _(dve):
            V = nc.vector
            step = Steps(dve, s["dve_step"])

            def link(ins):
                step(ins)
                step.sync()

            def hT_evac(b):
                L, sh = b // 2, shift_part(b)
                dve.wait_ge(s["mT_ready"], 48 * (L + 1))
                for k in range(KC):
                    dve.wait_ge(s["hT_tr"], 8 * b + k + 1)
                    V.tensor_scalar(hT[:, k, SAMPLE:TOK], bank[2 + k % 2][:, 0:P], mT[:, L, sh + 8 + k, 1:2],
                                    mT[:, L, sh + k, 1:2], ALU.mult, ALU.add).then_inc(s["hTp_ready"], 1)

            def residual(f, t, h, buf, out_sem=None):
                c = slice(h * 512, (h + 1) * 512)
                link(V.tensor_tensor(tmp[:, buf, :], f, gate_bc[:, int(t == NS), c], ALU.mult))
                ins = V.scalar_tensor_tensor(X[:, t, c], X[:, t, c], ALPHA, tmp[:, buf, :], ALU.mult, ALU.add)
                if out_sem is not None:
                    ins.then_inc(out_sem, 1)
                else:
                    step(ins)

            def layer_norm(b):
                step.sync()
                if b == 0:
                    dve.wait_ge(s["f_added"], 10)
                for t in range(NT):
                    for h in range(2):
                        step(V.bn_stats(st[:, t, h, :], X[:, t, h * 512:(h + 1) * 512]))
                step.sync()
                for t in range(NT):
                    step(V.bn_aggr(mv[:, t, :], st[:, t, :, :]))
                step.sync()
                link(V.tensor_scalar(rst[:, :], mv[:, :, 1], EPS, None, ALU.add))
                V.reciprocal(rst[:, :], rst[:, :]).then_inc(s["ln_stat"], 1)
                dve.wait_ge(s["ln_rstd"], b + 1)
                dve.wait_ge(s["ln_loaded"], 16 * (b + 1))
                for t in range(NT):
                    link(V.tensor_scalar(X[:, t, :], X[:, t, :], mv[:, t, 0:1], rst[:, t:t + 1], ALU.subtract, ALU.mult))
                    link(V.tensor_tensor(X[:, t, :], X[:, t, :], ln_gb[:, 0, :], ALU.mult))
                    V.tensor_tensor(X[:, t, :], X[:, t, :], ln_gb[:, 1, :], ALU.add).then_inc(s["x_ready"], 1)

            dve.wait_ge(s["par_loaded"], 16)
            for L in range(DEPTH):
                for c in (8, 32):
                    V.tensor_scalar(ada_bT[:, 48 * L + c:48 * L + c + 8], ada_bT[:, 48 * L + c:48 * L + c + 8],
                                    1.0, None, ALU.add).then_inc(s["adab_ready"], 1)
            hT_evac(0)
            for c in range(KC):
                i = (c // 4) * 8 + 4 + c % 4
                dve.wait_ge(s["glu_a"], i + 1)
                step(V.tensor_tensor(upad[:, c, 0:8, HALO:HALO + GRID_W], upad[:, c, 0:8, HALO:HALO + GRID_W],
                                     sig[:, c % 2, 0:SAMPLE].rearrange("p (r w) -> p r w", w=GRID_W), ALU.mult))
                step(V.tensor_tensor(upad[:, c, 8, HALO:PITCH], upad[:, c, 8, HALO:PITCH],
                                     sig[:, c % 2, SAMPLE:SAMPLE + PITCH - HALO], ALU.mult))
                step.sync()
                V.tensor_tensor(upad[:, c, 9, 0:PITCH - HALO], upad[:, c, 9, 0:PITCH - HALO],
                                sig[:, c % 2, SAMPLE + GRID_W - HALO:TOK], ALU.mult).then_inc(s["glu_sig"], 1)
                dve.wait_ge(s["glu_sig"], c + 1)
                vr = v[:, c, :].rearrange("p (r w) -> p r w", w=GRID_W)
                link(V.tensor_scalar(vr, upad[:, c, :, 0:GRID_W], dw_w[:, c, 0:1], dw_b[:, c:c + 1], ALU.mult, ALU.add))
                for k in range(1, TAPS):
                    ins = V.scalar_tensor_tensor(vr, upad[:, c, :, k:k + GRID_W], dw_w[:, c, k:k + 1], vr, ALU.mult, ALU.add)
                    if k < TAPS - 1:
                        link(ins)
                    else:
                        ins.then_inc(s["conv_ready"], 1)
            dve.wait_ge(s["conv_ready"], 8)
            dve.wait_ge(s["mean_mm"], 1)
            for k in range(KC):
                step(V.tensor_tensor(v[:, k, 0:SAMPLE], v[:, k, 0:SAMPLE], bank[0][:, :], ALU.subtract))
                step.sync()
                V.tensor_tensor(v[:, k, SAMPLE:TOK], v[:, k, SAMPLE:TOK], bank[2][:, 0:P], ALU.subtract).then_inc(s["centered"], 1)
            dve.wait_ge(s["var_mm"], 8)
            step(V.tensor_scalar(rstd[:, 0:SAMPLE], bank[1][:, :], EPS, None, ALU.add))
            link(V.tensor_scalar(rstd[:, SAMPLE:TOK], bank[3][:, 0:P], EPS, None, ALU.add))
            V.reciprocal(rstd[:, 0:SAMPLE], rstd[:, 0:SAMPLE]).then_inc(s["var_ready"], 1)
            V.reciprocal(rstd[:, SAMPLE:TOK], rstd[:, SAMPLE:TOK]).then_inc(s["var_ready"], 1)
            dve.wait_ge(s["rstd_ready"], 1)
            dve.wait_ge(s["centered"], 8)
            for k in range(KC):
                V.tensor_tensor(v[:, k, :], v[:, k, :], rstd, ALU.mult).then_inc(s["normed"], 1)
            dve.wait_ge(s["gate_ready"], 4)
            for i in range(2 * NT):
                dve.wait_ge(s["f_mm"], i + 1)
                if i >= 2:
                    dve.wait_ge(s["f_added"], i - 1)
                residual(bank[i % 8][:, :], i % NT, i // NT, i % 2, s["f_added"])
            layer_norm(0)

            def build_pg(L, p):
                Pi = 8 * L + p
                link(V.tensor_copy(ccol[:, 0, :, :], posT[:, :, bass.ds(2 * p, 2)]))
                link(V.tensor_copy(ccol[:, 1, :, :], aff[:, :, bass.ds(2 * p, 2)]))
                if not (L == 0 and isinstance(p, int) and p == 0):
                    dve.wait_ge(s["pt_tr"], 2 * Pi)
                for e in range(2):
                    for t in range(NS):
                        step(V.tensor_scalar(pg[:, t, e * CAP_S:(e + 1) * CAP_S], iota, ccol[:, 0, t, e:e + 1],
                                             ccol[:, 1, t, e:e + 1], ALU.is_equal, ALU.mult))
                step(V.tensor_scalar(pg_p[:, 0, :], iota[:, 0:32], ccol[:, 0, NS, 0:1], ccol[:, 1, NS, 0:1],
                                     ALU.is_equal, ALU.mult))
                step.sync()
                V.tensor_scalar(pg_p[:, 1, :], iota[:, 0:32], ccol[:, 0, NS, 1:2], ccol[:, 1, NS, 1:2],
                                ALU.is_equal, ALU.mult).then_inc(s["pg_ready"], 1)

            def build_psel(L, p):
                Pi = 8 * L + p
                link(V.tensor_copy(ccol[:, 2, :, :], posT[:, :, bass.ds(2 * p, 2)]))
                if not (isinstance(Pi, int) and Pi == 0):
                    dve.wait_ge(s["gather_mm"], 3 * Pi)
                for e in range(2):
                    for t in range(NS):
                        step(V.tensor_scalar(psel[:, t, e, :], iota, ccol[:, 2, t, e:e + 1], None, ALU.is_equal))
                step(V.tensor_scalar(psel_p[:, 0, :], iota[:, 0:CAP_P], ccol[:, 2, NS, 0:1], None, ALU.is_equal))
                step.sync()
                V.tensor_scalar(psel_p[:, 1, :], iota[:, 0:CAP_P], ccol[:, 2, NS, 1:2], None, ALU.is_equal)\
                 .then_inc(s["psel_ready"], 1)

            def hids(L, p, e):
                Ei = 16 * L + 2 * p + e
                if not (L == 0 and e == 0 and isinstance(p, int) and p == 0):
                    dve.wait_ge(s["hidT_tr"], 2 * Ei)
                for h in range(2):
                    dve.wait_ge(s["silu_ready"], 2 * Ei + (h + 1))
                    dve.wait_ge(s["gu_mm"], 4 * Ei + (2 * h + 2))
                    V.tensor_tensor(hid[0:SLOTS, h, :], sil[0:SLOTS, h, :], bank[2 * h + 1][0:SLOTS, :], ALU.mult)\
                     .then_inc(s["hid_ready"], 1)

            def hidT_evac(L, p, e):
                Ei = 16 * L + 2 * p + e
                for h in range(2):
                    dve.wait_ge(s["hidT_tr"], 2 * Ei + (h + 1))
                    V.tensor_copy(hidT[:, 4 * h:4 * h + 4, :],
                                  bank[4 + h][:, 0:4 * SLOTS].rearrange("p (k c) -> p k c", c=SLOTS))\
                     .then_inc(s["hidT_ready"], 1)

            def comb_add(Pi):
                dve.wait_ge(s["comb_added"], 10 * Pi) if not (isinstance(Pi, int) and Pi == 0) else None
                for i in range(2 * NT):
                    t, h = i // 2, i % 2
                    dve.wait_ge(s["comb_mm"], 10 * Pi + (i + 1))
                    f = facc_m[:, t, h * 512:(h + 1) * 512]
                    V.tensor_tensor(f, f, bank[6 + h][:, :], ALU.add).then_inc(s["comb_added"], 1)

            def pair(L, p, first, last):
                build_pg(L, p)
                if not last:
                    build_psel(L, p + 1)
                hids(L, p, 0)
                if not first:
                    comb_add(8 * L + p - 1)
                hidT_evac(L, p, 0)
                hids(L, p, 1)
                hidT_evac(L, p, 1)

            def moe(L):
                b = 2 * L + 1
                hT_evac(b)
                f = facc_m.rearrange("p a b -> p (a b)")
                if L == 1:
                    dve.wait_ge(s["st_out"], 32 * GROUPS)
                step(V.memset(f, 0.0))
                step(V.memset(out_p, 0.0))
                dve.wait_ge(s["logits_mm"], L + 1)
                lgp = bank[4][:, 0:NT * EXPERTS].rearrange("p (t e) -> p t e", e=EXPERTS)

                def bc(x):
                    return x.rearrange("p (t e) -> p t e", e=1).broadcast_to([P, NT, EXPERTS])

                link(V.tensor_reduce(small[:, 0, :], lgp, AX.X, ALU.max))
                V.tensor_tensor(lg, lgp, bc(small[:, 0, :]), ALU.subtract).then_inc(s["lg_ready"], 1)
                dve.wait_ge(s["exp_ready"], L + 1)
                link(V.tensor_reduce(small[:, 1, :], lg, AX.X, ALU.add))
                link(V.reciprocal(small[:, 2, :], small[:, 1, :]))
                V.tensor_tensor(aff, lg, bc(small[:, 2, :]), ALU.mult).then_inc(s["aff_ready"], 1)
                dve.wait_ge(s["aff_ready"], L + 1)
                dve.wait_ge(s["aff_tr"], L + 1)
                E = EXPERTS
                step(V.tensor_copy(work[0:E, 0:SAMPLE], bank[5][0:E, :]))
                link(V.tensor_copy(work[0:E, SAMPLE:TOK], bank[6][0:E, 0:P]))
                for lo, hi, cap in ((0, SAMPLE, CAP_S), (SAMPLE, TOK, CAP_P)):
                    for _ in range(cap // 8):
                        link(V.max(top8[0:E, :], work[0:E, lo:hi]))
                        link(V.match_replace(work[0:E, lo:hi], top8[0:E, :], work[0:E, lo:hi], -1.0))
                link(V.tensor_scalar(work[0:E, :], work[0:E, :], 0.0, None, ALU.is_lt))
                step(V.memset(affT[0:E, :], 1.0))
                step.sync()
                for lo, hi in ((0, SAMPLE), (SAMPLE, TOK)):
                    step(V.tensor_tensor_scan(pos[0:E, lo:hi], affT[0:E, lo:hi], work[0:E, lo:hi], 0.0, ALU.mult, ALU.add))
                step.sync()
                V.tensor_tensor(pos[0:E, :], pos[0:E, :], work[0:E, :], ALU.mult).then_inc(s["posm_ready"], 1)
                dve.wait_ge(s["pos_tr"], L + 1)
                link(V.tensor_copy(posT, bank[4][:, 0:NT * EXPERTS].rearrange("p (t e) -> p t e", e=EXPERTS)))
                build_psel(L, 0)
                pair(L, 0, True, False)
                n0 = step.n
                per = PAIR_STEPS
                with dve.Fori(1, PAIRS - 1) as p:
                    step.off = (p - 1) * per
                    pair(L, p, False, False)
                assert step.n - n0 == per, step.n - n0
                step.off = 0
                step.n = n0 + per * (PAIRS - 2)
                pair(L, PAIRS - 1, False, True)
                comb_add(8 * L + 7)
                dve.wait_ge(s["comb_added"], 80 * (L + 1))
                dve.wait_ge(s["gate_ready"], 4 * (b + 1))
                for t in range(NT):
                    for h in range(2):
                        residual(facc_m[:, t, h * 512:(h + 1) * 512], t, h, h)
                layer_norm(b)

            moe(0)

            hT_evac(2)
            step(V.memset(facc_s.rearrange("p a b -> p (a b)"), 0.0))
            dve.wait_ge(s["ssdp_loaded"], 32)
            dve.wait_ge(s["dtr_mm"], 1)
            w2 = [dtmp[:, i, :].rearrange("p (t h) -> p t h", h=64) for i in range(3)]
            rowb = srow[:, 0:64].rearrange("p (t h) -> p t h", t=1).broadcast_to([P, NT, 64])
            arow = srow[:, 64:128].rearrange("p (t h) -> p t h", t=1).broadcast_to([P, NT, 64])
            V.tensor_tensor(dt, bank[7][:, 0:NT * 64].rearrange("p (t h) -> p t h", h=64), rowb, ALU.add).then_inc(s["dt_a"], 1)
            dve.wait_ge(s["dt_a"], 1)
            link(V.tensor_scalar(w2[0], dt, -1.0, None, ALU.mult))
            V.tensor_tensor(w2[1], dt, w2[0], ALU.min).then_inc(s["dt_a"], 1)
            dve.wait_ge(s["dt_a"], 2)
            dve.wait_ge(s["dt_b"], 2)
            link(V.tensor_scalar(w2[0], w2[1], 1.0, None, ALU.add))
            V.tensor_copy(w2[2], w2[0]).then_inc(s["dt_a"], 1)
            link(V.tensor_scalar(w2[0], w2[0], -1.0, None, ALU.add))
            step(V.tensor_scalar(wst, w2[0], 0.0, None, ALU.is_equal))
            dve.wait_ge(s["dt_a"], 3)
            dve.wait_ge(s["dt_b"], 3)
            step.sync()
            link(V.tensor_scalar(w2[0], w2[0], 1e-30, None, ALU.max))
            link(V.reciprocal(w2[0], w2[0]))
            step(V.tensor_tensor(w2[0], w2[0], w2[2], ALU.mult))
            step.sync()
            link(V.tensor_tensor(w2[0], w2[0], wst, ALU.add))
            link(V.tensor_tensor(w2[0], w2[0], w2[1], ALU.mult))
            link(V.scalar_tensor_tensor(dt, dt, 0.0, w2[0], ALU.max, ALU.add))
            V.scalar_tensor_tensor(da, dt, -1.0, arow, ALU.mult, ALU.mult).then_inc(s["da_ready"], 1)

            def conv(g, j):
                i = 6 * g + j
                dve.wait_ge(s["raw_ready"], i + 1)
                if i >= 2:
                    dve.wait_ge(s["xf_ready"], i - 1)
                ch = (16 + g) if j == 0 else (20 + g) if j == 1 else 4 * g + j - 2
                a, b = cv[:, i % 2, 0:SAMPLE], cv[:, i % 2, SAMPLE:TOK]
                ra, rb = raw[:, i % 2, 0:SAMPLE + 4], raw[:, i % 2, SAMPLE + 4:]
                step(V.tensor_scalar(a, ra[:, 0:SAMPLE], sc_w[:, ch, 0:1], sc_b[:, ch:ch + 1], ALU.mult, ALU.add))
                step(V.tensor_scalar(b, rb[:, 0:P], sc_w[:, ch, 0:1], sc_b[:, ch:ch + 1], ALU.mult, ALU.add))
                for k in range(1, STAPS):
                    step.sync()
                    step(V.scalar_tensor_tensor(a, ra[:, k:k + SAMPLE], sc_w[:, ch, k:k + 1], a, ALU.mult, ALU.add))
                    ins = V.scalar_tensor_tensor(b, rb[:, k:k + P], sc_w[:, ch, k:k + 1], b, ALU.mult, ALU.add)
                    if k < STAPS - 1:
                        step(ins)
                    else:
                        step.sync()
                        ins.then_inc(s["cconv_ready"], 1)

            def xs_evac(g, j):
                n = 5 * g + (0 if j == 0 else j - 1)
                dve.wait_ge(s["xtr_mm"], n + 1)
                dst = Btok[:, NS, :] if j == 0 else xs[:, NS, (j - 2) * P:(j - 1) * P]
                V.tensor_copy(dst, bank[6 + n % 2][:, 0:P]).then_inc(s["xs_v"], 1)

            for g in range(GROUPS):
                if g:
                    dve.wait_ge(s["out_mm"], 10 * g)
                for j in range(6):
                    conv(g, j)
                    if j == 3:
                        xs_evac(g, 0)
                    if j >= 4:
                        xs_evac(g, j - 2)
                xs_evac(g, 4)
                xs_evac(g, 5)
                if g == 0:
                    dve.wait_ge(s["ex_ready"], 5)
                    V.tensor_tensor(wst, dt, Ex[:, :, 64:128], ALU.mult).then_inc(s["dt_c"], 1)
                dve.wait_ge(s["cb_mm"], g + 1)
                for dr in range(2):
                    m = m_le if dr == 0 else m_ge
                    V.tensor_tensor(CBm[:, dr, 0:SAMPLE].rearrange("p (t k) -> p t k", k=P),
                                    bank[4][:, :].rearrange("p (t k) -> p t k", k=P),
                                    m.rearrange("p (t k) -> p t k", t=1).broadcast_to([P, NS, P]), ALU.mult)\
                     .then_inc(s["cbm_ready"], 1)
                    V.tensor_tensor(CBm[:, dr, SAMPLE:TOK], bank[5][:, 0:P], m, ALU.mult).then_inc(s["cbm_ready"], 1)
                dve.wait_ge(s["cbm_ready"], 4 * (g + 1))
                dve.wait_ge(s["y_init"], NT * (g + 1))
                for i in range(2 * NT + 1):
                    if i < 2 * NT:
                        n = 10 * g + i
                        c, q = i // 2, i % 2
                        for dr in range(2):
                            a = 2 * (n % 2) + dr
                            h0 = 32 * dr + HG * g + 4 * q
                            if n >= 2:
                                dve.wait_ge(s["yd_mm"], n - 1)
                            V.tensor_tensor(Xd[:, a, :].rearrange("p (h d) -> p h d", d=HD),
                                            xs[:, c, 256 * q:256 * (q + 1)].rearrange("p (h d) -> p h d", d=HD),
                                            dt[:, c, h0:h0 + 4].rearrange("p (h d) -> p h d", d=1).broadcast_to([P, 4, HD]),
                                            ALU.mult).then_inc(s["xd_ready"], 1)
                            dve.wait_ge(s["exp_m"], 2 * n + dr + 1)
                            V.tensor_tensor(Em[:, a, :].rearrange("p (h k) -> p h k", k=P),
                                            Em[:, a, :].rearrange("p (h k) -> p h k", k=P),
                                            CBm[:, dr, c * P:(c + 1) * P].rearrange("p (h k) -> p h k", h=1)
                                            .broadcast_to([P, 4, P]), ALU.mult).then_inc(s["m_ready"], 1)
                    if i:
                        n = 10 * g + i - 1
                        c, q = (i - 1) // 2, (i - 1) % 2
                        dve.wait_ge(s["yd_mm"], n + 1)
                        y = Y[:, c, 256 * q:256 * (q + 1)]
                        V.tensor_tensor(y, y, bank[4 + n % 2][:, 0:256], ALU.add).then_inc(s["yd_added"], 1)
                dve.wait_ge(s["yd_added"], 10 * (g + 1))
                dve.wait_ge(s["state_loaded"], 32 * (g + 1))
                for i, (dr, c, off, stt) in enumerate(scan_tasks()):
                    noff = 8 * g + sum(x[2] for x in scan_tasks()[:i])
                    nst = 8 * g + sum(x[3] for x in scan_tasks()[:i])
                    h0 = 32 * dr + HG * g

                    def bc(x):
                        return x.rearrange("p (h d) -> p h d", d=1).broadcast_to([P, HG, HD])

                    if off:
                        dve.wait_ge(s["off_mm"], noff + 1)
                        tm = tmp[:, noff % 2, :]
                        link(V.tensor_tensor(tm.rearrange("p (h d) -> p h d", d=HD),
                                             bank[6][:, :].rearrange("p (h d) -> p h d", d=HD),
                                             bc(Ex[:, c, h0:h0 + HG]), ALU.mult))
                        V.tensor_tensor(Y[:, c, :], Y[:, c, :], tm, ALU.add).then_inc(s["off_added"], 1)
                    if stt:
                        pv = prevS[:, dr, :]
                        dve.wait_ge(s["st_mm"], nst + 1)
                        if off:
                            link(V.tensor_tensor(pv.rearrange("p (h d) -> p h d", d=HD), pv.rearrange("p (h d) -> p h d", d=HD),
                                                 bc(Ex[:, c, 128 + h0:128 + h0 + HG]), ALU.mult))
                            V.tensor_tensor(pv, pv, bank[7][:, :], ALU.add).then_inc(s["prev_ready"], 1)
                        else:
                            V.tensor_copy(pv, bank[7][:, :]).then_inc(s["prev_ready"], 1)
                        dve.wait_ge(s["prev_ready"], nst + 1)
                dve.wait_ge(s["off_added"], 8 * (g + 1))
                for t in range(NT):
                    n = NT * g + t
                    dve.wait_ge(s["z_silu"], n + 1)
                    V.tensor_tensor(Y[:, t, :], Y[:, t, :], zt[:, n % 2, :], ALU.mult).then_inc(s["y_z"], 1)
                    dve.wait_ge(s["y_z"], n + 1)
                    link(V.tensor_tensor_reduce(out=tmp[:, t % 2, :], in0=Y[:, t, :], in1=Y[:, t, :], scale=1.0, scalar=0.0,
                                                op0=ALU.mult, op1=ALU.add, accum_out=rms[:, 0, t:t + 1]))
                link(V.tensor_scalar(rms[:, 1, :], rms[:, 0, :], 1.0 / GC, EPS, ALU.mult, ALU.add))
                V.reciprocal(rms[:, 1, :], rms[:, 1, :]).then_inc(s["rms_a"], 1)
                dve.wait_ge(s["rms_b"], g + 1)
                for t in range(NT):
                    V.tensor_scalar(Y[:, t, :], Y[:, t, :], rms[:, 1, t:t + 1], None, ALU.mult).then_inc(s["y_normed"], 1)
                step.sync()
                for i in range(2 * NT):
                    t, h = i // 2, i % 2
                    dve.wait_ge(s["out_mm"], 10 * g + i + 1)
                    if g and i == 0:
                        dve.wait_ge(s["out_added"], 10 * g)
                    f = facc_s[:, t, h * 512:(h + 1) * 512]
                    V.tensor_tensor(f, f, bank[i % 8][:, :], ALU.add).then_inc(s["out_added"], 1)
            dve.wait_ge(s["out_added"], 40)
            for t in range(NT):
                for h in range(2):
                    residual(facc_s[:, t, h * 512:(h + 1) * 512], t, h, h)
            layer_norm(2)
            moe(1)


PAIR_STEPS = 2 + 9 + 1 + 9


def kernel(**inputs):
    import concourse.bacc as bacc
    from concourse.bass_utils import run_bass_kernel_spmd

    a = {k: np.asarray(x) for k, x in inputs.items()}

    def blocks(w):
        k, n = w.shape
        return w.reshape(k // P, P, n // 512, 512).transpose(2, 1, 0, 3).reshape(n // 512, P, -1)

    def feat(x):
        x = x.reshape(x.shape[:-1] + (-1, P))
        return np.moveaxis(x, -1, 0)

    units = np.empty((UNITS, P, UNIT), np.float32)
    units[U_ADA0:U_ADA0 + 12] = blocks(a["ada_w"][0])
    units[U_ADA1:U_ADA1 + 12] = blocks(a["ada_w"][1])
    units[U_PW1:U_PW1 + 4] = blocks(a["conv_pw1_w"][0])[[0, 2, 1, 3]]
    units[U_PW2:U_PW2 + 2] = blocks(a["conv_pw2_w"][0])
    for L, u0 in ((0, U_MOE0), (1, U_MOE1)):
        v = units[u0:u0 + 6 * EXPERTS].reshape(EXPERTS, 6, P, UNIT)
        for e in range(EXPERTS):
            g, u = blocks(a["moe_w_gate"][L, e]), blocks(a["moe_w_up"][L, e])
            v[e, 0], v[e, 2], v[e, 1], v[e, 3] = g[0], g[1], u[0], u[1]
            v[e, 4:6] = blocks(a["moe_w_down"][L, e])
    w_in, w_out = a["ssd_in_w"][0], a["ssd_out_w"][0]
    for g in range(GROUPS):
        u = U_SSD + 4 * g
        B = w_in[:, 4096 + g * P:4096 + (g + 1) * P]
        C = w_in[:, 4608 + g * P:4608 + (g + 1) * P]
        bc = np.concatenate([B, C], 1).reshape(KC, P, 256).transpose(1, 0, 2).reshape(P, -1)
        units[u, :, 0:UNIT // 2] = bc
        units[u, :, UNIT // 2:] = 0
        units[u + 1] = blocks(w_in[:, 2048 + g * GC:2048 + (g + 1) * GC])[0]
        units[u + 2] = blocks(w_in[:, g * GC:(g + 1) * GC])[0]
        units[u + 3] = w_out[g * GC:(g + 1) * GC].reshape(4, P, D).transpose(1, 0, 2).reshape(P, -1)

    x = np.concatenate([a["x_sample"].reshape(NS, P, D), a["x_prompt"].reshape(1, P, D)]).transpose(1, 0, 2)
    cols = {
        "ada_b": feat(a["ada_b"]), "pw1_b": feat(a["conv_pw1_b"][0]),
        "dw_w": feat(a["conv_dw_w"][0]).transpose(0, 2, 1), "dw_b": feat(a["conv_dw_b"][0]),
        "cln_g": feat(a["conv_ln_g"][0]), "cln_b": feat(a["conv_ln_b"][0]),
        "sc_w": feat(a["ssd_conv_w"][0]).transpose(0, 2, 1), "sc_b": feat(a["ssd_conv_b"][0]),
        "norm_w": feat(a["ssd_norm_w"][0]),
        "cond": np.stack([feat(a["c"][0]), feat(a["c_ctx"])], -1),
    }
    params = np.concatenate([cols[n].reshape(P, -1) for n in COLS], 1)
    i, j = np.arange(P)[:, None], np.arange(P)[None, :]
    consts = np.concatenate([i == j, i <= j, i >= j, i > j, i < j, np.ones((P, P)), np.full((P, P), 1.0 / D),
                             np.broadcast_to(np.arange(1, CAP_S + 1), (P, CAP_S))], 1).astype(np.float32)
    router = a["router_w"].reshape(DEPTH, KC, P, EXPERTS).transpose(2, 0, 1, 3)
    w_dt = w_in[:, 5120:5184].reshape(KC, P, 64).transpose(1, 0, 2)
    ln = np.stack([np.stack([a["ln_mix_g"][0], a["ln_mix_b"][0]]), np.stack([a["ln_ffn_g"][0], a["ln_ffn_b"][0]]),
                   np.stack([a["ln_mix_g"][1], a["ln_mix_b"][1]]), np.stack([a["ln_ffn_g"][1], a["ln_ffn_b"][1]])])
    rows = np.concatenate([a["ssd_dt_bias"][0].reshape(1, -1), a["ssd_a_log"][0].reshape(1, -1),
                           a["ssd_d_skip"][0].reshape(1, -1)], 1)
    state = a["state_ssd"][0, 0].transpose(0, 3, 1, 2).reshape(2, P, HEADS * HD)
    feeds = {"w_stream": units, "x_in": x, "params": params, "consts": consts, "router": router, "w_dt": w_dt,
             "ln_rows": ln, "pw2_b": a["conv_pw2_b"][0].reshape(1, -1), "ssd_rows": rows, "state_in": state}
    nc = bacc.Bacc("TRN2", target_bir_lowering=False, num_devices=1)
    arrays, args = {}, []
    for name, arr in feeds.items():
        arr = np.ascontiguousarray(arr)
        arrays[name] = arr
        args.append(nc.dram_tensor(name, arr.shape, mybir.dt.from_np(arr.dtype), kind="ExternalInput").ap())
    args.append(nc.dram_tensor("y_out", (P, NT, D), F32, kind="ExternalOutput").ap())
    args.append(nc.dram_tensor("state_out", (2, P, HEADS * HD), F32, kind="ExternalOutput").ap())
    build(nc, *args)
    r = run_bass_kernel_spmd(nc, [arrays], core_ids=[0])
    y = r.results[0]["y_out"].transpose(1, 0, 2)
    st = r.results[0]["state_out"].reshape(2, P, HEADS, HD).transpose(0, 2, 3, 1)
    return (np.ascontiguousarray(y[NS]).reshape(1, P, D), np.ascontiguousarray(y[:NS]).reshape(1, SAMPLE, D),
            np.ascontiguousarray(st)[None, None])
```

```python
from contextlib import ExitStack

import numpy as np

import concourse.bass as bass
from concourse import mybir

F32 = mybir.dt.float32
F32R = mybir.dt.float32r
ALU = mybir.AluOpType
ACT = mybir.ActivationFunctionType
AX = mybir.AxisListType

P = 128
D = 1024
KC = D // P
NS = 4
NT = 5
TOK = NT * P
SAMPLE = NS * P
DEPTH = 2
ALPHA = (2 * DEPTH) ** 0.25
EPS = 1e-5
TAPS = 31
HALO = TAPS // 2
GRID_W = 64
ROWS = TOK // GRID_W
PITCH = GRID_W + 2 * HALO
EXPERTS = 16
PAIRS = EXPERTS // 2
CAP_S, CAP_P = 64, 16
SLOTS = CAP_S + CAP_P
GROUPS = 4
GC = 512
HEADS = 32
HG = 8
HD = 64
STAPS = 5
R = 3
UNIT = KC * 512
HALF = UNIT // 2
NB = 3
HALVES = 12
POOL_LOW = (8, 9)

U_ADA0 = 0
U_PW1 = 12
U_ADA1 = 16
U_PW2 = 28
U_MOE0 = 30
U_SSD = U_MOE0 + 6 * EXPERTS
U_MOE1 = U_SSD + 4 * GROUPS
UNITS = U_MOE1 + 6 * EXPERTS

COLS = {}
_n = 0
for _name, _k in (("ada_b", 96), ("pw1_b", 16), ("dw_w", KC * TAPS), ("dw_b", KC), ("cln_g", KC), ("cln_b", KC),
                  ("sc_w", 24 * STAPS), ("sc_b", 24), ("norm_w", 16), ("cond", KC * 2)):
    COLS[_name] = (_n, _n + _k)
    _n += _k
NCOLS = _n
C_ID, C_LE, C_GE, C_GT, C_LT, C_ONE, C_MEAN, C_IOTA = (i * P for i in range(8))
NCONST = C_IOTA + CAP_S


def scan_tasks():
    back = [(1, c, 1, int(c > 0)) for c in range(NS - 1, -1, -1)] + [(1, NS, 0, 1)]
    fwd = [(0, c, 1, int(c < NS - 1)) for c in range(NS)] + [(0, NS, 0, 1)]
    out, last, noff, nst = [], [0, 0], 0, 0
    for task in (x for both in zip(back, fwd) for x in both):
        dr, _, off, stt = task
        out.append(task + (noff, nst, last[dr]))
        noff += off
        nst += stt
        if stt:
            last[dr] = nst
    return out


class Steps:

    def __init__(self, eng, sem):
        self.eng, self.sem, self.n, self.off = eng, sem, 0, 0

    def __call__(self, ins):
        ins.then_inc(self.sem, 1)
        self.n += 1

    def sync(self):
        self.eng.wait_ge(self.sem, self.off + self.n)


def build(nc, w_stream, x_in, params, consts, router, w_dt, ln_rows, pw2_b, ssd_rows, state_in, y_out, state_out):
    ctx = ExitStack()
    with ctx:
        def sb(name, shape):
            return ctx.enter_context(nc.sbuf_tensor(name, shape, F32))

        def sem(name):
            return ctx.enter_context(nc.semaphore(name))

        bank = [ctx.enter_context(nc.psum_tensor(f"bank{i}", [P, 512], F32)) for i in range(8)]

        ring = [sb(f"ring{i}", [P, UNIT]) for i in range(R)]
        X = sb("X", [P, NT, D])
        hT = sb("hT", [P, KC, TOK])
        cst = sb("cst", [P, NCONST])
        par = sb("par", [P, NCOLS])
        mT = sb("mT", [P, DEPTH, 48, 2])
        csil = sb("csil", [P, KC, 2])
        gate_bc = sb("gate_bc", [P, 2, D])
        ln_gb = sb("ln_gb", [P, 2, D])
        wr = sb("wr", [P, DEPTH, KC, EXPERTS])
        st = sb("st", [P, NT, 2, 6])
        mv = sb("mv", [P, NT, 2])
        rst = sb("rst", [P, NT])
        tmp = sb("tmp", [P, 2, 512])

        SCR = 23480
        scr_at = (nc.sbuf_base + 31) // 32 * 32
        scr = sb("scr", [P, SCR])
        at = {"conv": 0, "moe": 0, "ssd": 0}

        def take(stage, *shape):
            n = int(np.prod(shape))
            o = at[stage]
            at[stage] = o + n
            assert at[stage] <= SCR, (stage, at[stage])
            v = scr[:, o:o + n]
            if len(shape) == 2:
                return v.rearrange("p (a b) -> p a b", b=shape[1])
            if len(shape) == 3:
                return v.rearrange("p (a b c) -> p a b c", b=shape[1], c=shape[2])
            return v

        def take_r(name, stage, *shape):
            o = (at[stage] + 7) // 8 * 8
            at[stage] = o + int(np.prod(shape))
            assert at[stage] <= SCR, (stage, at[stage])
            return nc.alloc_sbuf_tensor_at(name, [P, *shape], F32R, offset=scr_at + 4 * o)

        upad = take("conv", KC, ROWS, PITCH)
        v = take("conv", KC, TOK)
        sig = take("conv", 2, TOK)
        sq = take("conv", 2, TOK)
        rstd = take("conv", TOK)
        pwb = take("conv", D)
        mrow = take("conv", 2, 512)
        xin = take("moe", 2, KC, SLOTS)
        hid = tmp
        gcol = take("moe", 2)
        psel = take("moe", NS, 2, CAP_S)
        psel_p = take("moe", 2, 2 * CAP_P)
        aff = take("moe", NT, EXPERTS)
        posT = take("moe", NT, EXPERTS)
        ccol = take("moe", 3, NT, 2)
        mark = at["moe"]
        affT = take("moe", TOK)
        work = take("moe", TOK)
        pos = take("moe", TOK)
        lg = take("moe", NT, EXPERTS)
        small = take("moe", 4, NT)
        top8 = take("moe", 8)
        at["moe"] = mark
        out_s = [take_r(f"out_s_{n}", "moe", D) for n in "hl"]
        out_p = [take_r(f"out_p_{n}", "moe", D) for n in "hl"]
        PT = take_r("PT", "moe", SAMPLE)
        PT_p = take_r("PT_p", "moe", P)
        xin_h = take_r("xin_h", "moe", 2, KC, SLOTS)
        xin_l = take_r("xin_l", "moe", 2, KC, SLOTS)
        hidT_h = take_r("hidT_h", "moe", KC, SLOTS)
        hidT_l = take_r("hidT_l", "moe", KC, SLOTS)
        w_h = [take_r(f"w_h{i}", "moe", 4, 512) for i in range(NB)]
        w_l = [take_r(f"w_l{i}", "moe", 4, 512) for i in range(NB)]
        facc_m = hT[:, :, :].rearrange("p a b -> p (a b)").rearrange("p (a b) -> p a b", b=D)
        facc_s = take("ssd", NT, D)
        xs = take("ssd", NT, GC)
        Y = take("ssd", NT, GC)
        Btok = take("ssd", NT, P)
        BT = take("ssd", TOK)
        CT = take("ssd", TOK)
        dt = take("ssd", NT, 64)
        da = take("ssd", NT, 64)
        Ex = take("ssd", NT, 192)
        wst = take("ssd", NT, 64)
        srow = take("ssd", 160)
        prevS = take("ssd", 2, GC)
        rms = take("ssd", 2, NT)
        mark = at["ssd"]
        CBm = take("ssd", 2, NT * P)
        at["ssd"] = mark
        dtmp = take("ssd", 3, NT * 64)
        at["ssd"] = mark + 2 * NT * P
        mark = at["ssd"]
        raw = take("ssd", 2, SAMPLE + P + 8)
        cv = take("ssd", 2, TOK)
        xf = take("ssd", 2, TOK)
        at["ssd"] = mark
        aM = take("ssd", 4, 512)
        Em = take("ssd", 4, 512)
        end = at["ssd"]
        at["ssd"] = mark
        zt14 = take("ssd", 4, GC)
        yT = take("ssd", 4, TOK)
        at["ssd"] = end
        Xd = take("ssd", 4, 256)
        at["ssd"] = end
        wdt = take("ssd", KC, 64)
        at["ssd"] = end + 4 * 256
        xw = take("ssd", 2, GC)
        zt0 = take("ssd", GC)
        zt = [zt0] + [zt14[:, i, :] for i in range(4)]

        ident = cst[:, C_ID:C_ID + P]
        m_le, m_ge = cst[:, C_LE:C_LE + P], cst[:, C_GE:C_GE + P]
        m_gt, m_lt = cst[:, C_GT:C_GT + P], cst[:, C_LT:C_LT + P]
        ones, mean_w = cst[:, C_ONE:C_ONE + P], cst[:, C_MEAN:C_MEAN + P]
        iota = cst[:, C_IOTA:C_IOTA + CAP_S]

        def par_v(name, *shape):
            a, b = COLS[name]
            w = par[:, a:b]
            return w.rearrange("p (a b) -> p a b", b=shape[-1]) if shape else w

        ada_bT = par_v("ada_b")
        pw1_b = par_v("pw1_b")
        dw_w = par_v("dw_w", TAPS)
        dw_b = par_v("dw_b")
        cln_g, cln_b = par_v("cln_g"), par_v("cln_b")
        sc_w, sc_b = par_v("sc_w", STAPS), par_v("sc_b")
        norm_w = par_v("norm_w")
        cond = par_v("cond")

        landed = [sem(f"slot_landed{i}") for i in range(R)]
        names = """x_loaded par_loaded cst_loaded wr_loaded ln_loaded pwb_loaded ssdp_loaded state_loaded
            dve_step act_step adab_ready cond_ready ada_mm mrow_ready ada_tr mT_ready
            hT_tr hTs_ready hTp_ready gate_mm gate_ready upad_zero pw1_done glu_a glu_sig conv_ready mean_mm centered
            sq_ready var_mm var_ready rstd_ready normed v_ready f_mm f_added ln_stat ln_rstd x_ready
            logits_mm lg_ready exp_ready aff_ready aff_tr posm_ready pos_tr psel_ready acol_ready out_split gather_mm xin_ready
            high_ready low_dve low_pool xsplit gated gu_mm silu_ready hid_ready hidT_tr hidT_ready down_mm down_out pt_tr pt_ready comb_mm comb_added
            dtr_mm dt_a dt_b dt_c da_ready cum_mm ex_ready cproj_mm raw_ready cconv_ready xf_ready xtr_mm xs_a xs_v
            z_mm z_silu y_z ss_ready rms_a rms_b y_normed ytr_mm yT_ready out_mm out_added cb_mm cbm_ready y_init
            aM_ready seg_mm exp_m m_ready xd_ready yd_mm yd_added xw_ready off_mm off_added st_mm prev_ready
            st_out y_stored""".split()

        s = {n: sem(n) for n in names}

        block = ctx.enter_context(nc.Block())
        hT_f = hT[:, :, :]

        def gate_part(stage):
            return 16 if stage % 2 == 0 else 40

        def shift_part(stage):
            return 0 if stage % 2 == 0 else 24

        def low_done(L, p, e, h):
            E = 16 * L + 2 * p + e
            if h in POOL_LOW:
                return s["low_pool"], len(POOL_LOW) * E + (POOL_LOW.index(h) + 1)
            mine = [x for x in range(HALVES) if x not in POOL_LOW]
            return s["low_dve"], len(mine) * E + (mine.index(h) + 1)

        @block.sync
        def _(sp):
            sp.dma_start(par[:, :], params).then_inc(s["par_loaded"], 16)
            for j in range(R):
                sp.dma_start(ring[j][:, :], w_stream[j]).then_inc(landed[j], 16)
            sp.dma_start(cst[:, :], consts).then_inc(s["cst_loaded"], 16)
            sp.dma_start(X[:, :, :], x_in).then_inc(s["x_loaded"], 16)

            def used(u):
                if u < U_PW1:
                    return s["ada_mm"], u + 1
                if u < U_ADA1:
                    return s["pw1_done"], 4 * (u - U_PW1 + 1)
                if u < U_PW2:
                    return s["ada_mm"], 12 + u - U_ADA1 + 1
                if u < U_MOE0:
                    return s["f_mm"], NT * (u - U_PW2 + 1)
                if U_SSD <= u < U_MOE1:
                    g, k = (u - U_SSD) // 4, (u - U_SSD) % 4
                    return ((s["cproj_mm"], 6 * g + 2), (s["cproj_mm"], 6 * g + 6), (s["z_mm"], NT * (g + 1)),
                            (s["out_mm"], 2 * NT * (g + 1)))[k]
                raise ValueError(u)

            def free(u, p):
                for L, u0 in ((0, U_MOE0), (1, U_MOE1)):
                    if u0 <= u < u0 + 6 * EXPERTS:
                        e, k = (u - u0) // 6, (u - u0) % 6
                        sp.wait_ge(*low_done(L, p, e, 2 * k + 1))
                        return
                sp.wait_ge(*used(u))

            def load(u, p=0):
                j = u % R
                free(u - R, p)
                w = UNIT // 2 if U_SSD <= u < U_MOE1 and (u - U_SSD) % 4 == 0 else UNIT
                sp.dma_start(ring[j][:, 0:w], w_stream[p * 12 + u, :, 0:w]).then_inc(landed[j], 16)

            for u in range(R, U_MOE0 + 12):
                load(u)
            with sp.Fori(0, PAIRS - 1) as p:
                for k in range(12):
                    load(U_MOE0 + 12 + k, p)
            for u in range(U_SSD, U_MOE1 + 12):
                load(u)
            with sp.Fori(0, PAIRS - 1) as p:
                for k in range(12):
                    load(U_MOE1 + 12 + k, p)
            for t in range(NT):
                sp.wait_ge(s["x_ready"], 15 + t + 1)
                sp.dma_start(y_out[:, t, :], X[:, t, :]).then_inc(s["y_stored"], 16)
            sp.wait_ge(s["y_stored"], 16 * NT)
            sp.wait_ge(s["st_out"], 16 * 2 * GROUPS)

        @block.tensor
        def _(pe):
            def unit_wait(u0, k, p=0):
                j = (u0 + k) % R
                pe.wait_ge(landed[j], 16 * ((u0 + k) // R + 1) + p * (16 * 12 // R))
                return ring[j][:, :].rearrange("p (k n) -> p k n", n=512)

            def ada(L, u0):
                def tr(u):
                    pe.wait_ge(s["mrow_ready"], 12 * L + u + 1)
                    for i in range(4):
                        ins = pe.transpose(bank[6 + u % 2][:, 2 * i:2 * i + 2], mrow[0:2, u % 2, i * P:(i + 1) * P],
                                           ident[0:2, 0:2])
                    ins.then_inc(s["ada_tr"], 1)

                for u in range(12):
                    w = unit_wait(u0, u)
                    if u >= 2:
                        pe.wait_ge(s["mrow_ready"], 12 * L + u - 1)
                    for k in range(KC):
                        ins = pe.matmul(bank[4 + u % 2][0:2, :], csil[:, k, :], w[:, k, :],
                                        start=(k == 0), stop=(k == KC - 1))
                    ins.then_inc(s["ada_mm"], 1)
                    if u:
                        if u >= 3:
                            pe.wait_ge(s["mT_ready"], 4 * (12 * L + u - 2))
                        tr(u - 1)
                pe.wait_ge(s["mT_ready"], 4 * (12 * L + 10))
                tr(11)

            def build_hT(b):
                if b == 0:
                    pe.wait_ge(s["x_loaded"], 16)
                else:
                    pe.wait_ge(s["x_ready"], 5 * b)
                for k in range(KC):
                    if k >= 2:
                        pe.wait_ge(s["hTs_ready"], 8 * b + k - 1)
                        pe.wait_ge(s["hTp_ready"], 8 * b + k - 1)
                    for t in range(NT):
                        out = bank[k % 2][:, t * P:(t + 1) * P] if t < NS else bank[2 + k % 2][:, 0:P]
                        ins = pe.transpose(out, X[:, t, k * P:(k + 1) * P], ident)
                    ins.then_inc(s["hT_tr"], 1)

            def gates(b):
                L, g0 = b // 2, gate_part(b)
                pe.wait_ge(s["mT_ready"], 48 * (L + 1))
                for c in range(2):
                    for h in range(2):
                        for i in range(4):
                            ins = pe.matmul(bank[4 + 2 * c + h][:, i * P:(i + 1) * P],
                                            mT[:, L, g0 + 4 * h + i, c:c + 1].broadcast_to([P, P]), ident,
                                            start=True, stop=True)
                        ins.then_inc(s["gate_mm"], 1)

            def hT_whole(b):
                pe.wait_ge(s["hTs_ready"], 8 * (b + 1))
                pe.wait_ge(s["hTp_ready"], 8 * (b + 1))

            pe.wait_ge(s["cst_loaded"], 16)
            pe.wait_ge(s["cond_ready"], 1)
            ada(0, U_ADA0)
            build_hT(0)
            gates(0)
            hT_whole(0)
            for i in range(16):
                if i % 4 == 0:
                    w = unit_wait(U_PW1, i // 4)
                if i >= 2:
                    pe.wait_ge(s["glu_a"], 1 * (i - 1))
                for k in range(KC):
                    lw = w[:, k, (i % 4) * P:(i % 4 + 1) * P]
                    pe.matmul(bank[i % 2][:, :], lw, hT[:, k, 0:SAMPLE], start=(k == 0), stop=(k == KC - 1))
                    ins = pe.matmul(bank[2 + i % 2][:, 0:P], lw, hT[:, k, SAMPLE:TOK], start=(k == 0), stop=(k == KC - 1))
                ins.then_inc(s["pw1_done"], 1)
            pe.wait_ge(s["gate_ready"], 4)
            ada(1, U_ADA1)
            for k in range(KC):
                pe.wait_ge(s["conv_ready"], k + 1)
                if k == 0:
                    pe.wait_ge(s["glu_a"], 16)
                pe.matmul(bank[0][:, :], mean_w, v[:, k, 0:SAMPLE], start=(k == 0), stop=(k == KC - 1))
                ins = pe.matmul(bank[2][:, 0:P], mean_w, v[:, k, SAMPLE:TOK], start=(k == 0), stop=(k == KC - 1))
            ins.then_inc(s["mean_mm"], 1)
            for k in range(KC):
                pe.wait_ge(s["sq_ready"], k + 1)
                pe.matmul(bank[1][:, :], mean_w, sq[:, k % 2, 0:SAMPLE], start=(k == 0), stop=(k == KC - 1))
                pe.matmul(bank[3][:, 0:P], mean_w, sq[:, k % 2, SAMPLE:TOK], start=(k == 0),
                          stop=(k == KC - 1)).then_inc(s["var_mm"], 1)
            pe.wait_ge(s["v_ready"], 8)
            pe.wait_ge(s["pwb_loaded"], 16)
            pe.wait_ge(s["mT_ready"], 96)
            for nb in range(2):
                w = unit_wait(U_PW2, nb)
                for t in range(NT):
                    i = nb * NT + t
                    if i >= 8:
                        pe.wait_ge(s["f_added"], i - 7)
                    for k in range(KC):
                        pe.matmul(bank[i % 8][:, :], v[:, k, t * P:(t + 1) * P], w[:, k, :], start=(k == 0), stop=False)
                    ins = pe.matmul(bank[i % 8][:, :], ones[0:1, :], pwb[0:1, nb * 512:(nb + 1) * 512],
                                    start=False, stop=True)
                    ins.then_inc(s["f_mm"], 1)

            def gather(Pi):
                pe.wait_ge(s["psel_ready"], Pi + 1)
                for k in range(KC):
                    ins = pe.matmul(bank[5][:, 128 + 32 * k:160 + 32 * k], X[:, NS, k * P:(k + 1) * P],
                                    psel_p[:, :, 0:CAP_P], start=True, stop=True)
                ins.then_inc(s["gather_mm"], 1)
                for half in range(2):
                    for kk in range(4):
                        k = 4 * half + kk
                        for t in range(NS):
                            ins = pe.matmul(bank[6 + half][:, kk * P:(kk + 1) * P], X[:, t, k * P:(k + 1) * P],
                                            psel[:, t, :, :], start=(t == 0), stop=(t == NS - 1))
                    ins.then_inc(s["gather_mm"], 1)

            def combine(Pi):
                pe.wait_ge(s["out_split"], 8 * Pi + 8)
                pe.wait_ge(s["pt_ready"], 3 * Pi + 3)
                for i in range(2 * NT):
                    t, h = i // 2, i % 2
                    if i >= 2:
                        pe.wait_ge(s["comb_added"], 10 * Pi + (i - 1))
                    for n in range(2):
                        if t < NS:
                            ins = pe.matmul(bank[6 + h][:, :], PT[:, t * P:(t + 1) * P],
                                            out_s[n][:, h * 512:(h + 1) * 512], start=(n == 0), stop=(n == 1))
                        else:
                            ins = pe.matmul(bank[6 + h][:, :], PT_p[0:64, :], out_p[n][0:64, h * 512:(h + 1) * 512],
                                            start=(n == 0), stop=(n == 1))
                    ins.then_inc(s["comb_mm"], 1)

            def expert(L, u0, p, e):
                Pi = 8 * L + p
                Ei = 16 * L + 2 * p + e
                if e == 0:
                    pe.wait_ge(s["xsplit"], Pi + 1)
                else:
                    pe.wait_ge(s["pt_ready"], 3 * Pi + 3)
                for i in range(4):
                    if i >= 2 and not (L == 0 and e == 0 and isinstance(p, int) and p == 0):
                        pe.wait_ge(s["out_split"], 4 * Ei + (-2 if i == 2 else 0))
                    if i == 3:
                        turn_hidden(L, p, e, 0)
                    for h in range(2):
                        split_product(L, p, e, 2 * i + h, bank[i], xin_h[:, e, :, :], xin_l[:, e, :, :])\
                            .then_inc(s["gu_mm"], 1)

            def split_product(L, p, e, m, out, ah, al):
                pe.wait_ge(*low_done(L, p, e, m))
                wh, wl = w_h[m % NB], w_l[m % NB]
                for k in range(4):
                    c = 4 * (m % 2) + k
                    pe.matmul(out[0:SLOTS, :], ah[:, c, :], wh[:, k, :], start=(c == 0), stop=False)
                    pe.matmul(out[0:SLOTS, :], ah[:, c, :], wl[:, k, :], start=False, stop=False)
                    ins = pe.matmul(out[0:SLOTS, :], al[:, c, :], wh[:, k, :], start=False, stop=(c == KC - 1))
                return ins

            def turn_hidden(L, p, e, h):
                pe.wait_ge(s["hid_ready"], 2 * (16 * L + 2 * p + e) + (h + 1))
                for i in range(4):
                    ins = pe.transpose(bank[4 + h][:, i * SLOTS:(i + 1) * SLOTS], hid[0:SLOTS, h, i * P:(i + 1) * P],
                                       ident[0:SLOTS, 0:SLOTS])
                ins.then_inc(s["hidT_tr"], 1)

            def expert_down(L, u0, p, e):
                Ei = 16 * L + 2 * p + e
                turn_hidden(L, p, e, 1)
                for h in range(2):
                    for q in range(2):
                        if h == 0:
                            pe.wait_ge(s["hidT_ready"], 2 * Ei + q + 1)
                        split_product(L, p, e, 8 + 2 * h + q, bank[2 + h], hidT_h, hidT_l).then_inc(s["down_mm"], 1)

            def pair(L, u0, p, first, last):
                Pi = 8 * L + p
                expert(L, u0, p, 0)
                pe.wait_ge(s["hid_ready"], 4 * Pi + 1)
                pe.wait_ge(s["acol_ready"], Pi + 1)
                for t in range(NS):
                    ins = pe.transpose(bank[0][:, t * P:(t + 1) * P], psel[:, t, :, :], ident)
                ins.then_inc(s["pt_tr"], 1)
                pe.transpose(bank[1][0:64, 0:P], psel_p[:, :, :], ident)
                for e in range(2):
                    for t in range(NS):
                        pe.matmul(bank[1][0:CAP_S, P + e:P + e + 1], psel[:, t, e, :], ccol[:, 1, t, e:e + 1],
                                  start=(t == 0), stop=(t == NS - 1))
                    ins = pe.matmul(bank[1][CAP_S:SLOTS, P + e:P + e + 1], psel_p[:, e, 0:CAP_P],
                                    ccol[:, 1, NS, e:e + 1], start=True, stop=True)
                ins.then_inc(s["pt_tr"], 1)
                if not first:
                    combine(Pi - 1)
                expert_down(L, u0, p, 0)
                expert(L, u0, p, 1)
                if not last:
                    if not first:
                        pe.wait_ge(s["comb_added"], 10 * Pi)
                    gather(Pi + 1)
                    pe.wait_ge(s["xin_ready"], 16 * Pi + 24)
                expert_down(L, u0, p, 1)

            def moe(L, u0):
                b = 2 * L + 1
                build_hT(b)
                gates(b)
                hT_whole(b)
                pe.wait_ge(s["gate_ready"], 4 * (b + 1))
                pe.wait_ge(s["wr_loaded"], 16)
                for t in range(NT):
                    for k in range(KC):
                        ins = pe.matmul(bank[4][:, t * EXPERTS:(t + 1) * EXPERTS], hT[:, k, t * P:(t + 1) * P],
                                        wr[:, L, k, :], start=(k == 0), stop=(k == KC - 1))
                ins.then_inc(s["logits_mm"], 1)
                pe.wait_ge(s["aff_ready"], L + 1)
                for t in range(NT):
                    out = bank[5][0:EXPERTS, t * P:(t + 1) * P] if t < NS else bank[6][0:EXPERTS, 0:P]
                    ins = pe.transpose(out, aff[:, t, :], ident)
                ins.then_inc(s["aff_tr"], 1)
                pe.wait_ge(s["posm_ready"], L + 1)
                for t in range(NT):
                    ins = pe.transpose(bank[4][:, t * EXPERTS:(t + 1) * EXPERTS], pos[0:EXPERTS, t * P:(t + 1) * P],
                                       ident[0:EXPERTS, 0:EXPERTS])
                ins.then_inc(s["pos_tr"], 1)
                gather(8 * L)
                pair(L, u0, 0, True, False)
                with pe.Fori(1, PAIRS - 1) as p:
                    pair(L, u0, p, False, False)
                pair(L, u0, PAIRS - 1, False, True)
                combine(8 * L + 7)

            moe(0, U_MOE0)

            build_hT(2)
            gates(2)
            hT_whole(2)
            pe.wait_ge(s["gate_ready"], 12)
            pe.wait_ge(s["ssdp_loaded"], 32)
            for t in range(NT):
                for k in range(KC):
                    ins = pe.matmul(bank[7][:, t * 64:(t + 1) * 64], hT[:, k, t * P:(t + 1) * P], wdt[:, k, :],
                                    start=(k == 0), stop=(k == KC - 1))
            ins.then_inc(s["dtr_mm"], 1)

            def ssd_project(g, j, w):
                i = 6 * g + j
                if i >= 2:
                    pe.wait_ge(s["raw_ready"], i - 1)
                c0 = (j if j < 2 else j - 2) * P
                for k in range(KC):
                    pe.matmul(bank[i % 2][:, :], w[:, k, c0:c0 + P], hT[:, k, 0:SAMPLE], start=(k == 0), stop=(k == KC - 1))
                    ins = pe.matmul(bank[2 + i % 2][:, 0:P], w[:, k, c0:c0 + P], hT[:, k, SAMPLE:TOK],
                                    start=(k == 0), stop=(k == KC - 1))
                ins.then_inc(s["cproj_mm"], 1)

            def ssd_turn(g, j):
                i = 6 * g + j
                n = 5 * g + (0 if j == 0 else j - 1)
                pe.wait_ge(s["xf_ready"], i + 1)
                if n >= 2:
                    pe.wait_ge(s["xs_a"], n - 1)
                    pe.wait_ge(s["xs_v"], n - 1)
                src = BT if j == 0 else xf[:, j % 2, :]
                for t in range(NT):
                    out = bank[4 + n % 2][:, t * P:(t + 1) * P] if t < NS else bank[6 + n % 2][:, 0:P]
                    ins = pe.transpose(out, src[:, t * P:(t + 1) * P], ident)
                ins.then_inc(s["xtr_mm"], 1)

            def z_part(g, t, k, w):
                ins = pe.matmul(bank[(0, 6, 7, 0, 1)[t]][:, :], hT[:, k, t * P:(t + 1) * P], w[:, k, :],
                                start=(k == 0), stop=(k == KC - 1))
                if k == KC - 1:
                    ins.then_inc(s["z_mm"], 1)

            for g in range(GROUPS):
                u0 = U_SSD + 4 * g
                if g:
                    pe.wait_ge(s["out_added"], 10 * g)
                j0 = u0 % R
                pe.wait_ge(landed[j0], 16 * (u0 // R + 1))
                w_bc = ring[j0][:, 0:UNIT // 2].rearrange("p (k n) -> p k n", n=256)
                ssd_project(g, 0, w_bc)
                if g == 0:
                    pe.wait_ge(s["dt_a"], 1)
                ssd_project(g, 1, w_bc)
                w_x = unit_wait(u0, 1)
                for j in range(2, 6):
                    ssd_project(g, j, w_x)
                    if j != 3:
                        ssd_turn(g, j - 2)
                w_z = unit_wait(u0, 2)
                pe.wait_ge(s["raw_ready"], 6 * g + 5)
                for k in range(KC):
                    z_part(g, 0, k, w_z)
                ssd_turn(g, 4)
                ssd_turn(g, 5)
                if g == 0:
                    pe.wait_ge(s["da_ready"], 1)
                    pe.wait_ge(s["xs_a"], 5)
                    pe.wait_ge(s["xs_v"], 5)
                    for c in range(NT):
                        bk = bank[(7, 7, 6, 6, 5)[c]]
                        o = 192 * (c % 2)
                        pe.matmul(bk[:, o:o + 32], m_le, da[:, c, 0:32], start=True, stop=True)
                        pe.matmul(bk[:, o + 32:o + 64], m_ge, da[:, c, 32:64], start=True, stop=True)
                        pe.matmul(bk[:, o + 64:o + 96], m_gt, da[:, c, 0:32], start=True, stop=True)
                        pe.matmul(bk[:, o + 96:o + 128], m_lt, da[:, c, 32:64], start=True, stop=True)
                        pe.matmul(bk[:, o + 128:o + 192], ones, da[:, c, :], start=True, stop=True).then_inc(s["cum_mm"], 1)
                pe.wait_ge(s["xs_a"], 5 * g + 5)
                pe.wait_ge(s["xs_v"], 5 * g + 5)
                if g == 0:
                    pe.wait_ge(s["ex_ready"], 5)
                for c in range(NT):
                    out = bank[4][:, c * P:(c + 1) * P] if c < NS else bank[5][:, 0:P]
                    ins = pe.matmul(out, BT[:, c * P:(c + 1) * P], CT[:, c * P:(c + 1) * P], start=True, stop=True)
                ins.then_inc(s["cb_mm"], 1)
                pe.wait_ge(s["raw_ready"], 6 * g + 6)
                pe.wait_ge(s["cbm_ready"], 4 * (g + 1))

                def seg(i):
                    n = 10 * g + i
                    if n >= 2:
                        pe.wait_ge(s["exp_m"], 2 * (n - 1))
                    for dr in range(2):
                        pe.wait_ge(s["aM_ready"], 2 * n + dr + 1)
                        for h in range(4):
                            ins = pe.matmul(bank[2 * dr + n % 2][:, h * P:(h + 1) * P],
                                            aM[:, 2 * (n % 2) + dr, h * P:(h + 1) * P], m_le if dr == 0 else m_ge,
                                            start=True, stop=True)
                        ins.then_inc(s["seg_mm"], 1)

                def ydiag(i):
                    n = 10 * g + i
                    if n >= 2:
                        pe.wait_ge(s["yd_added"], n - 1)
                    pe.wait_ge(s["m_ready"], 2 * n + 2)
                    pe.wait_ge(s["xd_ready"], 2 * n + 2)
                    for h in range(4):
                        for dr in range(2):
                            a = 2 * (n % 2) + dr
                            ins = pe.matmul(bank[4 + n % 2][:, h * HD:(h + 1) * HD], Em[:, a, h * P:(h + 1) * P],
                                            Xd[:, a, h * HD:(h + 1) * HD], start=(dr == 0), stop=(dr == 1))
                    ins.then_inc(s["yd_mm"], 1)

                pe.wait_ge(s["z_silu"], NT * g + 1)
                seg(0)
                for i in range(1, 2 * NT):
                    seg(i)
                    if i <= 2 * KC // 2:
                        for m in (2 * i - 2, 2 * i - 1):
                            z_part(g, 1 + m // KC, m % KC, w_z)
                    ydiag(i - 1)
                ydiag(2 * NT - 1)
                for i, (dr, c, off, stt, noff, nst, prev) in enumerate(scan_tasks()):
                    noff += 8 * g
                    nst += 8 * g
                    if off:
                        if noff % 8 < 2:
                            pe.wait_ge(s["yd_added"], 10 * (g + 1))
                        else:
                            pe.wait_ge(s["off_added"], noff - 1)
                        pe.wait_ge(s["state_loaded"], 32 * (g + 1))
                        if prev:
                            pe.wait_ge(s["prev_ready"], 8 * g + prev)
                        pe.matmul(bank[4 + noff % 2][:, :], CT[:, c * P:(c + 1) * P], prevS[:, dr, :],
                                  start=True, stop=True).then_inc(s["off_mm"], 1)
                    if stt:
                        pe.wait_ge(s["xw_ready"], nst + 1)
                        if nst % 8 < 2:
                            pe.wait_ge(s["z_silu"], NT * g + 2 + nst % 8)
                        else:
                            pe.wait_ge(s["prev_ready"], nst - 1)
                        pe.matmul(bank[6 + nst % 2][:, :], Btok[:, c, :], xw[:, nst % 2, :], start=True, stop=True)\
                          .then_inc(s["st_mm"], 1)
                    if i < KC:
                        if i == 0:
                            pe.wait_ge(s["exp_m"], 20 * (g + 1))
                        z_part(g, 3, i, w_z)
                for k in range(KC):
                    z_part(g, 4, k, w_z)
                j3 = (u0 + 3) % R
                pe.wait_ge(landed[j3], 16 * ((u0 + 3) // R + 1))
                w_o = ring[j3][:, :].rearrange("p (k n) -> p k n", n=D)

                def turn_y(t):
                    n = NT * g + t
                    pe.wait_ge(s["y_normed"], n + 1)
                    if t >= 2:
                        pe.wait_ge(s["yT_ready"], 4 * (n - 1))
                    for i in range(4):
                        ins = pe.transpose(bank[4 + t % 2][:, i * P:(i + 1) * P], Y[:, t, i * P:(i + 1) * P], ident)
                    ins.then_inc(s["ytr_mm"], 1)

                for t in range(NS):
                    turn_y(t)
                pe.wait_ge(s["z_silu"], NT * (g + 1))
                pe.wait_ge(s["prev_ready"], 8 * (g + 1))
                for i in range(2 * NT):
                    t, h = i // 2, i % 2
                    if i == 4:
                        turn_y(NS)
                    pe.wait_ge(s["yT_ready"], 4 * (NT * g + (NT if i >= 4 else t + 1)))
                    if i >= 8:
                        pe.wait_ge(s["out_added"], 10 * g + i - 7)
                    for k in range(4):
                        ins = pe.matmul(bank[i % 8][:, :], yT[:, k, t * P:(t + 1) * P], w_o[:, k, h * 512:(h + 1) * 512],
                                        start=(k == 0), stop=(k == 3))
                    ins.then_inc(s["out_mm"], 1)

            moe(1, U_MOE1)

        @block.scalar
        def _(act):
            step = Steps(act, s["act_step"])
            A = nc.scalar.activation

            def ada(L):
                def bias_cols(u):
                    act.wait_ge(s["ada_tr"], 12 * L + u + 1)
                    if L == 0 and u == 0:
                        act.wait_ge(s["adab_ready"], 4)
                    for i in range(4):
                        c = 4 * u + i
                        A(mT[:, L, c, :], bank[6 + u % 2][:, 2 * i:2 * i + 2], ACT.Identity,
                          bias=ada_bT[:, 48 * L + c:48 * L + c + 1]).then_inc(s["mT_ready"], 1)

                for u in range(12):
                    act.wait_ge(s["ada_mm"], 12 * L + u + 1)
                    if u >= 2:
                        act.wait_ge(s["ada_tr"], 12 * L + u - 1)
                    A(mrow[0:2, u % 2, :], bank[4 + u % 2][0:2, :], ACT.Copy).then_inc(s["mrow_ready"], 1)
                    if u:
                        bias_cols(u - 1)
                bias_cols(11)

            def hT_evac(b):
                L, sh = b // 2, shift_part(b)
                act.wait_ge(s["mT_ready"], 48 * (L + 1))
                for k in range(KC):
                    act.wait_ge(s["hT_tr"], 8 * b + k + 1)
                    A(hT[:, k, 0:SAMPLE], bank[k % 2][:, :], ACT.Identity, bias=mT[:, L, sh + k, 0:1],
                      scale=mT[:, L, sh + 8 + k, 0:1]).then_inc(s["hTs_ready"], 1)

            def gate_evac(b):
                for i in range(4):
                    act.wait_ge(s["gate_mm"], 4 * b + i + 1)
                    A(gate_bc[:, i // 2, (i % 2) * 512:(i % 2 + 1) * 512], bank[4 + i][:, :], ACT.Copy)\
                        .then_inc(s["gate_ready"], 1)

            def ln_sqrt(b):
                act.wait_ge(s["ln_stat"], b + 1)
                A(rst[:, :], rst[:, :], ACT.Sqrt).then_inc(s["ln_rstd"], 1)

            act.wait_ge(s["par_loaded"], 16)
            A(csil[:, :, :].rearrange("p a b -> p (a b)"), cond, ACT.Silu).then_inc(s["cond_ready"], 1)
            ada(0)
            hT_evac(0)
            gate_evac(0)
            act.wait_ge(s["upad_zero"], 1)
            for i in range(16):
                c = (i // 8) * 4 + i % 4
                act.wait_ge(s["pw1_done"], i + 1)
                a, b = bank[i % 2], bank[2 + i % 2]
                if (i // 4) % 2 == 0:
                    bias = pw1_b[:, c:c + 1]
                    step(A(upad[:, c, 0:8, HALO:HALO + GRID_W], a[:, :].rearrange("p (r w) -> p r w", w=GRID_W),
                           ACT.Identity, bias=bias))
                    step(A(upad[:, c, 8, HALO:PITCH], b[:, 0:PITCH - HALO], ACT.Identity, bias=bias))
                    step.sync()
                    A(upad[:, c, 9, 0:PITCH - HALO], b[:, GRID_W - HALO:P], ACT.Identity, bias=bias).then_inc(s["glu_a"], 1)
                else:
                    ng = (i // 8) * 4 + i % 4
                    if ng >= 2:
                        act.wait_ge(s["glu_sig"], ng - 1)
                    bias = pw1_b[:, 8 + c:9 + c]
                    step(A(sig[:, ng % 2, 0:SAMPLE], a[:, :], ACT.Sigmoid, bias=bias))
                    step.sync()
                    A(sig[:, ng % 2, SAMPLE:TOK], b[:, 0:P], ACT.Sigmoid, bias=bias).then_inc(s["glu_a"], 1)
            ada(1)
            for k in range(KC):
                act.wait_ge(s["centered"], k + 1)
                if k >= 2:
                    act.wait_ge(s["var_mm"], k - 1)
                A(sq[:, k % 2, :], v[:, k, :], ACT.Square).then_inc(s["sq_ready"], 1)
            act.wait_ge(s["var_ready"], 2)
            A(rstd, rstd, ACT.Sqrt).then_inc(s["rstd_ready"], 1)
            for k in range(KC):
                act.wait_ge(s["normed"], k + 1)
                A(v[:, k, :], v[:, k, :], ACT.Silu, bias=cln_b[:, k:k + 1], scale=cln_g[:, k:k + 1])\
                    .then_inc(s["v_ready"], 1)
            ln_sqrt(0)

            def xin_evac(L, Pi):
                sh = shift_part(1)
                act.wait_ge(s["gather_mm"], 3 * Pi + 1)
                for k in range(KC):
                    A(xin[:, :, k, CAP_S:SLOTS],
                      bank[5][:, 128 + 32 * k:160 + 32 * k].rearrange("p (e c) -> p e c", c=CAP_P), ACT.Identity,
                      bias=mT[:, L, sh + k, 1:2], scale=mT[:, L, sh + 8 + k, 1:2]).then_inc(s["xin_ready"], 1)
                for k in range(KC):
                    if k % 4 == 0:
                        act.wait_ge(s["gather_mm"], 3 * Pi + (2 + k // 4))
                    A(xin[:, :, k, 0:CAP_S],
                      bank[6 + k // 4][:, (k % 4) * P:(k % 4 + 1) * P].rearrange("p (e c) -> p e c", c=CAP_S),
                      ACT.Identity, bias=mT[:, L, sh + k, 0:1], scale=mT[:, L, sh + 8 + k, 0:1])\
                        .then_inc(s["xin_ready"], 1)

            def high(L, u0, p, e, m):
                Ei = 16 * L + 2 * p + e
                u = 6 * e + m // 2
                j = (u0 + u) % R
                act.wait_ge(landed[j], 16 * ((u0 + u) // R + 1) + p * (16 * 12 // R))
                if not (L == 0 and e == 0 and isinstance(p, int) and p == 0 and m < NB):
                    if m < NB:
                        act.wait_ge(s["down_mm"], 4 * Ei + (m - 2))
                    elif m < NB + 8:
                        act.wait_ge(s["gu_mm"], 8 * Ei + (m - NB + 1))
                    else:
                        act.wait_ge(s["down_mm"], 4 * Ei + (m - NB - 7))
                src = ring[j][:, (m % 2) * HALF:(m % 2 + 1) * HALF].rearrange("p (k n) -> p k n", n=512)
                A(w_h[m % NB][:, :, :], src, ACT.Copy).then_inc(s["high_ready"], 1)

            def silu(L, p, e, h):
                Ei = 16 * L + 2 * p + e
                act.wait_ge(s["gu_mm"], 8 * Ei + (4 * h + 2))
                if not (L == 0 and e == 0 and isinstance(p, int) and p == 0):
                    act.wait_ge(s["hidT_tr"], 2 * Ei + (h - 1))
                A(hid[0:SLOTS, h, :], bank[2 * h][0:SLOTS, :], ACT.Silu).then_inc(s["silu_ready"], 1)

            def down_evac(L, p, e, h):
                Ei = 16 * L + 2 * p + e
                act.wait_ge(s["down_mm"], 4 * Ei + (2 * h + 2))
                c = slice(h * 512, (h + 1) * 512)
                bk = bank[2 + h]
                A(bk[0:SLOTS, :], bk[0:SLOTS, :], ACT.Copy, scale=gcol[0:SLOTS, e:e + 1]).then_inc(s["gated"], 1)
                act.wait_ge(s["gated"], 2 * Ei + (h + 1))
                A(out_s[0][64 * e:64 * e + CAP_S, c], bk[0:CAP_S, :], ACT.Copy).then_inc(s["down_out"], 1)
                A(out_p[0][32 * e:32 * e + CAP_P, c], bk[CAP_S:SLOTS, :], ACT.Copy).then_inc(s["down_out"], 1)

            def pair(L, u0, p, last):
                Pi = 8 * L + p
                for e in range(2):
                    def nxt(m):
                        if e == 0:
                            high(L, u0, p, 1, m)
                        elif not last:
                            high(L, u0, p + 1, 0, m)

                    high(L, u0, p, e, 3)
                    high(L, u0, p, e, 4)
                    silu(L, p, e, 0)
                    for m in range(5, 9):
                        high(L, u0, p, e, m)
                    silu(L, p, e, 1)
                    high(L, u0, p, e, 9)
                    high(L, u0, p, e, 10)
                    if e == 0:
                        act.wait_ge(s["pt_tr"], 2 * Pi + 2)
                        if not (L == 0 and isinstance(p, int) and p == 0):
                            act.wait_ge(s["comb_mm"], 10 * Pi)
                            act.wait_ge(s["out_split"], 8 * Pi)
                        A(gcol[0:SLOTS, :], bank[1][0:SLOTS, P:P + 2], ACT.Copy).then_inc(s["pt_ready"], 1)
                        A(PT[:, :], bank[0][:, :], ACT.Copy).then_inc(s["pt_ready"], 1)
                        A(PT_p[0:64, :], bank[1][0:64, 0:P], ACT.Copy).then_inc(s["pt_ready"], 1)
                        act.wait_ge(s["pt_ready"], 3 * Pi + 1)
                    elif not last:
                        xin_evac(L, Pi + 1)
                    high(L, u0, p, e, 11)
                    nxt(0)
                    down_evac(L, p, e, 0)
                    nxt(1)
                    nxt(2)
                    down_evac(L, p, e, 1)

            def moe(L, u0):
                b = 2 * L + 1
                hT_evac(b)
                gate_evac(b)
                act.wait_ge(s["lg_ready"], L + 1)
                A(lg, lg, ACT.Exp).then_inc(s["exp_ready"], 1)
                for m in range(NB):
                    high(L, u0, 0, 0, m)
                xin_evac(L, 8 * L)
                pair(L, u0, 0, False)
                with act.Fori(1, PAIRS - 1) as p:
                    pair(L, u0, p, False)
                pair(L, u0, PAIRS - 1, True)
                ln_sqrt(b)

            moe(0, U_MOE0)

            hT_evac(2)
            gate_evac(2)
            act.wait_ge(s["ssdp_loaded"], 32)
            A(srow[:, 64:128], srow[:, 64:128], ACT.Exp).then_inc(s["dt_b"], 1)
            act.wait_ge(s["dt_a"], 2)
            A(dtmp[:, 1, :], dtmp[:, 1, :], ACT.Exp).then_inc(s["dt_b"], 1)
            act.wait_ge(s["dt_a"], 3)
            A(dtmp[:, 2, :], dtmp[:, 2, :], ACT.Ln).then_inc(s["dt_b"], 1)

            def ssd_raw(g, j):
                i = 6 * g + j
                act.wait_ge(s["cproj_mm"], i + 1)
                if i >= 2:
                    act.wait_ge(s["cconv_ready"], i - 1)
                step(A(raw[:, i % 2, 2:2 + SAMPLE], bank[i % 2][:, :], ACT.Copy))
                step.sync()
                A(raw[:, i % 2, SAMPLE + 6:SAMPLE + 6 + P], bank[2 + i % 2][:, 0:P], ACT.Copy).then_inc(s["raw_ready"], 1)

            def ssd_silu(g, j):
                i = 6 * g + j
                act.wait_ge(s["cconv_ready"], i + 1)
                if j >= 4:
                    act.wait_ge(s["xtr_mm"], 5 * g + j - 2)
                dst = (BT, CT)[j] if j < 2 else xf[:, j % 2, :]
                A(dst, cv[:, i % 2, :], ACT.Silu).then_inc(s["xf_ready"], 1)

            def ssd_xs(g, j):
                n = 5 * g + (0 if j == 0 else j - 1)
                act.wait_ge(s["xtr_mm"], n + 1)
                src = bank[4 + n % 2][:, :].rearrange("p (t c) -> p t c", c=P)
                dst = Btok[:, 0:NS, :] if j == 0 else xs[:, 0:NS, (j - 2) * P:(j - 1) * P]
                A(dst, src, ACT.Copy).then_inc(s["xs_a"], 1)

            def z_silu(g, t):
                act.wait_ge(s["z_mm"], NT * g + t + 1)
                A(zt[t], bank[(0, 6, 7, 0, 1)[t]][:, :], ACT.Silu).then_inc(s["z_silu"], 1)

            def rms_sqrt(g, ts, n):
                act.wait_ge(s["rms_a"], 2 * g + n)
                A(rms[:, 1, ts], rms[:, 1, ts], ACT.Sqrt).then_inc(s["rms_b"], 1)

            def yT_evac(g, t):
                act.wait_ge(s["ytr_mm"], NT * g + t + 1)
                for i in range(4):
                    A(yT[:, i, t * P:(t + 1) * P], bank[4 + t % 2][:, i * P:(i + 1) * P], ACT.Copy,
                      scale=norm_w[:, 4 * g + i:4 * g + i + 1]).then_inc(s["yT_ready"], 1)

            for g in range(GROUPS):
                act.wait_ge(s["upad_zero"], g + 2)
                ssd_raw(g, 0)
                for j in range(6):
                    if j < 5:
                        ssd_raw(g, j + 1)
                    ssd_silu(g, j)
                    if j == 2:
                        ssd_xs(g, 0)
                    if j >= 4:
                        ssd_xs(g, j - 2)
                z_silu(g, 0)
                ssd_xs(g, 4)
                ssd_xs(g, 5)
                if g == 0:
                    for c in range(NT):
                        act.wait_ge(s["cum_mm"], NT)
                        o = 192 * (c % 2)
                        A(Ex[:, c, :], bank[(7, 7, 6, 6, 5)[c]][:, o:o + 192], ACT.Exp).then_inc(s["ex_ready"], 1)
                for i in range(2 * NT):
                    n = 10 * g + i
                    if n >= 2:
                        act.wait_ge(s["yd_mm"], n - 1)
                    for dr in range(2):
                        act.wait_ge(s["seg_mm"], 2 * n + dr + 1)
                        A(Em[:, 2 * (n % 2) + dr, :], bank[2 * dr + n % 2][:, :], ACT.Exp).then_inc(s["exp_m"], 1)
                for t in range(1, NS):
                    z_silu(g, t)
                rms_sqrt(g, slice(0, NS), 1)
                z_silu(g, NS)
                for t in range(NS):
                    yT_evac(g, t)
                rms_sqrt(g, slice(NS, NT), 2)
                yT_evac(g, NS)
            ln_sqrt(2)
            moe(1, U_MOE1)

        @block.gpsimd
        def _(pool):
            def moe_low(L, u0):
                with pool.Fori(0, EXPERTS) as E:
                    for m in POOL_LOW:
                        j = (u0 + m // 2) % R
                        pool.wait_ge(s["high_ready"], HALVES * (16 * L + E) + (m + 1))
                        src = ring[j][:, (m % 2) * HALF:(m % 2 + 1) * HALF].rearrange("p (k n) -> p k n", n=512)
                        nc.gpsimd.tensor_tensor(w_l[m % NB][:, :, :], src, w_h[m % NB][:, :, :].bitcast(F32),
                                                ALU.subtract).then_inc(s["low_pool"], 1)

            pool.dma_start(wr[:, :, :, :], router).then_inc(s["wr_loaded"], 16)
            pool.dma_start(pwb[0:1, :], pw2_b).then_inc(s["pwb_loaded"], 16)
            pool.dma_start(ln_gb[:, :, :], ln_rows[0:1].partition_broadcast(P)).then_inc(s["ln_loaded"], 16)
            nc.gpsimd.memset(upad.rearrange("p a b c -> p (a b c)"), 0.0).then_inc(s["upad_zero"], 1)
            for b in range(1, 4):
                pool.wait_ge(s["x_ready"], 5 * b)
                pool.wait_ge(s["ln_loaded"], 16 * b)
                pool.dma_start(ln_gb[:, :, :], ln_rows[b:b + 1].partition_broadcast(P)).then_inc(s["ln_loaded"], 16)
                if b != 2:
                    moe_low(b // 2, U_MOE0 if b == 1 else U_MOE1)
                    continue
                pool.dma_start(srow, ssd_rows.partition_broadcast(P)).then_inc(s["ssdp_loaded"], 16)
                pool.dma_start(wdt, w_dt).then_inc(s["ssdp_loaded"], 16)
                for g in range(GROUPS):
                    if g:
                        pool.wait_ge(s["y_z"], NT * g)
                    nc.gpsimd.memset(raw, 0.0).then_inc(s["upad_zero"], 1)
                    for dr in range(2):
                        if g:
                            pool.wait_ge(s["off_mm"], 8 * g)
                            pool.wait_ge(s["st_out"], 32 * g)
                        pool.dma_start(prevS[:, dr, :], state_in[dr, :, g * GC:(g + 1) * GC]).then_inc(s["state_loaded"], 16)
                    pool.wait_ge(s["xs_a"], 5 * g + 5)
                    pool.wait_ge(s["xs_v"], 5 * g + 5)

                    def y_init():
                        skip = srow[:, 128 + HG * g:128 + HG * (g + 1)]
                        for t in range(NT):
                            nc.gpsimd.tensor_tensor(
                                Y[:, t, :].rearrange("p (h d) -> p h d", d=HD),
                                xs[:, t, :].rearrange("p (h d) -> p h d", d=HD),
                                skip.rearrange("p (h d) -> p h d", d=1).broadcast_to([P, HG, HD]),
                                ALU.mult).then_inc(s["y_init"], 1)
                    if g == 0:
                        pool.wait_ge(s["da_ready"], 1)
                    for i in range(2 * NT):
                        n = 10 * g + i
                        c, q = i // 2, i % 2
                        if i == 2:
                            y_init()
                        if n >= 2:
                            pool.wait_ge(s["seg_mm"], 2 * (n - 1))
                        for dr in range(2):
                            h0 = 32 * dr + HG * g + 4 * q
                            nc.gpsimd.tensor_tensor(
                                aM[:, 2 * (n % 2) + dr, :].rearrange("p (h k) -> p h k", k=P),
                                (m_gt if dr == 0 else m_lt).rearrange("p (h k) -> p h k", h=1).broadcast_to([P, 4, P]),
                                da[:, c, h0:h0 + 4].rearrange("p (h k) -> p h k", k=1).broadcast_to([P, 4, P]),
                                ALU.mult).then_inc(s["aM_ready"], 1)
                    for k, (dr, c) in enumerate([x[:2] for x in scan_tasks() if x[3]]):
                        n = 8 * g + k
                        if n >= 2:
                            pool.wait_ge(s["st_mm"], n - 1)
                        if n == 0:
                            pool.wait_ge(s["dt_c"], 1)
                        h0 = 32 * dr + HG * g
                        nc.gpsimd.tensor_tensor(
                            xw[:, n % 2, :].rearrange("p (h d) -> p h d", d=HD), xs[:, c, :].rearrange("p (h d) -> p h d", d=HD),
                            wst[:, c, h0:h0 + HG].rearrange("p (h d) -> p h d", d=1).broadcast_to([P, HG, HD]),
                            ALU.mult).then_inc(s["xw_ready"], 1)
                        if c == NS:
                            pool.wait_ge(s["prev_ready"], n + 1)
                            pool.dma_start(state_out[dr, :, g * GC:(g + 1) * GC], prevS[:, dr, :]).then_inc(s["st_out"], 16)

        @block.vector
        def _(dve):
            V = nc.vector
            step = Steps(dve, s["dve_step"])

            def link(ins):
                step(ins)
                step.sync()

            def hT_evac(b):
                L, sh = b // 2, shift_part(b)
                dve.wait_ge(s["mT_ready"], 48 * (L + 1))
                for k in range(KC):
                    dve.wait_ge(s["hT_tr"], 8 * b + k + 1)
                    V.tensor_scalar(hT[:, k, SAMPLE:TOK], bank[2 + k % 2][:, 0:P], mT[:, L, sh + 8 + k, 1:2],
                                    mT[:, L, sh + k, 1:2], ALU.mult, ALU.add).then_inc(s["hTp_ready"], 1)

            def residual(f, t, h, buf, out_sem=None):
                c = slice(h * 512, (h + 1) * 512)
                link(V.tensor_tensor(tmp[:, buf, :], f, gate_bc[:, int(t == NS), c], ALU.mult))
                ins = V.scalar_tensor_tensor(X[:, t, c], X[:, t, c], ALPHA, tmp[:, buf, :], ALU.mult, ALU.add)
                if out_sem is not None:
                    ins.then_inc(out_sem, 1)
                else:
                    step(ins)

            def layer_norm(b):
                step.sync()
                if b == 0:
                    dve.wait_ge(s["f_added"], 10)
                for t in range(NT):
                    for h in range(2):
                        step(V.bn_stats(st[:, t, h, :], X[:, t, h * 512:(h + 1) * 512]))
                step.sync()
                for t in range(NT):
                    step(V.bn_aggr(mv[:, t, :], st[:, t, :, :]))
                step.sync()
                link(V.tensor_scalar(rst[:, :], mv[:, :, 1], EPS, None, ALU.add))
                V.reciprocal(rst[:, :], rst[:, :]).then_inc(s["ln_stat"], 1)
                dve.wait_ge(s["ln_rstd"], b + 1)
                dve.wait_ge(s["ln_loaded"], 16 * (b + 1))
                for t in range(NT):
                    link(V.tensor_scalar(X[:, t, :], X[:, t, :], mv[:, t, 0:1], rst[:, t:t + 1], ALU.subtract, ALU.mult))
                    link(V.tensor_tensor(X[:, t, :], X[:, t, :], ln_gb[:, 0, :], ALU.mult))
                    V.tensor_tensor(X[:, t, :], X[:, t, :], ln_gb[:, 1, :], ALU.add).then_inc(s["x_ready"], 1)

            dve.wait_ge(s["par_loaded"], 16)
            for L in range(DEPTH):
                for c in (8, 32):
                    V.tensor_scalar(ada_bT[:, 48 * L + c:48 * L + c + 8], ada_bT[:, 48 * L + c:48 * L + c + 8],
                                    1.0, None, ALU.add).then_inc(s["adab_ready"], 1)
            hT_evac(0)
            for c in range(KC):
                i = (c // 4) * 8 + 4 + c % 4
                dve.wait_ge(s["glu_a"], i + 1)
                step(V.tensor_tensor(upad[:, c, 0:8, HALO:HALO + GRID_W], upad[:, c, 0:8, HALO:HALO + GRID_W],
                                     sig[:, c % 2, 0:SAMPLE].rearrange("p (r w) -> p r w", w=GRID_W), ALU.mult))
                step(V.tensor_tensor(upad[:, c, 8, HALO:PITCH], upad[:, c, 8, HALO:PITCH],
                                     sig[:, c % 2, SAMPLE:SAMPLE + PITCH - HALO], ALU.mult))
                step.sync()
                V.tensor_tensor(upad[:, c, 9, 0:PITCH - HALO], upad[:, c, 9, 0:PITCH - HALO],
                                sig[:, c % 2, SAMPLE + GRID_W - HALO:TOK], ALU.mult).then_inc(s["glu_sig"], 1)
                dve.wait_ge(s["glu_sig"], c + 1)
                vr = v[:, c, :].rearrange("p (r w) -> p r w", w=GRID_W)
                link(V.tensor_scalar(vr, upad[:, c, :, 0:GRID_W], dw_w[:, c, 0:1], dw_b[:, c:c + 1], ALU.mult, ALU.add))
                for k in range(1, TAPS):
                    ins = V.scalar_tensor_tensor(vr, upad[:, c, :, k:k + GRID_W], dw_w[:, c, k:k + 1], vr, ALU.mult, ALU.add)
                    if k < TAPS - 1:
                        link(ins)
                    else:
                        ins.then_inc(s["conv_ready"], 1)
            dve.wait_ge(s["conv_ready"], 8)
            dve.wait_ge(s["mean_mm"], 1)
            for k in range(KC):
                step(V.tensor_tensor(v[:, k, 0:SAMPLE], v[:, k, 0:SAMPLE], bank[0][:, :], ALU.subtract))
                step.sync()
                V.tensor_tensor(v[:, k, SAMPLE:TOK], v[:, k, SAMPLE:TOK], bank[2][:, 0:P], ALU.subtract).then_inc(s["centered"], 1)
            dve.wait_ge(s["var_mm"], 8)
            step(V.tensor_scalar(rstd[:, 0:SAMPLE], bank[1][:, :], EPS, None, ALU.add))
            link(V.tensor_scalar(rstd[:, SAMPLE:TOK], bank[3][:, 0:P], EPS, None, ALU.add))
            V.reciprocal(rstd[:, 0:SAMPLE], rstd[:, 0:SAMPLE]).then_inc(s["var_ready"], 1)
            V.reciprocal(rstd[:, SAMPLE:TOK], rstd[:, SAMPLE:TOK]).then_inc(s["var_ready"], 1)
            dve.wait_ge(s["rstd_ready"], 1)
            dve.wait_ge(s["centered"], 8)
            for k in range(KC):
                V.tensor_tensor(v[:, k, :], v[:, k, :], rstd, ALU.mult).then_inc(s["normed"], 1)
            dve.wait_ge(s["gate_ready"], 4)
            for i in range(2 * NT):
                dve.wait_ge(s["f_mm"], i + 1)
                if i >= 2:
                    dve.wait_ge(s["f_added"], i - 1)
                residual(bank[i % 8][:, :], i % NT, i // NT, i % 2, s["f_added"])
            layer_norm(0)

            def acol(L, p):
                Pi = 8 * L + p
                if not (isinstance(Pi, int) and Pi == 0):
                    dve.wait_ge(s["pt_tr"], 2 * Pi)
                V.tensor_copy(ccol[:, 1, :, :], aff[:, :, bass.ds(2 * p, 2)]).then_inc(s["acol_ready"], 1)

            def build_psel(L, p):
                Pi = 8 * L + p
                link(V.tensor_copy(ccol[:, 2, :, :], posT[:, :, bass.ds(2 * p, 2)]))
                if not (isinstance(Pi, int) and Pi == 0):
                    dve.wait_ge(s["gather_mm"], 3 * Pi)
                    dve.wait_ge(s["pt_tr"], 2 * Pi)
                for e in range(2):
                    for t in range(NS):
                        step(V.tensor_scalar(psel[:, t, e, :], iota, ccol[:, 2, t, e:e + 1], None, ALU.is_equal))
                step(V.tensor_scalar(psel_p[:, 0, :], iota[:, 0:2 * CAP_P], ccol[:, 2, NS, 0:1], None, ALU.is_equal))
                step.sync()
                V.tensor_scalar(psel_p[:, 1, :], iota[:, 0:2 * CAP_P], ccol[:, 2, NS, 1:2], None, ALU.is_equal)\
                 .then_inc(s["psel_ready"], 1)

            def hids(L, p, e, hs):
                Ei = 16 * L + 2 * p + e
                for h in hs:
                    dve.wait_ge(s["silu_ready"], 2 * Ei + (h + 1))
                    dve.wait_ge(s["gu_mm"], 8 * Ei + (4 * h + 4))
                    V.tensor_tensor(hid[0:SLOTS, h, :], hid[0:SLOTS, h, :], bank[2 * h + 1][0:SLOTS, :], ALU.mult)\
                     .then_inc(s["hid_ready"], 1)

            def hidT_evac(L, p, e, hs):
                Ei = 16 * L + 2 * p + e
                for h in hs:
                    dve.wait_ge(s["hidT_tr"], 2 * Ei + (h + 1))
                    src = bank[4 + h][:, 0:4 * SLOTS].rearrange("p (k c) -> p k c", c=SLOTS)
                    hi = hidT_h[:, 4 * h:4 * h + 4, :]
                    link(V.tensor_copy(hi, src))
                    V.tensor_tensor(hidT_l[:, 4 * h:4 * h + 4, :], src, hi.bitcast(F32), ALU.subtract)\
                     .then_inc(s["hidT_ready"], 1)

            def low(L, u0, p, e, m):
                j = (u0 + 6 * e + m // 2) % R
                dve.wait_ge(s["high_ready"], HALVES * (16 * L + 2 * p + e) + (m + 1))
                src = ring[j][:, (m % 2) * HALF:(m % 2 + 1) * HALF].rearrange("p (k n) -> p k n", n=512)
                V.tensor_tensor(w_l[m % NB][:, :, :], src, w_h[m % NB][:, :, :].bitcast(F32), ALU.subtract)\
                 .then_inc(s["low_dve"], 1)

            def out_low(L, p, e, h):
                En = 16 * L + 2 * p + e
                dve.wait_ge(s["down_out"], 4 * En + (2 * h - 2))
                c = slice(h * 512, (h + 1) * 512)
                bk = bank[2 + h]
                a = 1 - e
                V.tensor_tensor(out_s[1][64 * a:64 * a + CAP_S, c], bk[0:CAP_S, :],
                                out_s[0][64 * a:64 * a + CAP_S, c].bitcast(F32), ALU.subtract).then_inc(s["out_split"], 1)
                V.tensor_tensor(out_p[1][32 * a:32 * a + CAP_P, c], bk[CAP_S:SLOTS, :],
                                out_p[0][32 * a:32 * a + CAP_P, c].bitcast(F32), ALU.subtract).then_inc(s["out_split"], 1)

            def xin_split(Pi):
                dve.wait_ge(s["xin_ready"], 16 * Pi + 16)
                link(V.tensor_copy(xin_h[:, :, :, :], xin))
                V.tensor_tensor(xin_l[:, :, :, :], xin, xin_h[:, :, :, :].bitcast(F32), ALU.subtract)\
                 .then_inc(s["xsplit"], 1)

            def comb_add(Pi):
                dve.wait_ge(s["comb_added"], 10 * Pi) if not (isinstance(Pi, int) and Pi == 0) else None
                for i in range(2 * NT):
                    t, h = i // 2, i % 2
                    dve.wait_ge(s["comb_mm"], 10 * Pi + (i + 1))
                    f = facc_m[:, t, h * 512:(h + 1) * 512]
                    V.tensor_tensor(f, f, bank[6 + h][:, :], ALU.add).then_inc(s["comb_added"], 1)

            def pair(L, u0, p, first, last):
                for e in range(2):
                    low(L, u0, p, e, 3)
                    if e == 1 or not first:
                        out_low(L, p, e, 1)
                    if e == 0:
                        acol(L, p)
                    low(L, u0, p, e, 4)
                    low(L, u0, p, e, 5)
                    hids(L, p, e, (0,))
                    low(L, u0, p, e, 6)
                    low(L, u0, p, e, 7)
                    hidT_evac(L, p, e, (0,))
                    if e == 1 and not last:
                        build_psel(L, p + 1)
                    hids(L, p, e, (1,))
                    low(L, u0, p, e, 10)
                    if e == 0 and not first:
                        comb_add(8 * L + p - 1)
                    hidT_evac(L, p, e, (1,))
                    low(L, u0, p, e, 11)
                    if e == 1 and not last:
                        xin_split(8 * L + p + 1)
                    for m in range(3):
                        if e == 0:
                            low(L, u0, p, 1, m)
                        elif not last:
                            low(L, u0, p + 1, 0, m)
                        if m == 0:
                            if e == 0:
                                out_low(L, p, 1, 0)
                            else:
                                out_low(L, p + 1, 0, 0)
                if last:
                    out_low(L, p + 1, 0, 1)

            def moe(L, u0):
                b = 2 * L + 1
                hT_evac(b)
                f = facc_m.rearrange("p a b -> p (a b)")
                if L == 1:
                    dve.wait_ge(s["st_out"], 32 * GROUPS)
                dve.wait_ge(s["logits_mm"], L + 1)
                link(V.memset(f, 0.0))
                hT_zero = f[:, 0:D]
                lgp = bank[4][:, 0:NT * EXPERTS].rearrange("p (t e) -> p t e", e=EXPERTS)

                def bc(x):
                    return x.rearrange("p (t e) -> p t e", e=1).broadcast_to([P, NT, EXPERTS])

                link(V.tensor_reduce(small[:, 0, :], lgp, AX.X, ALU.max))
                V.tensor_tensor(lg, lgp, bc(small[:, 0, :]), ALU.subtract).then_inc(s["lg_ready"], 1)
                dve.wait_ge(s["exp_ready"], L + 1)
                link(V.tensor_reduce(small[:, 1, :], lg, AX.X, ALU.add))
                link(V.reciprocal(small[:, 2, :], small[:, 1, :]))
                V.tensor_tensor(aff, lg, bc(small[:, 2, :]), ALU.mult).then_inc(s["aff_ready"], 1)
                dve.wait_ge(s["aff_ready"], L + 1)
                dve.wait_ge(s["aff_tr"], L + 1)
                E = EXPERTS
                step(V.tensor_copy(work[0:E, 0:SAMPLE], bank[5][0:E, :]))
                link(V.tensor_copy(work[0:E, SAMPLE:TOK], bank[6][0:E, 0:P]))
                for lo, hi, cap in ((0, SAMPLE, CAP_S), (SAMPLE, TOK, CAP_P)):
                    for _ in range(cap // 8):
                        link(V.max(top8[0:E, :], work[0:E, lo:hi]))
                        link(V.match_replace(work[0:E, lo:hi], top8[0:E, :], work[0:E, lo:hi], -1.0))
                link(V.tensor_scalar(work[0:E, :], work[0:E, :], 0.0, None, ALU.is_lt))
                step(V.memset(affT[0:E, :], 1.0))
                step.sync()
                for lo, hi in ((0, SAMPLE), (SAMPLE, TOK)):
                    step(V.tensor_tensor_scan(pos[0:E, lo:hi], affT[0:E, lo:hi], work[0:E, lo:hi], 0.0, ALU.mult, ALU.add))
                step.sync()
                V.tensor_tensor(pos[0:E, :], pos[0:E, :], work[0:E, :], ALU.mult).then_inc(s["posm_ready"], 1)
                dve.wait_ge(s["pos_tr"], L + 1)
                link(V.tensor_copy(posT, bank[4][:, 0:NT * EXPERTS].rearrange("p (t e) -> p t e", e=EXPERTS)))
                build_psel(L, 0)
                for n in range(2):
                    step(V.tensor_copy(out_p[n][:, :], hT_zero))
                step.sync()
                for m in range(NB):
                    low(L, u0, 0, 0, m)
                xin_split(8 * L)
                pair(L, u0, 0, True, False)
                n0 = step.n
                per = PAIR_STEPS
                with dve.Fori(1, PAIRS - 1) as p:
                    step.off = (p - 1) * per
                    pair(L, u0, p, False, False)
                assert step.n - n0 == per, step.n - n0
                step.off = 0
                step.n = n0 + per * (PAIRS - 2)
                pair(L, u0, PAIRS - 1, False, True)
                comb_add(8 * L + 7)
                dve.wait_ge(s["comb_added"], 80 * (L + 1))
                dve.wait_ge(s["gate_ready"], 4 * (b + 1))
                for t in range(NT):
                    for h in range(2):
                        residual(facc_m[:, t, h * 512:(h + 1) * 512], t, h, h)
                layer_norm(b)

            moe(0, U_MOE0)

            hT_evac(2)
            step(V.memset(facc_s.rearrange("p a b -> p (a b)"), 0.0))
            dve.wait_ge(s["ssdp_loaded"], 32)
            dve.wait_ge(s["dtr_mm"], 1)
            w2 = [dtmp[:, i, :].rearrange("p (t h) -> p t h", h=64) for i in range(3)]
            rowb = srow[:, 0:64].rearrange("p (t h) -> p t h", t=1).broadcast_to([P, NT, 64])
            arow = srow[:, 64:128].rearrange("p (t h) -> p t h", t=1).broadcast_to([P, NT, 64])
            V.tensor_tensor(dt, bank[7][:, 0:NT * 64].rearrange("p (t h) -> p t h", h=64), rowb, ALU.add).then_inc(s["dt_a"], 1)
            dve.wait_ge(s["dt_a"], 1)
            link(V.tensor_scalar(w2[0], dt, -1.0, None, ALU.mult))
            V.tensor_tensor(w2[1], dt, w2[0], ALU.min).then_inc(s["dt_a"], 1)
            dve.wait_ge(s["dt_a"], 2)
            dve.wait_ge(s["dt_b"], 2)
            link(V.tensor_scalar(w2[0], w2[1], 1.0, None, ALU.add))
            V.tensor_copy(w2[2], w2[0]).then_inc(s["dt_a"], 1)
            link(V.tensor_scalar(w2[0], w2[0], -1.0, None, ALU.add))
            step(V.tensor_scalar(wst, w2[0], 0.0, None, ALU.is_equal))
            dve.wait_ge(s["dt_a"], 3)
            dve.wait_ge(s["dt_b"], 3)
            step.sync()
            link(V.tensor_scalar(w2[0], w2[0], 1e-30, None, ALU.max))
            link(V.reciprocal(w2[0], w2[0]))
            step(V.tensor_tensor(w2[0], w2[0], w2[2], ALU.mult))
            step.sync()
            link(V.tensor_tensor(w2[0], w2[0], wst, ALU.add))
            link(V.tensor_tensor(w2[0], w2[0], w2[1], ALU.mult))
            link(V.scalar_tensor_tensor(dt, dt, 0.0, w2[0], ALU.max, ALU.add))
            V.scalar_tensor_tensor(da, dt, -1.0, arow, ALU.mult, ALU.mult).then_inc(s["da_ready"], 1)

            def conv(g, j):
                i = 6 * g + j
                dve.wait_ge(s["raw_ready"], i + 1)
                if i >= 2:
                    dve.wait_ge(s["xf_ready"], i - 1)
                ch = (16 + g) if j == 0 else (20 + g) if j == 1 else 4 * g + j - 2
                a, b = cv[:, i % 2, 0:SAMPLE], cv[:, i % 2, SAMPLE:TOK]
                ra, rb = raw[:, i % 2, 0:SAMPLE + 4], raw[:, i % 2, SAMPLE + 4:]
                step(V.tensor_scalar(a, ra[:, 0:SAMPLE], sc_w[:, ch, 0:1], sc_b[:, ch:ch + 1], ALU.mult, ALU.add))
                step(V.tensor_scalar(b, rb[:, 0:P], sc_w[:, ch, 0:1], sc_b[:, ch:ch + 1], ALU.mult, ALU.add))
                for k in range(1, STAPS):
                    step.sync()
                    step(V.scalar_tensor_tensor(a, ra[:, k:k + SAMPLE], sc_w[:, ch, k:k + 1], a, ALU.mult, ALU.add))
                    ins = V.scalar_tensor_tensor(b, rb[:, k:k + P], sc_w[:, ch, k:k + 1], b, ALU.mult, ALU.add)
                    if k < STAPS - 1:
                        step(ins)
                    else:
                        step.sync()
                        ins.then_inc(s["cconv_ready"], 1)

            def xs_evac(g, j):
                n = 5 * g + (0 if j == 0 else j - 1)
                dve.wait_ge(s["xtr_mm"], n + 1)
                dst = Btok[:, NS, :] if j == 0 else xs[:, NS, (j - 2) * P:(j - 1) * P]
                V.tensor_copy(dst, bank[6 + n % 2][:, 0:P]).then_inc(s["xs_v"], 1)

            for g in range(GROUPS):
                if g:
                    dve.wait_ge(s["out_mm"], 10 * g)
                for j in range(6):
                    conv(g, j)
                    if j == 3:
                        xs_evac(g, 0)
                    if j >= 4:
                        xs_evac(g, j - 2)
                xs_evac(g, 4)
                xs_evac(g, 5)
                if g == 0:
                    dve.wait_ge(s["ex_ready"], 5)
                    V.tensor_tensor(wst, dt, Ex[:, :, 64:128], ALU.mult).then_inc(s["dt_c"], 1)
                dve.wait_ge(s["cb_mm"], g + 1)
                for dr in range(2):
                    m = m_le if dr == 0 else m_ge
                    V.tensor_tensor(CBm[:, dr, 0:SAMPLE].rearrange("p (t k) -> p t k", k=P),
                                    bank[4][:, :].rearrange("p (t k) -> p t k", k=P),
                                    m.rearrange("p (t k) -> p t k", t=1).broadcast_to([P, NS, P]), ALU.mult)\
                     .then_inc(s["cbm_ready"], 1)
                    V.tensor_tensor(CBm[:, dr, SAMPLE:TOK], bank[5][:, 0:P], m, ALU.mult).then_inc(s["cbm_ready"], 1)
                dve.wait_ge(s["cbm_ready"], 4 * (g + 1))
                for i in range(2 * NT + 1):
                    if i < 2 * NT:
                        n = 10 * g + i
                        c, q = i // 2, i % 2
                        for dr in range(2):
                            a = 2 * (n % 2) + dr
                            h0 = 32 * dr + HG * g + 4 * q
                            if n >= 2:
                                dve.wait_ge(s["yd_mm"], n - 1)
                            V.tensor_tensor(Xd[:, a, :].rearrange("p (h d) -> p h d", d=HD),
                                            xs[:, c, 256 * q:256 * (q + 1)].rearrange("p (h d) -> p h d", d=HD),
                                            dt[:, c, h0:h0 + 4].rearrange("p (h d) -> p h d", d=1).broadcast_to([P, 4, HD]),
                                            ALU.mult).then_inc(s["xd_ready"], 1)
                            dve.wait_ge(s["exp_m"], 2 * n + dr + 1)
                            V.tensor_tensor(Em[:, a, :].rearrange("p (h k) -> p h k", k=P),
                                            Em[:, a, :].rearrange("p (h k) -> p h k", k=P),
                                            CBm[:, dr, c * P:(c + 1) * P].rearrange("p (h k) -> p h k", h=1)
                                            .broadcast_to([P, 4, P]), ALU.mult).then_inc(s["m_ready"], 1)
                    if i:
                        n = 10 * g + i - 1
                        c, q = (i - 1) // 2, (i - 1) % 2
                        dve.wait_ge(s["yd_mm"], n + 1)
                        dve.wait_ge(s["y_init"], NT * (g + 1))
                        y = Y[:, c, 256 * q:256 * (q + 1)]
                        V.tensor_tensor(y, y, bank[4 + n % 2][:, 0:256], ALU.add).then_inc(s["yd_added"], 1)
                dve.wait_ge(s["yd_added"], 10 * (g + 1))
                dve.wait_ge(s["state_loaded"], 32 * (g + 1))
                for dr, c, off, stt, noff, nst, prev in scan_tasks():
                    noff += 8 * g
                    nst += 8 * g
                    h0 = 32 * dr + HG * g

                    def bc(x):
                        return x.rearrange("p (h d) -> p h d", d=1).broadcast_to([P, HG, HD])

                    if prev:
                        dve.wait_ge(s["prev_ready"], 8 * g + prev)
                    if off:
                        dve.wait_ge(s["off_mm"], noff + 1)
                        if noff:
                            dve.wait_ge(s["off_added"], noff)
                        tm = tmp[:, noff % 2, :]
                        link(V.tensor_tensor(tm.rearrange("p (h d) -> p h d", d=HD),
                                             bank[4 + noff % 2][:, :].rearrange("p (h d) -> p h d", d=HD),
                                             bc(Ex[:, c, h0:h0 + HG]), ALU.mult))
                        V.tensor_tensor(Y[:, c, :], Y[:, c, :], tm, ALU.add).then_inc(s["off_added"], 1)
                    if stt:
                        pv = prevS[:, dr, :]
                        own = bank[6 + nst % 2][:, :]
                        dve.wait_ge(s["st_mm"], nst + 1)
                        if off:
                            link(V.tensor_tensor(pv.rearrange("p (h d) -> p h d", d=HD), pv.rearrange("p (h d) -> p h d", d=HD),
                                                 bc(Ex[:, c, 128 + h0:128 + h0 + HG]), ALU.mult))
                            V.tensor_tensor(pv, pv, own, ALU.add).then_inc(s["prev_ready"], 1)
                        else:
                            V.tensor_copy(pv, own).then_inc(s["prev_ready"], 1)
                dve.wait_ge(s["off_added"], 8 * (g + 1))

                def norm_y(t0, t1, n):
                    for t in range(t0, t1):
                        dve.wait_ge(s["z_silu"], NT * g + t + 1)
                        V.tensor_tensor(Y[:, t, :], Y[:, t, :], zt[t], ALU.mult).then_inc(s["y_z"], 1)
                    for t in range(t0, t1):
                        dve.wait_ge(s["y_z"], NT * g + t + 1)
                        link(V.tensor_tensor_reduce(out=tmp[:, t % 2, :], in0=Y[:, t, :], in1=Y[:, t, :], scale=1.0,
                                                    scalar=0.0, op0=ALU.mult, op1=ALU.add, accum_out=rms[:, 0, t:t + 1]))
                    link(V.tensor_scalar(rms[:, 1, t0:t1], rms[:, 0, t0:t1], 1.0 / GC, EPS, ALU.mult, ALU.add))
                    V.reciprocal(rms[:, 1, t0:t1], rms[:, 1, t0:t1]).then_inc(s["rms_a"], 1)
                    dve.wait_ge(s["rms_b"], 2 * g + n)
                    for t in range(t0, t1):
                        V.tensor_scalar(Y[:, t, :], Y[:, t, :], rms[:, 1, t:t + 1], None, ALU.mult)\
                         .then_inc(s["y_normed"], 1)

                norm_y(0, NS, 1)
                norm_y(NS, NT, 2)
                step.sync()
                for i in range(2 * NT):
                    t, h = i // 2, i % 2
                    dve.wait_ge(s["out_mm"], 10 * g + i + 1)
                    if g and i == 0:
                        dve.wait_ge(s["out_added"], 10 * g)
                    f = facc_s[:, t, h * 512:(h + 1) * 512]
                    V.tensor_tensor(f, f, bank[i % 8][:, :], ALU.add).then_inc(s["out_added"], 1)
            dve.wait_ge(s["out_added"], 40)
            for t in range(NT):
                for h in range(2):
                    residual(facc_s[:, t, h * 512:(h + 1) * 512], t, h, h)
            layer_norm(2)
            moe(1, U_MOE1)


PAIR_STEPS = 1 + 9 + 4 + 1


def kernel(**inputs):
    import concourse.bacc as bacc
    from concourse.bass_utils import run_bass_kernel_spmd

    a = {k: np.asarray(x) for k, x in inputs.items()}

    def blocks(w):
        k, n = w.shape
        return w.reshape(k // P, P, n // 512, 512).transpose(2, 1, 0, 3).reshape(n // 512, P, -1)

    def feat(x):
        x = x.reshape(x.shape[:-1] + (-1, P))
        return np.moveaxis(x, -1, 0)

    units = np.empty((UNITS, P, UNIT), np.float32)
    units[U_ADA0:U_ADA0 + 12] = blocks(a["ada_w"][0])
    units[U_ADA1:U_ADA1 + 12] = blocks(a["ada_w"][1])
    units[U_PW1:U_PW1 + 4] = blocks(a["conv_pw1_w"][0])[[0, 2, 1, 3]]
    units[U_PW2:U_PW2 + 2] = blocks(a["conv_pw2_w"][0])
    for L, u0 in ((0, U_MOE0), (1, U_MOE1)):
        v = units[u0:u0 + 6 * EXPERTS].reshape(EXPERTS, 6, P, UNIT)
        for e in range(EXPERTS):
            g, u = blocks(a["moe_w_gate"][L, e]), blocks(a["moe_w_up"][L, e])
            v[e, 0], v[e, 2], v[e, 1], v[e, 3] = g[0], g[1], u[0], u[1]
            v[e, 4:6] = blocks(a["moe_w_down"][L, e])
    w_in, w_out = a["ssd_in_w"][0], a["ssd_out_w"][0]
    for g in range(GROUPS):
        u = U_SSD + 4 * g
        B = w_in[:, 4096 + g * P:4096 + (g + 1) * P]
        C = w_in[:, 4608 + g * P:4608 + (g + 1) * P]
        bc = np.concatenate([B, C], 1).reshape(KC, P, 256).transpose(1, 0, 2).reshape(P, -1)
        units[u, :, 0:UNIT // 2] = bc
        units[u, :, UNIT // 2:] = 0
        units[u + 1] = blocks(w_in[:, 2048 + g * GC:2048 + (g + 1) * GC])[0]
        units[u + 2] = blocks(w_in[:, g * GC:(g + 1) * GC])[0]
        units[u + 3] = w_out[g * GC:(g + 1) * GC].reshape(4, P, D).transpose(1, 0, 2).reshape(P, -1)

    x = np.concatenate([a["x_sample"].reshape(NS, P, D), a["x_prompt"].reshape(1, P, D)]).transpose(1, 0, 2)
    cols = {
        "ada_b": feat(a["ada_b"]), "pw1_b": feat(a["conv_pw1_b"][0]),
        "dw_w": feat(a["conv_dw_w"][0]).transpose(0, 2, 1), "dw_b": feat(a["conv_dw_b"][0]),
        "cln_g": feat(a["conv_ln_g"][0]), "cln_b": feat(a["conv_ln_b"][0]),
        "sc_w": feat(a["ssd_conv_w"][0]).transpose(0, 2, 1), "sc_b": feat(a["ssd_conv_b"][0]),
        "norm_w": feat(a["ssd_norm_w"][0]),
        "cond": np.stack([feat(a["c"][0]), feat(a["c_ctx"])], -1),
    }
    params = np.concatenate([cols[n].reshape(P, -1) for n in COLS], 1)
    i, j = np.arange(P)[:, None], np.arange(P)[None, :]
    consts = np.concatenate([i == j, i <= j, i >= j, i > j, i < j, np.ones((P, P)), np.full((P, P), 1.0 / D),
                             np.broadcast_to(np.arange(1, CAP_S + 1), (P, CAP_S))], 1).astype(np.float32)
    router = a["router_w"].reshape(DEPTH, KC, P, EXPERTS).transpose(2, 0, 1, 3)
    w_dt = w_in[:, 5120:5184].reshape(KC, P, 64).transpose(1, 0, 2)
    ln = np.stack([np.stack([a["ln_mix_g"][0], a["ln_mix_b"][0]]), np.stack([a["ln_ffn_g"][0], a["ln_ffn_b"][0]]),
                   np.stack([a["ln_mix_g"][1], a["ln_mix_b"][1]]), np.stack([a["ln_ffn_g"][1], a["ln_ffn_b"][1]])])
    rows = np.concatenate([a["ssd_dt_bias"][0].reshape(1, -1), a["ssd_a_log"][0].reshape(1, -1),
                           a["ssd_d_skip"][0].reshape(1, -1)], 1)
    state = a["state_ssd"][0, 0].transpose(0, 3, 1, 2).reshape(2, P, HEADS * HD)
    feeds = {"w_stream": units, "x_in": x, "params": params, "consts": consts, "router": router, "w_dt": w_dt,
             "ln_rows": ln, "pw2_b": a["conv_pw2_b"][0].reshape(1, -1), "ssd_rows": rows, "state_in": state}
    nc = bacc.Bacc("TRN2", target_bir_lowering=False, num_devices=1)
    arrays, args = {}, []
    for name, arr in feeds.items():
        arr = np.ascontiguousarray(arr)
        arrays[name] = arr
        args.append(nc.dram_tensor(name, arr.shape, mybir.dt.from_np(arr.dtype), kind="ExternalInput").ap())
    args.append(nc.dram_tensor("y_out", (P, NT, D), F32, kind="ExternalOutput").ap())
    args.append(nc.dram_tensor("state_out", (2, P, HEADS * HD), F32, kind="ExternalOutput").ap())
    build(nc, *args)
    r = run_bass_kernel_spmd(nc, [arrays], core_ids=[0])
    y = r.results[0]["y_out"].transpose(1, 0, 2)
    st = r.results[0]["state_out"].reshape(2, P, HEADS, HD).transpose(0, 2, 3, 1)
    return (np.ascontiguousarray(y[NS]).reshape(1, P, D), np.ascontiguousarray(y[:NS]).reshape(1, SAMPLE, D),
            np.ascontiguousarray(st)[None, None])
```

```python
from contextlib import ExitStack

import numpy as np

import concourse.bass as bass
from concourse import mybir

F32 = mybir.dt.float32
F32R = mybir.dt.float32r
ALU = mybir.AluOpType
ACT = mybir.ActivationFunctionType
AX = mybir.AxisListType

P = 128
D = 1024
KC = D // P
NS = 4
NT = 5
TOK = NT * P
SAMPLE = NS * P
DEPTH = 2
ALPHA = (2 * DEPTH) ** 0.25
EPS = 1e-5
TAPS = 31
HALO = TAPS // 2
GRID_W = 64
ROWS = TOK // GRID_W
PITCH = GRID_W + 2 * HALO
EXPERTS = 16
PAIRS = EXPERTS // 2
CAP_S, CAP_P = 64, 16
SLOTS = CAP_S + CAP_P
GROUPS = 4
GC = 512
HEADS = 32
HG = 8
HD = 64
STAPS = 5
R = 3
UNIT = KC * 512
HALF = UNIT // 2
NB = 3
HALVES = 12
COMB_BANKS = (6, 7, 4)
POOL_LOW = (8, 9)

CONV_DVE = ((0,), (1, 2), (4, 5), (6, 7))
CONV_ORDER = [c for cs in CONV_DVE for c in cs]
CONV_POOL = (3,)

U_ADA0 = 0
U_PW1 = 12
U_ADA1 = 16
U_PW2 = 28
U_MOE0 = 30
U_SSD = U_MOE0 + 6 * EXPERTS
U_MOE1 = U_SSD + 4 * GROUPS
UNITS = U_MOE1 + 6 * EXPERTS

COLS = {}
_n = 0
for _name, _k in (("ada_b", 96), ("pw1_b", 16), ("dw_w", KC * TAPS), ("dw_b", KC), ("cln_g", KC), ("cln_b", KC),
                  ("sc_w", 24 * STAPS), ("sc_b", 24), ("norm_w", 16), ("cond", KC * 2)):
    COLS[_name] = (_n, _n + _k)
    _n += _k
NCOLS = _n
C_ID, C_LE, C_GE, C_GT, C_LT, C_ONE, C_MEAN, C_IOTA = (i * P for i in range(8))
NCONST = C_IOTA + CAP_S


def scan_tasks():
    back = [(1, c, 1, int(c > 0)) for c in range(NS - 1, -1, -1)] + [(1, NS, 0, 1)]
    fwd = [(0, c, 1, int(c < NS - 1)) for c in range(NS)] + [(0, NS, 0, 1)]
    out, last, noff, nst = [], [0, 0], 0, 0
    for task in (x for both in zip(back, fwd) for x in both):
        dr, _, off, stt = task
        out.append(task + (noff, nst, last[dr]))
        noff += off
        nst += stt
        if stt:
            last[dr] = nst
    return out


class Steps:

    def __init__(self, eng, sem):
        self.eng, self.sem, self.n, self.off = eng, sem, 0, 0

    def __call__(self, ins):
        ins.then_inc(self.sem, 1)
        self.n += 1

    def sync(self, but=0):
        self.eng.wait_ge(self.sem, self.off + self.n - but)


def build(nc, w_stream, x_in, params, consts, router, w_dt, ln_rows, pw2_b, ssd_rows, state_in, y_out, state_out):
    ctx = ExitStack()
    with ctx:
        def sb(name, shape):
            return ctx.enter_context(nc.sbuf_tensor(name, shape, F32))

        def sem(name):
            return ctx.enter_context(nc.semaphore(name))

        bank = [ctx.enter_context(nc.psum_tensor(f"bank{i}", [P, 512], F32)) for i in range(8)]

        ring, ring_low = [], []
        for i in range(R):
            slot_at = (nc.sbuf_base + 31) // 32 * 32
            ring.append(sb(f"ring{i}", [P, UNIT]))
            ring_low.append(nc.alloc_sbuf_tensor_at(f"ring_low{i}", [P, UNIT], F32R, offset=slot_at))
        X = sb("X", [P, NT, D])
        hT = sb("hT", [P, KC, TOK])
        cst = sb("cst", [P, NCONST])
        par = sb("par", [P, NCOLS])
        mT = sb("mT", [P, DEPTH, 48, 2])
        csil = sb("csil", [P, KC, 2])
        gate_bc = sb("gate_bc", [P, 2, D])
        ln_gb = sb("ln_gb", [P, 2, D])
        wr = sb("wr", [P, DEPTH, KC, EXPERTS])
        st = sb("st", [P, NT, 2, 6])
        mv = sb("mv", [P, NT, 2])
        rst = sb("rst", [P, NT])
        nmean = sb("nmean", [P, 2, NT])
        tmp = sb("tmp", [P, 2, 512])

        SCR = 23472
        scr_at = (nc.sbuf_base + 31) // 32 * 32
        scr = sb("scr", [P, SCR])
        at = {"conv": 0, "moe": 0, "ssd": 0}

        def take(stage, *shape):
            n = int(np.prod(shape))
            o = at[stage]
            at[stage] = o + n
            assert at[stage] <= SCR, (stage, at[stage])
            v = scr[:, o:o + n]
            if len(shape) == 2:
                return v.rearrange("p (a b) -> p a b", b=shape[1])
            if len(shape) == 3:
                return v.rearrange("p (a b c) -> p a b c", b=shape[1], c=shape[2])
            return v

        def take_r(name, stage, *shape):
            o = (at[stage] + 7) // 8 * 8
            at[stage] = o + int(np.prod(shape))
            assert at[stage] <= SCR, (stage, at[stage])
            return nc.alloc_sbuf_tensor_at(name, [P, *shape], F32R, offset=scr_at + 4 * o)

        upad = take("conv", KC, ROWS, PITCH)
        v = take("conv", KC, TOK)
        sig = take("conv", KC, TOK)
        pconv = take("conv", 2, TOK)
        sq = take("conv", 2, TOK)
        rstd = take("conv", TOK)
        pwb = take("conv", D)
        mrow = take("conv", 2, 512)
        xin = take("moe", 2, KC, SLOTS)
        hid = tmp
        gcol = take("moe", 2)
        psel = take("moe", NS, 2, CAP_S)
        psel_p = take("moe", 2, 2 * CAP_P)
        aff = take("moe", NT, EXPERTS)
        posT = take("moe", NT, EXPERTS)
        ccol = take("moe", 3, NT, 2)
        mark = at["moe"]
        affT = take("moe", TOK)
        work = take("moe", TOK)
        pos = take("moe", TOK)
        lg = take("moe", NT, EXPERTS)
        small = take("moe", 4, NT)
        top8 = take("moe", 8)
        at["moe"] = mark
        out_s = [take_r(f"out_s_{n}", "moe", D) for n in "hl"]
        out_p = [take_r(f"out_p_{n}", "moe", D) for n in "hl"]
        PT = take_r("PT", "moe", SAMPLE)
        PT_p = take_r("PT_p", "moe", P)
        xin_h = take_r("xin_h", "moe", 2, KC, SLOTS)
        xin_l = take_r("xin_l", "moe", 2, KC, SLOTS)
        hidT_h = take_r("hidT_h", "moe", KC, SLOTS)
        hidT_l = take_r("hidT_l", "moe", KC, SLOTS)
        w_h = [take_r(f"w_h{i}", "moe", 4, 512) for i in range(NB)]
        w_l = [take_r(f"w_l{i}", "moe", 4, 512) for i in range(NB)]
        facc_m = hT[:, :, :].rearrange("p a b -> p (a b)").rearrange("p (a b) -> p a b", b=D)
        facc_s = take("ssd", NT, D)
        XS_AT = at["ssd"]
        xs = take("ssd", NT, GC)
        Y = take("ssd", NT, GC)
        Btok = take("ssd", NT, P)
        BT = take("ssd", TOK)
        CT = take("ssd", TOK)
        dt = take("ssd", NT, 64)
        da = take("ssd", NT, 64)
        Ex = take("ssd", NT, 192)
        wst = take("ssd", NT, 64)
        srow = take("ssd", 160)
        prevS = take("ssd", 2, GC)
        rms = take("ssd", 2, NT)
        mark = at["ssd"]
        CB_AT = (mark + 7) // 8 * 8
        CBm = take("ssd", 2, NT * P)
        at["ssd"] = mark
        dtmp = take("ssd", 3, NT * 64)
        at["ssd"] = mark + 2 * NT * P
        mark = at["ssd"] = (at["ssd"] + 7) // 8 * 8
        raw = take("ssd", 2, SAMPLE + P + 8)
        cv = take("ssd", 2, TOK)
        xf = take("ssd", 2, TOK)
        at["ssd"] = mark
        aM = take("ssd", 4, 512)
        Em = take("ssd", 4, 512)
        end = at["ssd"]
        at["ssd"] = mark
        zt14 = take("ssd", 4, GC)
        yT_h = take_r("yT_h", "ssd", 4, TOK)
        yT_l4 = take_r("yT_l4", "ssd", 4, P)
        at["ssd"] = mark
        yT_l = take_r("yT_l", "ssd", NS, 4, P)
        at["ssd"] = end
        Xd = take("ssd", 4, 256)
        at["ssd"] = end
        wdt = take("ssd", KC, 64)
        at["ssd"] = end + 4 * 256
        after_xw = at["ssd"]
        xw = take("ssd", 2, GC)
        wo_h = []
        for at["ssd"] in (CB_AT, XS_AT, XS_AT + D, after_xw):
            wo_h.append(take_r(f"wo_h{len(wo_h)}", "ssd", D))
        at["ssd"] = after_xw + 2 * GC
        zt0 = take("ssd", GC)
        zt = [zt0] + [zt14[:, i, :] for i in range(4)]

        ident = cst[:, C_ID:C_ID + P]
        m_le, m_ge = cst[:, C_LE:C_LE + P], cst[:, C_GE:C_GE + P]
        m_gt, m_lt = cst[:, C_GT:C_GT + P], cst[:, C_LT:C_LT + P]
        ones, mean_w = cst[:, C_ONE:C_ONE + P], cst[:, C_MEAN:C_MEAN + P]
        iota = cst[:, C_IOTA:C_IOTA + CAP_S]

        def par_v(name, *shape):
            a, b = COLS[name]
            w = par[:, a:b]
            return w.rearrange("p (a b) -> p a b", b=shape[-1]) if shape else w

        ada_bT = par_v("ada_b")
        pw1_b = par_v("pw1_b")
        dw_w = par_v("dw_w", TAPS)
        dw_b = par_v("dw_b")
        cln_g, cln_b = par_v("cln_g"), par_v("cln_b")
        sc_w, sc_b = par_v("sc_w", STAPS), par_v("sc_b")
        norm_w = par_v("norm_w")
        cond = par_v("cond")

        landed = [sem(f"slot_landed{i}") for i in range(R)]
        names = """wo_high wo_low yT_low lgT_ready logits_tr pool_step glu_sig_pool conv_pool x_loaded par_loaded cst_loaded wr_loaded ln_loaded pwb_loaded ssdp_loaded state_loaded
            dve_step act_step adab_ready cond_ready ada_mm mrow_ready ada_tr mT_ready
            hT_tr hTs_ready hTp_ready gate_mm gate_ready upad_zero pw1_done glu_a glu_sig conv_ready mean_mm centered
            sq_ready var_mm var_ready rstd_ready normed v_ready f_mm f_added ln_stat ln_normed ln_scaled x_ready
            logits_mm lg_ready exp_ready aff_ready aff_tr posm_ready pos_tr psel_ready acol_ready out_split gather_mm xin_ready
            high_ready low_dve low_pool xsplit gated gu_mm silu_ready hid_ready hidT_tr hidT_ready down_mm down_out pt_tr pt_ready comb_mm comb_added
            dtr_mm dt_a dt_b dt_c da_ready cum_mm ex_ready cproj_mm raw_ready cconv_ready xf_ready xtr_mm xs_a xs_v
            z_mm z_silu y_z rms_a rms_b y_normed ytr_mm yT_ready out_mm out_added cb_mm cbm_ready y_init
            aM_ready seg_mm exp_m m_ready xd_ready yd_mm yd_added xw_ready off_mm off_added st_mm prev_ready
            st_out y_stored""".split()

        s = {n: sem(n) for n in names}

        block = ctx.enter_context(nc.Block())

        def gate_part(stage):
            return 16 if stage % 2 == 0 else 40

        def shift_part(stage):
            return 0 if stage % 2 == 0 else 24

        def low_done(L, p, e, h):
            E = 16 * L + 2 * p + e
            if h in POOL_LOW:
                return s["low_pool"], len(POOL_LOW) * E + (POOL_LOW.index(h) + 1)
            mine = [x for x in range(HALVES) if x not in POOL_LOW]
            return s["low_dve"], len(mine) * E + (mine.index(h) + 1)

        def glu(c, eng, step, gated, n_gated):
            i = (c // 4) * 8 + 4 + c % 4
            step.eng.wait_ge(s["glu_a"], i + 1)
            step(eng.tensor_tensor(upad[:, c, 0:8, HALO:HALO + GRID_W], upad[:, c, 0:8, HALO:HALO + GRID_W],
                                   sig[:, c, 0:SAMPLE].rearrange("p (r w) -> p r w", w=GRID_W), ALU.mult))
            step(eng.tensor_tensor(upad[:, c, 8, HALO:PITCH], upad[:, c, 8, HALO:PITCH],
                                   sig[:, c, SAMPLE:SAMPLE + PITCH - HALO], ALU.mult))
            step.sync()
            eng.tensor_tensor(upad[:, c, 9, 0:PITCH - HALO], upad[:, c, 9, 0:PITCH - HALO],
                              sig[:, c, SAMPLE + GRID_W - HALO:TOK], ALU.mult).then_inc(gated, 1)
            step.eng.wait_ge(gated, n_gated)

        def taps(c):
            return v[:, c, :].rearrange("p (r w) -> p r w", w=GRID_W), lambda k: upad[:, c, :, k:k + GRID_W]

        @block.sync
        def _(sp):
            sp.dma_start(par[:, :], params).then_inc(s["par_loaded"], 16)
            for j in range(R):
                sp.dma_start(ring[j][:, :], w_stream[j]).then_inc(landed[j], 16)
                if j == 0:
                    sp.dma_start(cst[:, :], consts).then_inc(s["cst_loaded"], 16)
            sp.dma_start(X[:, :, :], x_in).then_inc(s["x_loaded"], 16)

            def used(u):
                if u < U_PW1:
                    return s["ada_mm"], u + 1
                if u < U_ADA1:
                    return s["pw1_done"], 4 * (u - U_PW1 + 1)
                if u < U_PW2:
                    return s["ada_mm"], 12 + u - U_ADA1 + 1
                if u < U_MOE0:
                    return s["f_mm"], NT * (u - U_PW2 + 1)
                if U_SSD <= u < U_MOE1:
                    g, k = (u - U_SSD) // 4, (u - U_SSD) % 4
                    return ((s["cproj_mm"], 6 * g + 2), (s["cproj_mm"], 6 * g + 6), (s["z_mm"], NT * (g + 1)),
                            (s["out_mm"], 2 * NT * (g + 1)))[k]
                raise ValueError(u)

            def free(u, p):
                for L, u0 in ((0, U_MOE0), (1, U_MOE1)):
                    if u0 <= u < u0 + 6 * EXPERTS:
                        e, k = (u - u0) // 6, (u - u0) % 6
                        sp.wait_ge(*low_done(L, p, e, 2 * k + 1))
                        return
                sp.wait_ge(*used(u))

            def load(u, p=0):
                j = u % R
                free(u - R, p)
                w = UNIT // 2 if U_SSD <= u < U_MOE1 and (u - U_SSD) % 4 == 0 else UNIT
                sp.dma_start(ring[j][:, 0:w], w_stream[p * 12 + u, :, 0:w]).then_inc(landed[j], 16)

            for u in range(R, U_MOE0 + 12):
                load(u)
            with sp.Fori(0, PAIRS - 1) as p:
                for k in range(12):
                    load(U_MOE0 + 12 + k, p)
            for u in range(U_SSD, U_MOE1 + 12):
                load(u)
            with sp.Fori(0, PAIRS - 1) as p:
                for k in range(12):
                    load(U_MOE1 + 12 + k, p)
            for t in range(NT):
                sp.wait_ge(s["x_ready"], 15 + t + 1)
                sp.dma_start(y_out[:, t, :], X[:, t, :]).then_inc(s["y_stored"], 16)
            sp.wait_ge(s["y_stored"], 16 * NT)
            sp.wait_ge(s["st_out"], 16 * 2 * GROUPS)

        @block.tensor
        def _(pe):
            def unit_wait(u0, k, p=0):
                j = (u0 + k) % R
                pe.wait_ge(landed[j], 16 * ((u0 + k) // R + 1) + p * (16 * 12 // R))
                return ring[j][:, :].rearrange("p (k n) -> p k n", n=512)

            def ada(L, u0):
                def tr(u):
                    pe.wait_ge(s["mrow_ready"], 12 * L + u + 1)
                    for i in range(4):
                        ins = pe.transpose(bank[6 + u % 2][:, 2 * i:2 * i + 2], mrow[0:2, u % 2, i * P:(i + 1) * P],
                                           ident[0:2, 0:2])
                    ins.then_inc(s["ada_tr"], 1)

                for u in range(12):
                    w = unit_wait(u0, u)
                    if u >= 2:
                        pe.wait_ge(s["mrow_ready"], 12 * L + u - 1)
                    for k in range(KC):
                        ins = pe.matmul(bank[4 + u % 2][0:2, :], csil[:, k, :], w[:, k, :],
                                        start=(k == 0), stop=(k == KC - 1))
                    ins.then_inc(s["ada_mm"], 1)
                    if u:
                        if L == 0 and u == 1:
                            pe.wait_ge(s["cst_loaded"], 16)
                        if u >= 3:
                            pe.wait_ge(s["mT_ready"], 4 * (12 * L + u - 2))
                        tr(u - 1)
                pe.wait_ge(s["mT_ready"], 4 * (12 * L + 10))
                tr(11)

            def build_hT(b, behind=None):
                if b == 0:
                    pe.wait_ge(s["x_loaded"], 16)
                else:
                    pe.wait_ge(s["x_ready"], 5 * b)
                for k in range(KC):
                    if k >= 2:
                        pe.wait_ge(s["hTs_ready"], 8 * b + k - 1)
                        pe.wait_ge(s["hTp_ready"], 8 * b + k - 1)
                    for t in range(NT):
                        out = bank[k % 2][:, t * P:(t + 1) * P] if t < NS else bank[2 + k % 2][:, 0:P]
                        ins = pe.transpose(out, X[:, t, k * P:(k + 1) * P], ident)
                    ins.then_inc(s["hT_tr"], 1)
                    if behind and k >= 2:
                        behind(k - 2)
                if behind:
                    hT_whole(b)
                    behind(KC - 2)
                    behind(KC - 1)

            def gates(b, b0=4):
                L, g0 = b // 2, gate_part(b)
                pe.wait_ge(s["mT_ready"], 48 * (L + 1))
                for c in range(2):
                    for h in range(2):
                        for i in range(4):
                            ins = pe.matmul(bank[b0 + 2 * c + h][:, i * P:(i + 1) * P],
                                            mT[:, L, g0 + 4 * h + i, c:c + 1].broadcast_to([P, P]), ident,
                                            start=True, stop=True)
                        ins.then_inc(s["gate_mm"], 1)

            def hT_whole(b):
                pe.wait_ge(s["hTs_ready"], 8 * (b + 1))
                pe.wait_ge(s["hTp_ready"], 8 * (b + 1))

            pe.wait_ge(s["cond_ready"], 1)
            ada(0, U_ADA0)
            build_hT(0)
            gates(0)
            hT_whole(0)
            for i in range(16):
                if i % 4 == 0:
                    w = unit_wait(U_PW1, i // 4)
                if i >= 2:
                    pe.wait_ge(s["glu_a"], i - 1)
                for k in range(KC):
                    lw = w[:, k, (i % 4) * P:(i % 4 + 1) * P]
                    pe.matmul(bank[i % 2][:, :], lw, hT[:, k, 0:SAMPLE], start=(k == 0), stop=(k == KC - 1))
                    ins = pe.matmul(bank[2 + i % 2][:, 0:P], lw, hT[:, k, SAMPLE:TOK], start=(k == 0), stop=(k == KC - 1))
                ins.then_inc(s["pw1_done"], 1)
            pe.wait_ge(s["gate_ready"], 4)
            ada(1, U_ADA1)
            pe.wait_ge(s["glu_a"], 16)
            for i, k in enumerate(CONV_ORDER[:5] + list(CONV_POOL) + CONV_ORDER[5:]):
                if k in CONV_ORDER:
                    pe.wait_ge(s["conv_ready"], CONV_ORDER.index(k) + 1)
                else:
                    pe.wait_ge(s["conv_pool"], CONV_POOL.index(k) + 1)
                pe.matmul(bank[0][:, :], mean_w, v[:, k, 0:SAMPLE], start=(i == 0), stop=(i == KC - 1))
                ins = pe.matmul(bank[2][:, 0:P], mean_w, v[:, k, SAMPLE:TOK], start=(i == 0), stop=(i == KC - 1))
            ins.then_inc(s["mean_mm"], 1)
            for k in range(KC):
                pe.wait_ge(s["sq_ready"], k + 1)
                pe.matmul(bank[1][:, :], mean_w, sq[:, k % 2, 0:SAMPLE], start=(k == 0), stop=(k == KC - 1))
                pe.matmul(bank[3][:, 0:P], mean_w, sq[:, k % 2, SAMPLE:TOK], start=(k == 0),
                          stop=(k == KC - 1)).then_inc(s["var_mm"], 1)
            pe.wait_ge(s["v_ready"], 8)
            pe.wait_ge(s["pwb_loaded"], 16)
            pe.wait_ge(s["mT_ready"], 96)
            for nb in range(2):
                w = unit_wait(U_PW2, nb)
                for t in range(NT):
                    i = nb * NT + t
                    if i >= 8:
                        pe.wait_ge(s["f_added"], i - 7)
                    for k in range(KC):
                        pe.matmul(bank[i % 8][:, :], v[:, k, t * P:(t + 1) * P], w[:, k, :], start=(k == 0), stop=False)
                    ins = pe.matmul(bank[i % 8][:, :], ones[0:1, :], pwb[0:1, nb * 512:(nb + 1) * 512],
                                    start=False, stop=True)
                    ins.then_inc(s["f_mm"], 1)

            def gather(Pi):
                pe.wait_ge(s["psel_ready"], Pi + 1)
                for k in range(KC):
                    ins = pe.matmul(bank[5][:, 128 + 32 * k:160 + 32 * k], X[:, NS, k * P:(k + 1) * P],
                                    psel_p[:, :, 0:CAP_P], start=True, stop=True)
                ins.then_inc(s["gather_mm"], 1)
                for half in range(2):
                    for kk in range(4):
                        k = 4 * half + kk
                        for t in range(NS):
                            ins = pe.matmul(bank[6 + half][:, kk * P:(kk + 1) * P], X[:, t, k * P:(k + 1) * P],
                                            psel[:, t, :, :], start=(t == 0), stop=(t == NS - 1))
                    ins.then_inc(s["gather_mm"], 1)

            def combine(Pi):
                pe.wait_ge(s["out_split"], 8 * Pi + 8)
                pe.wait_ge(s["pt_ready"], 3 * Pi + 3)
                for i in range(2 * NT):
                    t, h = i // 2, i % 2
                    out = bank[COMB_BANKS[i % 3]][:, :]
                    if i >= 3:
                        pe.wait_ge(s["comb_added"], 10 * Pi + (i - 2))
                    for n in range(2):
                        if t < NS:
                            ins = pe.matmul(out, PT[:, t * P:(t + 1) * P],
                                            out_s[n][:, h * 512:(h + 1) * 512], start=(n == 0), stop=(n == 1))
                        else:
                            ins = pe.matmul(out, PT_p[0:64, :], out_p[n][0:64, h * 512:(h + 1) * 512],
                                            start=(n == 0), stop=(n == 1))
                    ins.then_inc(s["comb_mm"], 1)

            def expert(L, u0, p, e):
                Pi = 8 * L + p
                Ei = 16 * L + 2 * p + e
                if e == 0:
                    pe.wait_ge(s["xsplit"], Pi + 1)
                else:
                    pe.wait_ge(s["pt_ready"], 3 * Pi + 3)
                for i in range(4):
                    if i >= 2 and not (L == 0 and e == 0 and isinstance(p, int) and p == 0):
                        pe.wait_ge(s["out_split"], 4 * Ei + (-2 if i == 2 else 0))
                    if i == 3:
                        if e == 1 and not (isinstance(p, int) and p == 0):
                            pe.wait_ge(s["comb_added"], 10 * Pi)
                        turn_hidden(L, p, e, 0)
                    for h in range(2):
                        split_product(L, p, e, 2 * i + h, bank[i], xin_h[:, e, :, :], xin_l[:, e, :, :])\
                            .then_inc(s["gu_mm"], 1)

            def split_product(L, p, e, m, out, ah, al):
                pe.wait_ge(*low_done(L, p, e, m))
                wh, wl = w_h[m % NB], w_l[m % NB]
                for k in range(4):
                    c = 4 * (m % 2) + k
                    pe.matmul(out[0:SLOTS, :], ah[:, c, :], wh[:, k, :], start=(c == 0), stop=False)
                    pe.matmul(out[0:SLOTS, :], ah[:, c, :], wl[:, k, :], start=False, stop=False)
                    ins = pe.matmul(out[0:SLOTS, :], al[:, c, :], wh[:, k, :], start=False, stop=(c == KC - 1))
                return ins

            def turn_hidden(L, p, e, h):
                pe.wait_ge(s["hid_ready"], 2 * (16 * L + 2 * p + e) + (h + 1))
                for i in range(4):
                    ins = pe.transpose(bank[4 + h][:, i * SLOTS:(i + 1) * SLOTS], hid[0:SLOTS, h, i * P:(i + 1) * P],
                                       ident[0:SLOTS, 0:SLOTS])
                ins.then_inc(s["hidT_tr"], 1)

            def expert_down(L, u0, p, e):
                Ei = 16 * L + 2 * p + e
                for h in range(2):
                    for q in range(2):
                        if h == 0:
                            pe.wait_ge(s["hidT_ready"], 2 * Ei + q + 1)
                        split_product(L, p, e, 8 + 2 * h + q, bank[2 + h], hidT_h, hidT_l).then_inc(s["down_mm"], 1)

            def pair(L, u0, p, first, last):
                Pi = 8 * L + p
                expert(L, u0, p, 0)
                pe.wait_ge(s["hid_ready"], 4 * Pi + 1)
                pe.wait_ge(s["acol_ready"], Pi + 1)
                for t in range(NS):
                    ins = pe.transpose(bank[0][:, t * P:(t + 1) * P], psel[:, t, :, :], ident)
                ins.then_inc(s["pt_tr"], 1)
                pe.transpose(bank[1][0:64, 0:P], psel_p[:, :, :], ident)
                for e in range(2):
                    for t in range(NS):
                        pe.matmul(bank[1][0:CAP_S, P + e:P + e + 1], psel[:, t, e, :], ccol[:, 1, t, e:e + 1],
                                  start=(t == 0), stop=(t == NS - 1))
                    ins = pe.matmul(bank[1][CAP_S:SLOTS, P + e:P + e + 1], psel_p[:, e, 0:CAP_P],
                                    ccol[:, 1, NS, e:e + 1], start=True, stop=True)
                ins.then_inc(s["pt_tr"], 1)
                turn_hidden(L, p, 0, 1)
                if not first:
                    pe.wait_ge(s["hidT_ready"], 4 * Pi + 1)
                    combine(Pi - 1)
                expert_down(L, u0, p, 0)
                expert(L, u0, p, 1)
                if not last:
                    if not first:
                        pe.wait_ge(s["comb_added"], 10 * Pi)
                    gather(Pi + 1)
                    pe.wait_ge(s["xin_ready"], 16 * Pi + 24)
                turn_hidden(L, p, 1, 1)
                expert_down(L, u0, p, 1)

            def moe(L, u0):
                b = 2 * L + 1
                pe.wait_ge(s["wr_loaded"], 16)

                def logits(k):
                    for out, lo, hi in ((bank[4], 0, SAMPLE), (bank[5], SAMPLE, TOK)):
                        ins = pe.matmul(out[0:EXPERTS, 0:hi - lo], wr[:, L, k, :], hT[:, k, lo:hi],
                                        start=(k == 0), stop=(k == KC - 1))
                    if k == KC - 1:
                        ins.then_inc(s["logits_mm"], 1)

                build_hT(b, logits)
                pe.wait_ge(s["lgT_ready"], L + 1)
                for t in range(NT):
                    ins = pe.transpose(bank[7][:, t * EXPERTS:(t + 1) * EXPERTS], work[0:EXPERTS, t * P:(t + 1) * P],
                                       ident[0:EXPERTS, 0:EXPERTS])
                ins.then_inc(s["logits_tr"], 1)
                pe.wait_ge(s["aff_ready"], L + 1)
                for t in range(NT):
                    out = bank[5][0:EXPERTS, t * P:(t + 1) * P] if t < NS else bank[6][0:EXPERTS, 0:P]
                    ins = pe.transpose(out, aff[:, t, :], ident)
                ins.then_inc(s["aff_tr"], 1)
                gates(b, 0)
                pe.wait_ge(s["posm_ready"], L + 1)
                for t in range(NT):
                    ins = pe.transpose(bank[4][:, t * EXPERTS:(t + 1) * EXPERTS], pos[0:EXPERTS, t * P:(t + 1) * P],
                                       ident[0:EXPERTS, 0:EXPERTS])
                ins.then_inc(s["pos_tr"], 1)
                gather(8 * L)
                pe.wait_ge(s["gate_ready"], 4 * (b + 1))
                pair(L, u0, 0, True, False)
                with pe.Fori(1, PAIRS - 1) as p:
                    pair(L, u0, p, False, False)
                pair(L, u0, PAIRS - 1, False, True)
                combine(8 * L + 7)

            moe(0, U_MOE0)

            build_hT(2)
            gates(2)
            hT_whole(2)
            pe.wait_ge(s["gate_ready"], 12)
            pe.wait_ge(s["ssdp_loaded"], 32)
            for t in range(NT):
                for k in range(KC):
                    ins = pe.matmul(bank[7][:, t * 64:(t + 1) * 64], hT[:, k, t * P:(t + 1) * P], wdt[:, k, :],
                                    start=(k == 0), stop=(k == KC - 1))
            ins.then_inc(s["dtr_mm"], 1)

            def ssd_project(g, j, w):
                i = 6 * g + j
                if i >= 2:
                    pe.wait_ge(s["raw_ready"], i - 1)
                c0 = (j if j < 2 else j - 2) * P
                for k in range(KC):
                    pe.matmul(bank[i % 2][:, :], w[:, k, c0:c0 + P], hT[:, k, 0:SAMPLE], start=(k == 0), stop=(k == KC - 1))
                    ins = pe.matmul(bank[2 + i % 2][:, 0:P], w[:, k, c0:c0 + P], hT[:, k, SAMPLE:TOK],
                                    start=(k == 0), stop=(k == KC - 1))
                ins.then_inc(s["cproj_mm"], 1)

            def ssd_turn(g, j):
                i = 6 * g + j
                n = 5 * g + (0 if j == 0 else j - 1)
                pe.wait_ge(s["xf_ready"], i + 1)
                if n >= 2:
                    pe.wait_ge(s["xs_a"], n - 1)
                    pe.wait_ge(s["xs_v"], n - 1)
                src = BT if j == 0 else xf[:, j % 2, :]
                for t in range(NT):
                    out = bank[4 + n % 2][:, t * P:(t + 1) * P] if t < NS else bank[6 + n % 2][:, 0:P]
                    ins = pe.transpose(out, src[:, t * P:(t + 1) * P], ident)
                ins.then_inc(s["xtr_mm"], 1)

            def z_part(g, t, k, w):
                ins = pe.matmul(bank[(0, 6, 7, 0, 1)[t]][:, :], hT[:, k, t * P:(t + 1) * P], w[:, k, :],
                                start=(k == 0), stop=(k == KC - 1))
                if k == KC - 1:
                    ins.then_inc(s["z_mm"], 1)

            for g in range(GROUPS):
                u0 = U_SSD + 4 * g
                if g:
                    pe.wait_ge(s["out_added"], 10 * g)
                j0 = u0 % R
                pe.wait_ge(landed[j0], 16 * (u0 // R + 1))
                w_bc = ring[j0][:, 0:UNIT // 2].rearrange("p (k n) -> p k n", n=256)
                ssd_project(g, 0, w_bc)
                if g == 0:
                    pe.wait_ge(s["dt_a"], 1)
                ssd_project(g, 1, w_bc)
                w_x = unit_wait(u0, 1)
                for j in range(2, 6):
                    ssd_project(g, j, w_x)
                    if j != 3:
                        ssd_turn(g, j - 2)
                w_z = unit_wait(u0, 2)
                pe.wait_ge(s["raw_ready"], 6 * g + 5)
                for k in range(KC):
                    z_part(g, 0, k, w_z)
                ssd_turn(g, 4)
                ssd_turn(g, 5)
                if g == 0:
                    pe.wait_ge(s["da_ready"], 1)
                    pe.wait_ge(s["xs_a"], 5)
                    pe.wait_ge(s["xs_v"], 5)
                    for c in range(NT):
                        bk = bank[(7, 7, 6, 6, 5)[c]]
                        o = 192 * (c % 2)
                        pe.matmul(bk[:, o:o + 32], m_le, da[:, c, 0:32], start=True, stop=True)
                        pe.matmul(bk[:, o + 32:o + 64], m_ge, da[:, c, 32:64], start=True, stop=True)
                        pe.matmul(bk[:, o + 64:o + 96], m_gt, da[:, c, 0:32], start=True, stop=True)
                        pe.matmul(bk[:, o + 96:o + 128], m_lt, da[:, c, 32:64], start=True, stop=True)
                        pe.matmul(bk[:, o + 128:o + 192], ones, da[:, c, :], start=True, stop=True).then_inc(s["cum_mm"], 1)
                pe.wait_ge(s["xs_a"], 5 * g + 5)
                pe.wait_ge(s["xs_v"], 5 * g + 5)
                if g == 0:
                    pe.wait_ge(s["ex_ready"], 5)
                for c in range(NT):
                    out = bank[4][:, c * P:(c + 1) * P] if c < NS else bank[5][:, 0:P]
                    ins = pe.matmul(out, BT[:, c * P:(c + 1) * P], CT[:, c * P:(c + 1) * P], start=True, stop=True)
                ins.then_inc(s["cb_mm"], 1)
                pe.wait_ge(s["raw_ready"], 6 * g + 6)
                pe.wait_ge(s["cbm_ready"], 4 * (g + 1))

                def seg(i):
                    n = 10 * g + i
                    if n >= 2:
                        pe.wait_ge(s["exp_m"], 2 * (n - 1))
                    for dr in range(2):
                        pe.wait_ge(s["aM_ready"], 2 * n + dr + 1)
                        for h in range(4):
                            ins = pe.matmul(bank[2 * dr + n % 2][:, h * P:(h + 1) * P],
                                            aM[:, 2 * (n % 2) + dr, h * P:(h + 1) * P], m_le if dr == 0 else m_ge,
                                            start=True, stop=True)
                        ins.then_inc(s["seg_mm"], 1)

                def ydiag(i):
                    n = 10 * g + i
                    if n >= 2:
                        pe.wait_ge(s["yd_added"], n - 1)
                    pe.wait_ge(s["m_ready"], 2 * n + 2)
                    pe.wait_ge(s["xd_ready"], 2 * n + 2)
                    for h in range(4):
                        for dr in range(2):
                            a = 2 * (n % 2) + dr
                            ins = pe.matmul(bank[4 + n % 2][:, h * HD:(h + 1) * HD], Em[:, a, h * P:(h + 1) * P],
                                            Xd[:, a, h * HD:(h + 1) * HD], start=(dr == 0), stop=(dr == 1))
                    ins.then_inc(s["yd_mm"], 1)

                pe.wait_ge(s["z_silu"], NT * g + 1)
                seg(0)
                for i in range(1, 2 * NT):
                    seg(i)
                    if i <= KC:
                        for m in (2 * i - 2, 2 * i - 1):
                            z_part(g, 1 + m // KC, m % KC, w_z)
                    ydiag(i - 1)
                ydiag(2 * NT - 1)
                for i, (dr, c, off, stt, noff, nst, prev) in enumerate(scan_tasks()):
                    noff += 8 * g
                    nst += 8 * g
                    if off:
                        if noff % 8 < 2:
                            pe.wait_ge(s["yd_added"], 10 * (g + 1))
                        else:
                            pe.wait_ge(s["off_added"], noff - 1)
                        pe.wait_ge(s["state_loaded"], 32 * (g + 1))
                        if prev:
                            pe.wait_ge(s["prev_ready"], 8 * g + prev)
                        pe.matmul(bank[4 + noff % 2][:, :], CT[:, c * P:(c + 1) * P], prevS[:, dr, :],
                                  start=True, stop=True).then_inc(s["off_mm"], 1)
                    if stt:
                        pe.wait_ge(s["xw_ready"], nst + 1)
                        if nst % 8 < 2:
                            pe.wait_ge(s["z_silu"], NT * g + 2 + nst % 8)
                        else:
                            pe.wait_ge(s["prev_ready"], nst - 1)
                        pe.matmul(bank[6 + nst % 2][:, :], Btok[:, c, :], xw[:, nst % 2, :], start=True, stop=True)\
                          .then_inc(s["st_mm"], 1)
                    if i < KC:
                        if i == 0:
                            pe.wait_ge(s["exp_m"], 20 * (g + 1))
                        z_part(g, 3, i, w_z)
                for k in range(KC):
                    z_part(g, 4, k, w_z)
                j3 = (u0 + 3) % R
                pe.wait_ge(landed[j3], 16 * ((u0 + 3) // R + 1))
                wo_l = ring_low[j3][:, :].rearrange("p (k n) -> p k n", n=D)

                def turn_y(t):
                    n = NT * g + t
                    pe.wait_ge(s["y_normed"], n + 1)
                    if t == 2:
                        pe.wait_ge(s["prev_ready"], 8 * (g + 1))
                    if t == NS:
                        pe.wait_ge(s["yT_low"], 4 * (NT * g + 1))
                    for i in range(4):
                        ins = pe.transpose(bank[4 + t % NS][:, i * P:(i + 1) * P], Y[:, t, i * P:(i + 1) * P], ident)
                    ins.then_inc(s["ytr_mm"], 1)

                for t in range(NS):
                    turn_y(t)
                pe.wait_ge(s["wo_high"], 4 * (g + 1))
                pe.wait_ge(s["z_silu"], NT * (g + 1))
                pe.wait_ge(s["prev_ready"], 8 * (g + 1))
                for i in range(2 * NT):
                    t, h = i // 2, i % 2
                    if i == 4:
                        turn_y(NS)
                    pe.wait_ge(s["yT_low"], 4 * (NT * g + (NT if i >= 4 else t + 1)))
                    if i >= 8:
                        pe.wait_ge(s["out_added"], 10 * g + i - 7)
                    n = slice(h * 512, (h + 1) * 512)
                    for k in range(4):
                        yh = yT_h[:, k, t * P:(t + 1) * P]
                        yl = yT_l[:, t, k, :] if t < NS else yT_l4[:, k, :]
                        pe.matmul(bank[i % 8][:, :], yh, wo_h[k][:, n], start=(k == 0), stop=False)
                        pe.matmul(bank[i % 8][:, :], yl, wo_h[k][:, n], start=False, stop=False)
                    for k in range(4):
                        if i == 0:
                            pe.wait_ge(s["wo_low"], 4 * g + k + 1)
                        ins = pe.matmul(bank[i % 8][:, :], yT_h[:, k, t * P:(t + 1) * P], wo_l[:, k, n],
                                        start=False, stop=(k == 3))
                    ins.then_inc(s["out_mm"], 1)

            moe(1, U_MOE1)

        @block.scalar
        def _(act):
            step = Steps(act, s["act_step"])
            A = nc.scalar.activation

            def ada(L):
                def bias_cols(u):
                    act.wait_ge(s["ada_tr"], 12 * L + u + 1)
                    if L == 0 and u == 0:
                        act.wait_ge(s["adab_ready"], 4)
                    for i in range(4):
                        c = 4 * u + i
                        A(mT[:, L, c, :], bank[6 + u % 2][:, 2 * i:2 * i + 2], ACT.Identity,
                          bias=ada_bT[:, 48 * L + c:48 * L + c + 1]).then_inc(s["mT_ready"], 1)

                for u in range(12):
                    act.wait_ge(s["ada_mm"], 12 * L + u + 1)
                    if u >= 2:
                        act.wait_ge(s["ada_tr"], 12 * L + u - 1)
                    A(mrow[0:2, u % 2, :], bank[4 + u % 2][0:2, :], ACT.Copy).then_inc(s["mrow_ready"], 1)
                    if u:
                        bias_cols(u - 1)
                bias_cols(11)

            def hT_evac(b):
                L, sh = b // 2, shift_part(b)
                act.wait_ge(s["mT_ready"], 48 * (L + 1))
                for k in range(KC):
                    act.wait_ge(s["hT_tr"], 8 * b + k + 1)
                    A(hT[:, k, 0:SAMPLE], bank[k % 2][:, :], ACT.Identity, bias=mT[:, L, sh + k, 0:1],
                      scale=mT[:, L, sh + 8 + k, 0:1]).then_inc(s["hTs_ready"], 1)

            def gate_evac(b, b0=4):
                for i in range(4):
                    act.wait_ge(s["gate_mm"], 4 * b + i + 1)
                    A(gate_bc[:, i // 2, (i % 2) * 512:(i % 2 + 1) * 512], bank[b0 + i][:, :], ACT.Copy)\
                        .then_inc(s["gate_ready"], 1)

            def normalise(b):
                for t in range(NT):
                    act.wait_ge(s["ln_stat"], NT * b + t + 1)
                    r = rst[:, t:t + 1]
                    step(A(r, r, ACT.Sqrt))
                    step.sync()
                    step(A(nmean[:, 1, t:t + 1], nmean[:, 0, t:t + 1], ACT.Copy, scale=r))
                    step.sync()
                    A(X[:, t, :], X[:, t, :], ACT.Identity, bias=nmean[:, 1, t:t + 1], scale=r)\
                        .then_inc(s["ln_normed"], 1)

            act.wait_ge(s["par_loaded"], 16)
            A(csil[:, :, :].rearrange("p a b -> p (a b)"), cond, ACT.Silu).then_inc(s["cond_ready"], 1)
            ada(0)
            hT_evac(0)
            gate_evac(0)
            act.wait_ge(s["upad_zero"], 1)
            for i in range(16):
                c = (i // 8) * 4 + i % 4
                act.wait_ge(s["pw1_done"], i + 1)
                a, b = bank[i % 2], bank[2 + i % 2]
                if (i // 4) % 2 == 0:
                    bias = pw1_b[:, c:c + 1]
                    step(A(upad[:, c, 0:8, HALO:HALO + GRID_W], a[:, :].rearrange("p (r w) -> p r w", w=GRID_W),
                           ACT.Identity, bias=bias))
                    step(A(upad[:, c, 8, HALO:PITCH], b[:, 0:PITCH - HALO], ACT.Identity, bias=bias))
                    step.sync()
                    A(upad[:, c, 9, 0:PITCH - HALO], b[:, GRID_W - HALO:P], ACT.Identity, bias=bias).then_inc(s["glu_a"], 1)
                else:
                    bias = pw1_b[:, 8 + c:9 + c]
                    step(A(sig[:, c, 0:SAMPLE], a[:, :], ACT.Sigmoid, bias=bias))
                    step.sync()
                    A(sig[:, c, SAMPLE:TOK], b[:, 0:P], ACT.Sigmoid, bias=bias).then_inc(s["glu_a"], 1)
            ada(1)
            for k in range(KC):
                act.wait_ge(s["centered"], k + 1)
                if k >= 2:
                    act.wait_ge(s["var_mm"], k - 1)
                A(sq[:, k % 2, :], v[:, k, :], ACT.Square).then_inc(s["sq_ready"], 1)
            act.wait_ge(s["var_ready"], 2)
            A(rstd, rstd, ACT.Sqrt).then_inc(s["rstd_ready"], 1)
            for k in range(KC):
                act.wait_ge(s["normed"], k + 1)
                A(v[:, k, :], v[:, k, :], ACT.Silu, bias=cln_b[:, k:k + 1], scale=cln_g[:, k:k + 1])\
                    .then_inc(s["v_ready"], 1)
            normalise(0)

            def xin_evac(L, Pi):
                sh = shift_part(1)
                act.wait_ge(s["gather_mm"], 3 * Pi + 1)
                for k in range(KC):
                    A(xin[:, :, k, CAP_S:SLOTS],
                      bank[5][:, 128 + 32 * k:160 + 32 * k].rearrange("p (e c) -> p e c", c=CAP_P), ACT.Identity,
                      bias=mT[:, L, sh + k, 1:2], scale=mT[:, L, sh + 8 + k, 1:2]).then_inc(s["xin_ready"], 1)
                for k in range(KC):
                    if k % 4 == 0:
                        act.wait_ge(s["gather_mm"], 3 * Pi + (2 + k // 4))
                    A(xin[:, :, k, 0:CAP_S],
                      bank[6 + k // 4][:, (k % 4) * P:(k % 4 + 1) * P].rearrange("p (e c) -> p e c", c=CAP_S),
                      ACT.Identity, bias=mT[:, L, sh + k, 0:1], scale=mT[:, L, sh + 8 + k, 0:1])\
                        .then_inc(s["xin_ready"], 1)

            def high(L, u0, p, e, m):
                Ei = 16 * L + 2 * p + e
                u = 6 * e + m // 2
                j = (u0 + u) % R
                act.wait_ge(landed[j], 16 * ((u0 + u) // R + 1) + p * (16 * 12 // R))
                if not (L == 0 and e == 0 and isinstance(p, int) and p == 0 and m < NB):
                    if m < NB:
                        act.wait_ge(s["down_mm"], 4 * Ei + (m - 2))
                    elif m < NB + 8:
                        act.wait_ge(s["gu_mm"], 8 * Ei + (m - NB + 1))
                    else:
                        act.wait_ge(s["down_mm"], 4 * Ei + (m - NB - 7))
                src = ring[j][:, (m % 2) * HALF:(m % 2 + 1) * HALF].rearrange("p (k n) -> p k n", n=512)
                A(w_h[m % NB][:, :, :], src, ACT.Copy).then_inc(s["high_ready"], 1)

            def silu(L, p, e, h):
                Ei = 16 * L + 2 * p + e
                act.wait_ge(s["gu_mm"], 8 * Ei + (4 * h + 2))
                if not (L == 0 and e == 0 and isinstance(p, int) and p == 0):
                    act.wait_ge(s["hidT_tr"], 2 * Ei + (h - 1))
                A(hid[0:SLOTS, h, :], bank[2 * h][0:SLOTS, :], ACT.Silu).then_inc(s["silu_ready"], 1)

            def down_evac(L, p, e, h):
                Ei = 16 * L + 2 * p + e
                act.wait_ge(s["down_mm"], 4 * Ei + (2 * h + 2))
                c = slice(h * 512, (h + 1) * 512)
                bk = bank[2 + h]
                A(bk[0:SLOTS, :], bk[0:SLOTS, :], ACT.Copy, scale=gcol[0:SLOTS, e:e + 1]).then_inc(s["gated"], 1)
                act.wait_ge(s["gated"], 2 * Ei + (h + 1))
                A(out_s[0][64 * e:64 * e + CAP_S, c], bk[0:CAP_S, :], ACT.Copy).then_inc(s["down_out"], 1)
                A(out_p[0][32 * e:32 * e + CAP_P, c], bk[CAP_S:SLOTS, :], ACT.Copy).then_inc(s["down_out"], 1)

            def pair(L, u0, p, last):
                Pi = 8 * L + p
                for e in range(2):
                    def nxt(m):
                        if e == 0:
                            high(L, u0, p, 1, m)
                        elif not last:
                            high(L, u0, p + 1, 0, m)

                    high(L, u0, p, e, 3)
                    high(L, u0, p, e, 4)
                    silu(L, p, e, 0)
                    for m in range(5, 9):
                        high(L, u0, p, e, m)
                    silu(L, p, e, 1)
                    high(L, u0, p, e, 9)
                    high(L, u0, p, e, 10)
                    if e == 0:
                        act.wait_ge(s["pt_tr"], 2 * Pi + 2)
                        if not (L == 0 and isinstance(p, int) and p == 0):
                            act.wait_ge(s["comb_mm"], 10 * Pi)
                            act.wait_ge(s["out_split"], 8 * Pi)
                        A(gcol[0:SLOTS, :], bank[1][0:SLOTS, P:P + 2], ACT.Copy).then_inc(s["pt_ready"], 1)
                        A(PT[:, :], bank[0][:, :], ACT.Copy).then_inc(s["pt_ready"], 1)
                        A(PT_p[0:64, :], bank[1][0:64, 0:P], ACT.Copy).then_inc(s["pt_ready"], 1)
                        act.wait_ge(s["pt_ready"], 3 * Pi + 1)
                    elif not last:
                        xin_evac(L, Pi + 1)
                    high(L, u0, p, e, 11)
                    nxt(0)
                    nxt(1)
                    down_evac(L, p, e, 0)
                    nxt(2)
                    down_evac(L, p, e, 1)

            def moe(L, u0):
                b = 2 * L + 1
                hT_evac(b)
                act.wait_ge(s["lg_ready"], L + 1)
                A(lg, lg, ACT.Exp).then_inc(s["exp_ready"], 1)
                gate_evac(b, 0)
                for m in range(NB):
                    high(L, u0, 0, 0, m)
                xin_evac(L, 8 * L)
                pair(L, u0, 0, False)
                with act.Fori(1, PAIRS - 1) as p:
                    pair(L, u0, p, False)
                pair(L, u0, PAIRS - 1, True)
                normalise(b)

            moe(0, U_MOE0)

            hT_evac(2)
            gate_evac(2)
            act.wait_ge(s["ssdp_loaded"], 32)
            A(srow[:, 64:128], srow[:, 64:128], ACT.Exp).then_inc(s["dt_b"], 1)
            act.wait_ge(s["dt_a"], 2)
            A(dtmp[:, 1, :], dtmp[:, 1, :], ACT.Exp).then_inc(s["dt_b"], 1)
            act.wait_ge(s["dt_a"], 3)
            A(dtmp[:, 2, :], dtmp[:, 2, :], ACT.Ln).then_inc(s["dt_b"], 1)

            def ssd_raw(g, j):
                i = 6 * g + j
                act.wait_ge(s["cproj_mm"], i + 1)
                if i >= 2:
                    act.wait_ge(s["cconv_ready"], i - 1)
                step(A(raw[:, i % 2, 2:2 + SAMPLE], bank[i % 2][:, :], ACT.Copy))
                step.sync()
                A(raw[:, i % 2, SAMPLE + 6:SAMPLE + 6 + P], bank[2 + i % 2][:, 0:P], ACT.Copy).then_inc(s["raw_ready"], 1)

            def ssd_silu(g, j):
                i = 6 * g + j
                act.wait_ge(s["cconv_ready"], i + 1)
                if j >= 4:
                    act.wait_ge(s["xtr_mm"], 5 * g + j - 2)
                dst = (BT, CT)[j] if j < 2 else xf[:, j % 2, :]
                A(dst, cv[:, i % 2, :], ACT.Silu).then_inc(s["xf_ready"], 1)

            def ssd_xs(g, j):
                n = 5 * g + (0 if j == 0 else j - 1)
                act.wait_ge(s["xtr_mm"], n + 1)
                src = bank[4 + n % 2][:, :].rearrange("p (t c) -> p t c", c=P)
                dst = Btok[:, 0:NS, :] if j == 0 else xs[:, 0:NS, (j - 2) * P:(j - 1) * P]
                A(dst, src, ACT.Copy).then_inc(s["xs_a"], 1)

            def z_silu(g, t):
                act.wait_ge(s["z_mm"], NT * g + t + 1)
                A(zt[t], bank[(0, 6, 7, 0, 1)[t]][:, :], ACT.Silu).then_inc(s["z_silu"], 1)

            def rms_sqrt(g, ts, n):
                act.wait_ge(s["rms_a"], 2 * g + n)
                A(rms[:, 1, ts], rms[:, 1, ts], ACT.Sqrt).then_inc(s["rms_b"], 1)

            def yT_evac(g, t):
                act.wait_ge(s["ytr_mm"], NT * g + t + 1)
                for i in range(4):
                    A(yT_h[:, i, t * P:(t + 1) * P], bank[4 + t % NS][:, i * P:(i + 1) * P], ACT.Copy,
                      scale=norm_w[:, 4 * g + i:4 * g + i + 1]).then_inc(s["yT_ready"], 1)

            for g in range(GROUPS):
                act.wait_ge(s["upad_zero"], g + 2)
                ssd_raw(g, 0)
                for j in range(6):
                    if j < 5:
                        ssd_raw(g, j + 1)
                    ssd_silu(g, j)
                    if j == 2:
                        ssd_xs(g, 0)
                    if j >= 4:
                        ssd_xs(g, j - 2)
                z_silu(g, 0)
                ssd_xs(g, 4)
                ssd_xs(g, 5)
                if g == 0:
                    for c in range(NT):
                        act.wait_ge(s["cum_mm"], NT)
                        o = 192 * (c % 2)
                        A(Ex[:, c, :], bank[(7, 7, 6, 6, 5)[c]][:, o:o + 192], ACT.Exp).then_inc(s["ex_ready"], 1)
                for i in range(2 * NT):
                    n = 10 * g + i
                    if n >= 2:
                        act.wait_ge(s["yd_mm"], n - 1)
                    for dr in range(2):
                        act.wait_ge(s["seg_mm"], 2 * n + dr + 1)
                        A(Em[:, 2 * (n % 2) + dr, :], bank[2 * dr + n % 2][:, :], ACT.Exp).then_inc(s["exp_m"], 1)
                for t in range(1, NS):
                    z_silu(g, t)
                j3 = (U_SSD + 4 * g + 3) % R
                act.wait_ge(landed[j3], 16 * ((U_SSD + 4 * g + 3) // R + 1))
                act.wait_ge(s["m_ready"], 20 * (g + 1))
                for k in range(4):
                    if k == 1:
                        act.wait_ge(s["xw_ready"], 8 * (g + 1))
                    if k == 3:
                        act.wait_ge(s["st_mm"], 8 * (g + 1))
                    A(wo_h[k][:, :], ring[j3][:, k * D:(k + 1) * D], ACT.Copy).then_inc(s["wo_high"], 1)
                rms_sqrt(g, slice(0, NS), 1)
                z_silu(g, NS)
                for t in range(NT):
                    if t == 3:
                        rms_sqrt(g, slice(NS, NT), 2)
                    yT_evac(g, t)
            normalise(2)
            moe(1, U_MOE1)

        @block.gpsimd
        def _(pool):
            def moe_low(L, u0):
                with pool.Fori(0, EXPERTS) as E:
                    for m in POOL_LOW:
                        j = (u0 + m // 2) % R
                        pool.wait_ge(s["high_ready"], HALVES * (16 * L + E) + (m + 1))
                        src = ring[j][:, (m % 2) * HALF:(m % 2 + 1) * HALF].rearrange("p (k n) -> p k n", n=512)
                        nc.gpsimd.tensor_tensor(w_l[m % NB][:, :, :], src, w_h[m % NB][:, :, :].bitcast(F32),
                                                ALU.subtract).then_inc(s["low_pool"], 1)

            pool.dma_start(wr[:, :, :, :], router).then_inc(s["wr_loaded"], 16)
            pool.dma_start(pwb[0:1, :], pw2_b).then_inc(s["pwb_loaded"], 16)
            pool.dma_start(ln_gb[:, :, :], ln_rows[0:1].partition_broadcast(P)).then_inc(s["ln_loaded"], 16)
            nc.gpsimd.memset(upad.rearrange("p a b c -> p (a b c)"), 0.0).then_inc(s["upad_zero"], 1)
            pool_step = Steps(pool, s["pool_step"])
            for c in CONV_POOL:
                glu(c, nc.gpsimd, pool_step, s["glu_sig_pool"], CONV_POOL.index(c) + 1)
                out, rows = taps(c)
                pool_step(nc.gpsimd.tensor_scalar(out, rows(0), dw_w[:, c, 0:1], dw_b[:, c:c + 1], ALU.mult, ALU.add))
                for k in range(1, TAPS):
                    prod = pconv[:, k % 2, :].rearrange("p (r w) -> p r w", w=GRID_W)
                    pool_step(nc.gpsimd.tensor_scalar(prod, rows(k), dw_w[:, c, k:k + 1], None, ALU.mult))
                    pool_step.sync()
                    ins = nc.gpsimd.tensor_tensor(out, out, prod, ALU.add)
                    if k < TAPS - 1:
                        pool_step(ins)
                    else:
                        ins.then_inc(s["conv_pool"], 1)

            def ln_shift(b):
                pool.wait_ge(s["ln_loaded"], 16 * (b + 1))
                for t in range(NT):
                    if t < NT - 1:
                        pool.wait_ge(s["ln_normed"], NT * b + t + 1)
                        pool_step(nc.gpsimd.tensor_tensor(X[:, t, :], X[:, t, :], ln_gb[:, 0, :], ALU.mult))
                        pool_step.sync()
                    else:
                        pool.wait_ge(s["ln_scaled"], b + 1)
                    nc.gpsimd.tensor_tensor(X[:, t, :], X[:, t, :], ln_gb[:, 1, :], ALU.add).then_inc(s["x_ready"], 1)

            ln_shift(0)
            for b in range(1, 4):
                pool.wait_ge(s["x_ready"], 5 * b)
                pool.wait_ge(s["ln_loaded"], 16 * b)
                pool.dma_start(ln_gb[:, :, :], ln_rows[b:b + 1].partition_broadcast(P)).then_inc(s["ln_loaded"], 16)
                if b != 2:
                    moe_low(b // 2, U_MOE0 if b == 1 else U_MOE1)
                    ln_shift(b)
                    continue
                pool.dma_start(srow, ssd_rows.partition_broadcast(P)).then_inc(s["ssdp_loaded"], 16)
                pool.dma_start(wdt, w_dt).then_inc(s["ssdp_loaded"], 16)
                for g in range(GROUPS):
                    if g:
                        pool.wait_ge(s["out_mm"], 10 * g)
                    nc.gpsimd.memset(raw, 0.0).then_inc(s["upad_zero"], 1)
                    for dr in range(2):
                        if g:
                            pool.wait_ge(s["off_mm"], 8 * g)
                            pool.wait_ge(s["st_out"], 32 * g)
                        pool.dma_start(prevS[:, dr, :], state_in[dr, :, g * GC:(g + 1) * GC]).then_inc(s["state_loaded"], 16)
                    pool.wait_ge(s["xs_a"], 5 * g + 5)
                    pool.wait_ge(s["xs_v"], 5 * g + 5)

                    def y_init():
                        skip = srow[:, 128 + HG * g:128 + HG * (g + 1)]
                        for t in range(NT):
                            nc.gpsimd.tensor_tensor(
                                Y[:, t, :].rearrange("p (h d) -> p h d", d=HD),
                                xs[:, t, :].rearrange("p (h d) -> p h d", d=HD),
                                skip.rearrange("p (h d) -> p h d", d=1).broadcast_to([P, HG, HD]),
                                ALU.mult).then_inc(s["y_init"], 1)
                    if g == 0:
                        pool.wait_ge(s["da_ready"], 1)
                    for i in range(2 * NT):
                        n = 10 * g + i
                        c, q = i // 2, i % 2
                        if i == 2:
                            y_init()
                        if n >= 2:
                            pool.wait_ge(s["seg_mm"], 2 * (n - 1))
                        for dr in range(2):
                            h0 = 32 * dr + HG * g + 4 * q
                            nc.gpsimd.tensor_tensor(
                                aM[:, 2 * (n % 2) + dr, :].rearrange("p (h k) -> p h k", k=P),
                                (m_gt if dr == 0 else m_lt).rearrange("p (h k) -> p h k", h=1).broadcast_to([P, 4, P]),
                                da[:, c, h0:h0 + 4].rearrange("p (h k) -> p h k", k=1).broadcast_to([P, 4, P]),
                                ALU.mult).then_inc(s["aM_ready"], 1)
                    for k, (dr, c) in enumerate([x[:2] for x in scan_tasks() if x[3]]):
                        n = 8 * g + k
                        if n >= 2:
                            pool.wait_ge(s["st_mm"], n - 1)
                        if n == 0:
                            pool.wait_ge(s["dt_c"], 1)
                        h0 = 32 * dr + HG * g
                        nc.gpsimd.tensor_tensor(
                            xw[:, n % 2, :].rearrange("p (h d) -> p h d", d=HD), xs[:, c, :].rearrange("p (h d) -> p h d", d=HD),
                            wst[:, c, h0:h0 + HG].rearrange("p (h d) -> p h d", d=1).broadcast_to([P, HG, HD]),
                            ALU.mult).then_inc(s["xw_ready"], 1)
                    j3 = (U_SSD + 4 * g + 3) % R
                    for k in range(4):
                        pool.wait_ge(s["wo_high"], 4 * g + k + 1)
                        w = slice(k * D, (k + 1) * D)
                        nc.gpsimd.tensor_tensor(ring_low[j3][:, w], ring[j3][:, w], wo_h[k][:, :].bitcast(F32),
                                                ALU.subtract).then_inc(s["wo_low"], 1)
                    for dr, n in ((1, 7), (0, 8)):
                        pool.wait_ge(s["prev_ready"], 8 * g + n)
                        pool.dma_start(state_out[dr, :, g * GC:(g + 1) * GC], prevS[:, dr, :]).then_inc(s["st_out"], 16)
                ln_shift(2)

        @block.vector
        def _(dve):
            V = nc.vector
            step = Steps(dve, s["dve_step"])

            def link(ins):
                step(ins)
                step.sync()

            def hT_evac(b):
                L, sh = b // 2, shift_part(b)
                dve.wait_ge(s["mT_ready"], 48 * (L + 1))
                for k in range(KC):
                    dve.wait_ge(s["hT_tr"], 8 * b + k + 1)
                    V.tensor_scalar(hT[:, k, SAMPLE:TOK], bank[2 + k % 2][:, 0:P], mT[:, L, sh + 8 + k, 1:2],
                                    mT[:, L, sh + k, 1:2], ALU.mult, ALU.add).then_inc(s["hTp_ready"], 1)

            def residual(f, t, h, buf, out_sem=None):
                c = slice(h * 512, (h + 1) * 512)
                link(V.tensor_tensor(tmp[:, buf, :], f, gate_bc[:, int(t == NS), c], ALU.mult))
                ins = V.scalar_tensor_tensor(X[:, t, c], X[:, t, c], ALPHA, tmp[:, buf, :], ALU.mult, ALU.add)
                if out_sem is not None:
                    ins.then_inc(out_sem, 1)
                else:
                    step(ins)

            def ln_stats(b, t):
                step.sync()
                for h in range(2):
                    step(V.bn_stats(st[:, t, h, :], X[:, t, h * 512:(h + 1) * 512]))
                step.sync()
                link(V.bn_aggr(mv[:, t, :], st[:, t, :, :]))
                step(V.tensor_scalar(nmean[:, 0, t:t + 1], mv[:, t, 0:1], -1.0, None, ALU.mult))
                link(V.tensor_scalar(rst[:, t:t + 1], mv[:, t, 1:2], EPS, None, ALU.add))
                V.reciprocal(rst[:, t:t + 1], rst[:, t:t + 1]).then_inc(s["ln_stat"], 1)

            def ln_scale(b):
                t = NT - 1
                dve.wait_ge(s["ln_normed"], NT * (b + 1))
                dve.wait_ge(s["ln_loaded"], 16 * (b + 1))
                V.tensor_tensor(X[:, t, :], X[:, t, :], ln_gb[:, 0, :], ALU.mult).then_inc(s["ln_scaled"], 1)

            def finish_tile(b, t, f):
                for h in range(2):
                    residual(f[:, t, h * 512:(h + 1) * 512], t, h, h)
                ln_stats(b, t)
                if t == NT - 1:
                    ln_scale(b)

            dve.wait_ge(s["par_loaded"], 16)
            for L in range(DEPTH):
                for c in (8, 32):
                    V.tensor_scalar(ada_bT[:, 48 * L + c:48 * L + c + 8], ada_bT[:, 48 * L + c:48 * L + c + 8],
                                    1.0, None, ALU.add).then_inc(s["adab_ready"], 1)
            hT_evac(0)
            for chunks in CONV_DVE:
                for c in chunks:
                    glu(c, V, step, s["glu_sig"], CONV_ORDER.index(c) + 1)
                for k in range(TAPS):
                    for j, c in enumerate(chunks):
                        out, rows = taps(c)
                        if k == 0:
                            step(V.tensor_scalar(out, rows(0), dw_w[:, c, 0:1], dw_b[:, c:c + 1], ALU.mult, ALU.add))
                            continue
                        step.sync(len(chunks) - 1 - (j if k == TAPS - 1 else 0))
                        ins = V.scalar_tensor_tensor(out, rows(k), dw_w[:, c, k:k + 1], out, ALU.mult, ALU.add)
                        if k < TAPS - 1:
                            step(ins)
                        else:
                            ins.then_inc(s["conv_ready"], 1)
            dve.wait_ge(s["conv_ready"], len(CONV_ORDER))
            dve.wait_ge(s["conv_pool"], len(CONV_POOL))
            dve.wait_ge(s["mean_mm"], 1)
            for k in range(KC):
                step(V.tensor_tensor(v[:, k, 0:SAMPLE], v[:, k, 0:SAMPLE], bank[0][:, :], ALU.subtract))
                step.sync()
                V.tensor_tensor(v[:, k, SAMPLE:TOK], v[:, k, SAMPLE:TOK], bank[2][:, 0:P], ALU.subtract).then_inc(s["centered"], 1)
            dve.wait_ge(s["var_mm"], 8)
            step(V.tensor_scalar(rstd[:, 0:SAMPLE], bank[1][:, :], EPS, None, ALU.add))
            link(V.tensor_scalar(rstd[:, SAMPLE:TOK], bank[3][:, 0:P], EPS, None, ALU.add))
            V.reciprocal(rstd[:, 0:SAMPLE], rstd[:, 0:SAMPLE]).then_inc(s["var_ready"], 1)
            V.reciprocal(rstd[:, SAMPLE:TOK], rstd[:, SAMPLE:TOK]).then_inc(s["var_ready"], 1)
            dve.wait_ge(s["rstd_ready"], 1)
            dve.wait_ge(s["centered"], 8)
            for k in range(KC):
                V.tensor_tensor(v[:, k, :], v[:, k, :], rstd, ALU.mult).then_inc(s["normed"], 1)
            dve.wait_ge(s["gate_ready"], 4)
            for i in range(2 * NT):
                dve.wait_ge(s["f_mm"], i + 1)
                if i >= 2:
                    dve.wait_ge(s["f_added"], i - 1)
                t = i % NT
                residual(bank[i % 8][:, :], t, i // NT, i % 2, s["f_added"])
                if i >= NT:
                    dve.wait_ge(s["f_added"], i + 1)
                    ln_stats(0, t)
            ln_scale(0)

            def acol(L, p):
                Pi = 8 * L + p
                if not (isinstance(Pi, int) and Pi == 0):
                    dve.wait_ge(s["pt_tr"], 2 * Pi)
                V.tensor_copy(ccol[:, 1, :, :], aff[:, :, bass.ds(2 * p, 2)]).then_inc(s["acol_ready"], 1)

            def build_psel(L, p):
                Pi = 8 * L + p
                link(V.tensor_copy(ccol[:, 2, :, :], posT[:, :, bass.ds(2 * p, 2)]))
                if not (isinstance(Pi, int) and Pi == 0):
                    dve.wait_ge(s["gather_mm"], 3 * Pi)
                    dve.wait_ge(s["pt_tr"], 2 * Pi)
                for e in range(2):
                    for t in range(NS):
                        step(V.tensor_scalar(psel[:, t, e, :], iota, ccol[:, 2, t, e:e + 1], None, ALU.is_equal))
                step(V.tensor_scalar(psel_p[:, 0, :], iota[:, 0:2 * CAP_P], ccol[:, 2, NS, 0:1], None, ALU.is_equal))
                step.sync()
                V.tensor_scalar(psel_p[:, 1, :], iota[:, 0:2 * CAP_P], ccol[:, 2, NS, 1:2], None, ALU.is_equal)\
                 .then_inc(s["psel_ready"], 1)

            def hids(L, p, e, hs):
                Ei = 16 * L + 2 * p + e
                for h in hs:
                    dve.wait_ge(s["silu_ready"], 2 * Ei + (h + 1))
                    dve.wait_ge(s["gu_mm"], 8 * Ei + (4 * h + 4))
                    V.tensor_tensor(hid[0:SLOTS, h, :], hid[0:SLOTS, h, :], bank[2 * h + 1][0:SLOTS, :], ALU.mult)\
                     .then_inc(s["hid_ready"], 1)

            def hidT_evac(L, p, e, hs):
                Ei = 16 * L + 2 * p + e
                for h in hs:
                    dve.wait_ge(s["hidT_tr"], 2 * Ei + (h + 1))
                    src = bank[4 + h][:, 0:4 * SLOTS].rearrange("p (k c) -> p k c", c=SLOTS)
                    hi = hidT_h[:, 4 * h:4 * h + 4, :]
                    link(V.tensor_copy(hi, src))
                    V.tensor_tensor(hidT_l[:, 4 * h:4 * h + 4, :], src, hi.bitcast(F32), ALU.subtract)\
                     .then_inc(s["hidT_ready"], 1)

            def low(L, u0, p, e, m):
                j = (u0 + 6 * e + m // 2) % R
                dve.wait_ge(s["high_ready"], HALVES * (16 * L + 2 * p + e) + (m + 1))
                src = ring[j][:, (m % 2) * HALF:(m % 2 + 1) * HALF].rearrange("p (k n) -> p k n", n=512)
                V.tensor_tensor(w_l[m % NB][:, :, :], src, w_h[m % NB][:, :, :].bitcast(F32), ALU.subtract)\
                 .then_inc(s["low_dve"], 1)

            def out_low(L, p, e, h):
                En = 16 * L + 2 * p + e
                dve.wait_ge(s["down_out"], 4 * En + (2 * h - 2))
                c = slice(h * 512, (h + 1) * 512)
                bk = bank[2 + h]
                a = 1 - e
                V.tensor_tensor(out_s[1][64 * a:64 * a + CAP_S, c], bk[0:CAP_S, :],
                                out_s[0][64 * a:64 * a + CAP_S, c].bitcast(F32), ALU.subtract).then_inc(s["out_split"], 1)
                V.tensor_tensor(out_p[1][32 * a:32 * a + CAP_P, c], bk[CAP_S:SLOTS, :],
                                out_p[0][32 * a:32 * a + CAP_P, c].bitcast(F32), ALU.subtract).then_inc(s["out_split"], 1)

            def xin_split(Pi):
                dve.wait_ge(s["xin_ready"], 16 * Pi + 16)
                link(V.tensor_copy(xin_h[:, :, :, :], xin))
                V.tensor_tensor(xin_l[:, :, :, :], xin, xin_h[:, :, :, :].bitcast(F32), ALU.subtract)\
                 .then_inc(s["xsplit"], 1)

            def comb_add(Pi, halves=range(2 * NT)):
                if not (isinstance(Pi, int) and Pi == 0):
                    dve.wait_ge(s["comb_added"], 10 * Pi)
                for i in halves:
                    t, h = i // 2, i % 2
                    dve.wait_ge(s["comb_mm"], 10 * Pi + (i + 1))
                    f = facc_m[:, t, h * 512:(h + 1) * 512]
                    V.tensor_tensor(f, f, bank[COMB_BANKS[i % 3]][:, :], ALU.add).then_inc(s["comb_added"], 1)

            def pair(L, u0, p, first, last):
                for e in range(2):
                    low(L, u0, p, e, 3)
                    low(L, u0, p, e, 4)
                    if e == 1 or not first:
                        out_low(L, p, e, 1)
                    if e == 0:
                        acol(L, p)
                    low(L, u0, p, e, 5)
                    hids(L, p, e, (0,))
                    low(L, u0, p, e, 6)
                    low(L, u0, p, e, 7)
                    hidT_evac(L, p, e, (0,))
                    if e == 1 and not last:
                        build_psel(L, p + 1)
                    hids(L, p, e, (1,))
                    if e == 0:
                        hidT_evac(L, p, e, (1,))
                        if not first:
                            comb_add(8 * L + p - 1)
                    low(L, u0, p, e, 10)
                    if e == 1:
                        hidT_evac(L, p, e, (1,))
                    if e == 1 and not last:
                        xin_split(8 * L + p + 1)
                    low(L, u0, p, e, 11)
                    for m in range(3):
                        if e == 0:
                            low(L, u0, p, 1, m)
                        elif not last:
                            low(L, u0, p + 1, 0, m)
                        if m == 1:
                            if e == 0:
                                out_low(L, p, 1, 0)
                            else:
                                out_low(L, p + 1, 0, 0)
                if last:
                    out_low(L, p + 1, 0, 1)

            def moe(L, u0):
                b = 2 * L + 1
                hT_evac(b)
                f = facc_m.rearrange("p a b -> p (a b)")
                if L == 1:
                    dve.wait_ge(s["st_out"], 32 * GROUPS)
                step(V.memset(affT[0:EXPERTS, :], 1.0))
                dve.wait_ge(s["logits_mm"], L + 1)
                step(V.tensor_copy(work[0:EXPERTS, 0:SAMPLE], bank[4][0:EXPERTS, :]))
                step.sync()
                V.tensor_copy(work[0:EXPERTS, SAMPLE:TOK], bank[5][0:EXPERTS, 0:P]).then_inc(s["lgT_ready"], 1)
                dve.wait_ge(s["logits_tr"], L + 1)
                lgp = bank[7][:, 0:NT * EXPERTS].rearrange("p (t e) -> p t e", e=EXPERTS)

                def bc(x):
                    return x.rearrange("p (t e) -> p t e", e=1).broadcast_to([P, NT, EXPERTS])

                link(V.tensor_reduce(small[:, 0, :], lgp, AX.X, ALU.max))
                V.tensor_tensor(lg, lgp, bc(small[:, 0, :]), ALU.subtract).then_inc(s["lg_ready"], 1)
                dve.wait_ge(s["exp_ready"], L + 1)
                link(V.tensor_reduce(small[:, 1, :], lg, AX.X, ALU.add))
                link(V.reciprocal(small[:, 2, :], small[:, 1, :]))
                V.tensor_tensor(aff, lg, bc(small[:, 2, :]), ALU.mult).then_inc(s["aff_ready"], 1)
                dve.wait_ge(s["aff_ready"], L + 1)
                dve.wait_ge(s["aff_tr"], L + 1)
                E = EXPERTS
                step(V.tensor_copy(work[0:E, 0:SAMPLE], bank[5][0:E, :]))
                link(V.tensor_copy(work[0:E, SAMPLE:TOK], bank[6][0:E, 0:P]))
                for lo, hi, cap in ((0, SAMPLE, CAP_S), (SAMPLE, TOK, CAP_P)):
                    for _ in range(cap // 8):
                        link(V.max(top8[0:E, :], work[0:E, lo:hi]))
                        link(V.match_replace(work[0:E, lo:hi], top8[0:E, :], work[0:E, lo:hi], -1.0))
                link(V.tensor_scalar(work[0:E, :], work[0:E, :], 0.0, None, ALU.is_lt))
                for lo, hi in ((0, SAMPLE), (SAMPLE, TOK)):
                    step(V.tensor_tensor_scan(pos[0:E, lo:hi], affT[0:E, lo:hi], work[0:E, lo:hi], 0.0, ALU.mult, ALU.add))
                step.sync()
                V.tensor_tensor(pos[0:E, :], pos[0:E, :], work[0:E, :], ALU.mult).then_inc(s["posm_ready"], 1)
                dve.wait_ge(s["pos_tr"], L + 1)
                link(V.tensor_copy(posT, bank[4][:, 0:NT * EXPERTS].rearrange("p (t e) -> p t e", e=EXPERTS)))
                build_psel(L, 0)
                for m in range(NB):
                    low(L, u0, 0, 0, m)
                link(V.memset(f, 0.0))
                for n in range(2):
                    step(V.tensor_copy(out_p[n][:, :], f[:, 0:D]))
                step.sync()
                xin_split(8 * L)
                pair(L, u0, 0, True, False)
                n0 = step.n
                per = PAIR_STEPS
                with dve.Fori(1, PAIRS - 1) as p:
                    step.off = (p - 1) * per
                    pair(L, u0, p, False, False)
                assert step.n - n0 == per, step.n - n0
                step.off = 0
                step.n = n0 + per * (PAIRS - 2)
                pair(L, u0, PAIRS - 1, False, True)
                dve.wait_ge(s["gate_ready"], 4 * (b + 1))
                for t in range(NT):
                    comb_add(8 * L + 7, (2 * t, 2 * t + 1))
                    dve.wait_ge(s["comb_added"], 10 * (8 * L + 7) + 2 * t + 2)
                    finish_tile(b, t, facc_m)

            moe(0, U_MOE0)

            hT_evac(2)
            step(V.memset(facc_s.rearrange("p a b -> p (a b)"), 0.0))
            dve.wait_ge(s["ssdp_loaded"], 32)
            dve.wait_ge(s["dtr_mm"], 1)
            w2 = [dtmp[:, i, :].rearrange("p (t h) -> p t h", h=64) for i in range(3)]
            rowb = srow[:, 0:64].rearrange("p (t h) -> p t h", t=1).broadcast_to([P, NT, 64])
            arow = srow[:, 64:128].rearrange("p (t h) -> p t h", t=1).broadcast_to([P, NT, 64])
            V.tensor_tensor(dt, bank[7][:, 0:NT * 64].rearrange("p (t h) -> p t h", h=64), rowb, ALU.add).then_inc(s["dt_a"], 1)
            dve.wait_ge(s["dt_a"], 1)
            link(V.tensor_scalar(w2[0], dt, -1.0, None, ALU.mult))
            V.tensor_tensor(w2[1], dt, w2[0], ALU.min).then_inc(s["dt_a"], 1)
            dve.wait_ge(s["dt_a"], 2)
            dve.wait_ge(s["dt_b"], 2)
            link(V.tensor_scalar(w2[0], w2[1], 1.0, None, ALU.add))
            V.tensor_copy(w2[2], w2[0]).then_inc(s["dt_a"], 1)
            link(V.tensor_scalar(w2[0], w2[0], -1.0, None, ALU.add))
            step(V.tensor_scalar(wst, w2[0], 0.0, None, ALU.is_equal))
            dve.wait_ge(s["dt_a"], 3)
            dve.wait_ge(s["dt_b"], 3)
            step.sync()
            link(V.tensor_scalar(w2[0], w2[0], 1e-30, None, ALU.max))
            link(V.reciprocal(w2[0], w2[0]))
            step(V.tensor_tensor(w2[0], w2[0], w2[2], ALU.mult))
            step.sync()
            link(V.tensor_tensor(w2[0], w2[0], wst, ALU.add))
            link(V.tensor_tensor(w2[0], w2[0], w2[1], ALU.mult))
            link(V.scalar_tensor_tensor(dt, dt, 0.0, w2[0], ALU.max, ALU.add))
            V.scalar_tensor_tensor(da, dt, -1.0, arow, ALU.mult, ALU.mult).then_inc(s["da_ready"], 1)

            def conv(g, j):
                i = 6 * g + j
                dve.wait_ge(s["raw_ready"], i + 1)
                if i >= 2:
                    dve.wait_ge(s["xf_ready"], i - 1)
                ch = (16 + g) if j == 0 else (20 + g) if j == 1 else 4 * g + j - 2
                a, b = cv[:, i % 2, 0:SAMPLE], cv[:, i % 2, SAMPLE:TOK]
                ra, rb = raw[:, i % 2, 0:SAMPLE + 4], raw[:, i % 2, SAMPLE + 4:]
                step(V.tensor_scalar(a, ra[:, 0:SAMPLE], sc_w[:, ch, 0:1], sc_b[:, ch:ch + 1], ALU.mult, ALU.add))
                step(V.tensor_scalar(b, rb[:, 0:P], sc_w[:, ch, 0:1], sc_b[:, ch:ch + 1], ALU.mult, ALU.add))
                for k in range(1, STAPS):
                    step.sync()
                    step(V.scalar_tensor_tensor(a, ra[:, k:k + SAMPLE], sc_w[:, ch, k:k + 1], a, ALU.mult, ALU.add))
                    ins = V.scalar_tensor_tensor(b, rb[:, k:k + P], sc_w[:, ch, k:k + 1], b, ALU.mult, ALU.add)
                    if k < STAPS - 1:
                        step(ins)
                    else:
                        step.sync()
                        ins.then_inc(s["cconv_ready"], 1)

            def xs_evac(g, j):
                n = 5 * g + (0 if j == 0 else j - 1)
                dve.wait_ge(s["xtr_mm"], n + 1)
                dst = Btok[:, NS, :] if j == 0 else xs[:, NS, (j - 2) * P:(j - 1) * P]
                V.tensor_copy(dst, bank[6 + n % 2][:, 0:P]).then_inc(s["xs_v"], 1)

            for g in range(GROUPS):
                if g:
                    dve.wait_ge(s["out_mm"], 10 * g)
                for j in range(6):
                    conv(g, j)
                    if j == 3:
                        xs_evac(g, 0)
                    if j >= 4:
                        xs_evac(g, j - 2)
                xs_evac(g, 4)
                xs_evac(g, 5)
                if g == 0:
                    dve.wait_ge(s["ex_ready"], 5)
                    V.tensor_tensor(wst, dt, Ex[:, :, 64:128], ALU.mult).then_inc(s["dt_c"], 1)
                dve.wait_ge(s["cb_mm"], g + 1)
                for dr in range(2):
                    m = m_le if dr == 0 else m_ge
                    V.tensor_tensor(CBm[:, dr, 0:SAMPLE].rearrange("p (t k) -> p t k", k=P),
                                    bank[4][:, :].rearrange("p (t k) -> p t k", k=P),
                                    m.rearrange("p (t k) -> p t k", t=1).broadcast_to([P, NS, P]), ALU.mult)\
                     .then_inc(s["cbm_ready"], 1)
                    V.tensor_tensor(CBm[:, dr, SAMPLE:TOK], bank[5][:, 0:P], m, ALU.mult).then_inc(s["cbm_ready"], 1)
                dve.wait_ge(s["cbm_ready"], 4 * (g + 1))
                for i in range(2 * NT + 1):
                    if i < 2 * NT:
                        n = 10 * g + i
                        c, q = i // 2, i % 2
                        for dr in range(2):
                            a = 2 * (n % 2) + dr
                            h0 = 32 * dr + HG * g + 4 * q
                            if n >= 2:
                                dve.wait_ge(s["yd_mm"], n - 1)
                            V.tensor_tensor(Xd[:, a, :].rearrange("p (h d) -> p h d", d=HD),
                                            xs[:, c, 256 * q:256 * (q + 1)].rearrange("p (h d) -> p h d", d=HD),
                                            dt[:, c, h0:h0 + 4].rearrange("p (h d) -> p h d", d=1).broadcast_to([P, 4, HD]),
                                            ALU.mult).then_inc(s["xd_ready"], 1)
                            dve.wait_ge(s["exp_m"], 2 * n + dr + 1)
                            V.tensor_tensor(Em[:, a, :].rearrange("p (h k) -> p h k", k=P),
                                            Em[:, a, :].rearrange("p (h k) -> p h k", k=P),
                                            CBm[:, dr, c * P:(c + 1) * P].rearrange("p (h k) -> p h k", h=1)
                                            .broadcast_to([P, 4, P]), ALU.mult).then_inc(s["m_ready"], 1)
                    if i:
                        n = 10 * g + i - 1
                        c, q = (i - 1) // 2, (i - 1) % 2
                        dve.wait_ge(s["yd_mm"], n + 1)
                        dve.wait_ge(s["y_init"], NT * (g + 1))
                        y = Y[:, c, 256 * q:256 * (q + 1)]
                        V.tensor_tensor(y, y, bank[4 + n % 2][:, 0:256], ALU.add).then_inc(s["yd_added"], 1)
                dve.wait_ge(s["yd_added"], 10 * (g + 1))
                dve.wait_ge(s["state_loaded"], 32 * (g + 1))
                for dr, c, off, stt, noff, nst, prev in scan_tasks():
                    noff += 8 * g
                    nst += 8 * g
                    h0 = 32 * dr + HG * g

                    def bc(x):
                        return x.rearrange("p (h d) -> p h d", d=1).broadcast_to([P, HG, HD])

                    if prev:
                        dve.wait_ge(s["prev_ready"], 8 * g + prev)
                    if off:
                        dve.wait_ge(s["off_mm"], noff + 1)
                        if noff:
                            dve.wait_ge(s["off_added"], noff)
                        tm = tmp[:, noff % 2, :]
                        link(V.tensor_tensor(tm.rearrange("p (h d) -> p h d", d=HD),
                                             bank[4 + noff % 2][:, :].rearrange("p (h d) -> p h d", d=HD),
                                             bc(Ex[:, c, h0:h0 + HG]), ALU.mult))
                        V.tensor_tensor(Y[:, c, :], Y[:, c, :], tm, ALU.add).then_inc(s["off_added"], 1)
                    if stt:
                        pv = prevS[:, dr, :]
                        own = bank[6 + nst % 2][:, :]
                        dve.wait_ge(s["st_mm"], nst + 1)
                        if off:
                            link(V.tensor_tensor(pv.rearrange("p (h d) -> p h d", d=HD), pv.rearrange("p (h d) -> p h d", d=HD),
                                                 bc(Ex[:, c, 128 + h0:128 + h0 + HG]), ALU.mult))
                            V.tensor_tensor(pv, pv, own, ALU.add).then_inc(s["prev_ready"], 1)
                        else:
                            V.tensor_copy(pv, own).then_inc(s["prev_ready"], 1)
                dve.wait_ge(s["off_added"], 8 * (g + 1))

                def norm_y(t0, t1, n):
                    for t in range(t0, t1):
                        dve.wait_ge(s["z_silu"], NT * g + t + 1)
                        V.tensor_tensor(Y[:, t, :], Y[:, t, :], zt[t], ALU.mult).then_inc(s["y_z"], 1)
                    for t in range(t0, t1):
                        dve.wait_ge(s["y_z"], NT * g + t + 1)
                        link(V.tensor_tensor_reduce(out=tmp[:, t % 2, :], in0=Y[:, t, :], in1=Y[:, t, :], scale=1.0,
                                                    scalar=0.0, op0=ALU.mult, op1=ALU.add, accum_out=rms[:, 0, t:t + 1]))
                    link(V.tensor_scalar(rms[:, 1, t0:t1], rms[:, 0, t0:t1], 1.0 / GC, EPS, ALU.mult, ALU.add))
                    V.reciprocal(rms[:, 1, t0:t1], rms[:, 1, t0:t1]).then_inc(s["rms_a"], 1)
                    dve.wait_ge(s["rms_b"], 2 * g + n)
                    for t in range(t0, t1):
                        V.tensor_scalar(Y[:, t, :], Y[:, t, :], rms[:, 1, t:t + 1], None, ALU.mult)\
                         .then_inc(s["y_normed"], 1)

                norm_y(0, NS, 1)
                for t in range(NT):
                    if t == 3:
                        norm_y(NS, NT, 2)
                    dve.wait_ge(s["yT_ready"], 4 * (NT * g + t + 1))
                    for i in range(4):
                        c = 4 * g + i
                        V.scalar_tensor_tensor(yT_l[:, t, i, :] if t < NS else yT_l4[:, i, :],
                                               bank[4 + t % NS][:, i * P:(i + 1) * P], norm_w[:, c:c + 1],
                                               yT_h[:, i, t * P:(t + 1) * P].bitcast(F32), ALU.mult, ALU.subtract)\
                         .then_inc(s["yT_low"], 1)
                step.sync()
                for i in range(2 * NT):
                    t, h = i // 2, i % 2
                    dve.wait_ge(s["out_mm"], 10 * g + i + 1)
                    if g and i == 0:
                        dve.wait_ge(s["out_added"], 10 * g)
                    f = facc_s[:, t, h * 512:(h + 1) * 512]
                    V.tensor_tensor(f, f, bank[i % 8][:, :], ALU.add).then_inc(s["out_added"], 1)
                    if g == GROUPS - 1 and h == 1:
                        dve.wait_ge(s["out_added"], 10 * g + i + 1)
                        finish_tile(2, t, facc_s)
            moe(1, U_MOE1)


PAIR_STEPS = 1 + 9 + 4 + 1


def kernel(**inputs):
    import concourse.bacc as bacc
    from concourse.bass_utils import run_bass_kernel_spmd

    a = {k: np.asarray(x) for k, x in inputs.items()}

    def blocks(w):
        k, n = w.shape
        return w.reshape(k // P, P, n // 512, 512).transpose(2, 1, 0, 3).reshape(n // 512, P, -1)

    def feat(x):
        x = x.reshape(x.shape[:-1] + (-1, P))
        return np.moveaxis(x, -1, 0)

    units = np.empty((UNITS, P, UNIT), np.float32)
    units[U_ADA0:U_ADA0 + 12] = blocks(a["ada_w"][0])
    units[U_ADA1:U_ADA1 + 12] = blocks(a["ada_w"][1])
    units[U_PW1:U_PW1 + 4] = blocks(a["conv_pw1_w"][0])[[0, 2, 1, 3]]
    units[U_PW2:U_PW2 + 2] = blocks(a["conv_pw2_w"][0])
    for L, u0 in ((0, U_MOE0), (1, U_MOE1)):
        v = units[u0:u0 + 6 * EXPERTS].reshape(EXPERTS, 6, P, UNIT)
        for e in range(EXPERTS):
            g, u = blocks(a["moe_w_gate"][L, e]), blocks(a["moe_w_up"][L, e])
            v[e, 0], v[e, 2], v[e, 1], v[e, 3] = g[0], g[1], u[0], u[1]
            v[e, 4:6] = blocks(a["moe_w_down"][L, e])
    w_in, w_out = a["ssd_in_w"][0], a["ssd_out_w"][0]
    for g in range(GROUPS):
        u = U_SSD + 4 * g
        B = w_in[:, 4096 + g * P:4096 + (g + 1) * P]
        C = w_in[:, 4608 + g * P:4608 + (g + 1) * P]
        bc = np.concatenate([B, C], 1).reshape(KC, P, 256).transpose(1, 0, 2).reshape(P, -1)
        units[u, :, 0:UNIT // 2] = bc
        units[u, :, UNIT // 2:] = 0
        units[u + 1] = blocks(w_in[:, 2048 + g * GC:2048 + (g + 1) * GC])[0]
        units[u + 2] = blocks(w_in[:, g * GC:(g + 1) * GC])[0]
        units[u + 3] = w_out[g * GC:(g + 1) * GC].reshape(4, P, D).transpose(1, 0, 2).reshape(P, -1)

    x = np.concatenate([a["x_sample"].reshape(NS, P, D), a["x_prompt"].reshape(1, P, D)]).transpose(1, 0, 2)
    cols = {
        "ada_b": feat(a["ada_b"]), "pw1_b": feat(a["conv_pw1_b"][0]),
        "dw_w": feat(a["conv_dw_w"][0]).transpose(0, 2, 1), "dw_b": feat(a["conv_dw_b"][0]),
        "cln_g": feat(a["conv_ln_g"][0]), "cln_b": feat(a["conv_ln_b"][0]),
        "sc_w": feat(a["ssd_conv_w"][0]).transpose(0, 2, 1), "sc_b": feat(a["ssd_conv_b"][0]),
        "norm_w": feat(a["ssd_norm_w"][0]),
        "cond": np.stack([feat(a["c"][0]), feat(a["c_ctx"])], -1),
    }
    params = np.concatenate([cols[n].reshape(P, -1) for n in COLS], 1)
    i, j = np.arange(P)[:, None], np.arange(P)[None, :]
    consts = np.concatenate([i == j, i <= j, i >= j, i > j, i < j, np.ones((P, P)), np.full((P, P), 1.0 / D),
                             np.broadcast_to(np.arange(1, CAP_S + 1), (P, CAP_S))], 1).astype(np.float32)
    router = a["router_w"].reshape(DEPTH, KC, P, EXPERTS).transpose(2, 0, 1, 3)
    w_dt = w_in[:, 5120:5184].reshape(KC, P, 64).transpose(1, 0, 2)
    ln = np.stack([np.stack([a["ln_mix_g"][0], a["ln_mix_b"][0]]), np.stack([a["ln_ffn_g"][0], a["ln_ffn_b"][0]]),
                   np.stack([a["ln_mix_g"][1], a["ln_mix_b"][1]]), np.stack([a["ln_ffn_g"][1], a["ln_ffn_b"][1]])])
    rows = np.concatenate([a["ssd_dt_bias"][0].reshape(1, -1), a["ssd_a_log"][0].reshape(1, -1),
                           a["ssd_d_skip"][0].reshape(1, -1)], 1)
    state = a["state_ssd"][0, 0].transpose(0, 3, 1, 2).reshape(2, P, HEADS * HD)
    feeds = {"w_stream": units, "x_in": x, "params": params, "consts": consts, "router": router, "w_dt": w_dt,
             "ln_rows": ln, "pw2_b": a["conv_pw2_b"][0].reshape(1, -1), "ssd_rows": rows, "state_in": state}
    nc = bacc.Bacc("TRN2", target_bir_lowering=False, num_devices=1)
    arrays, args = {}, []
    for name, arr in feeds.items():
        arr = np.ascontiguousarray(arr)
        arrays[name] = arr
        args.append(nc.dram_tensor(name, arr.shape, mybir.dt.from_np(arr.dtype), kind="ExternalInput").ap())
    args.append(nc.dram_tensor("y_out", (P, NT, D), F32, kind="ExternalOutput").ap())
    args.append(nc.dram_tensor("state_out", (2, P, HEADS * HD), F32, kind="ExternalOutput").ap())
    build(nc, *args)
    r = run_bass_kernel_spmd(nc, [arrays], core_ids=[0])
    y = r.results[0]["y_out"].transpose(1, 0, 2)
    st = r.results[0]["state_out"].reshape(2, P, HEADS, HD).transpose(0, 2, 3, 1)
    return (np.ascontiguousarray(y[NS]).reshape(1, P, D), np.ascontiguousarray(y[:NS]).reshape(1, SAMPLE, D),
            np.ascontiguousarray(st)[None, None])
```
